# Optimizing a Trainium2 kernel written in Bass

```python
import jax, jax.numpy as jnp
from jax import lax
import numpy as np

D_MODEL = 1024
BATCH = 1
SEQ = 256
DEPTH = 1

GRID_W = 64
CTX_LEN = 256
EPS = 1e-6

GROUP_DIM = 64
CONV_GROUPS = 4
CONV_W = CONV_GROUPS * GROUP_DIM
CONV_K = 3
SGU_GROUPS = 4
SGU_W = SGU_GROUPS * GROUP_DIM
CHUNK = 128
NA_HEADS = 8
NA_HEAD_DIM = GROUP_DIM
NA_W = NA_HEADS * NA_HEAD_DIM
NA_KH = 8
NA_KW = 16

MIX_W = CONV_W + SGU_W + NA_W
IN_W = 3 * CONV_W + 2 * SGU_W + 3 * NA_W

PEER_HEADS = 8
PEER_NKEYS = 128
PEER_N = PEER_NKEYS * PEER_NKEYS
PEER_DKEY = 256
PEER_TOPK = 16
TOKEN_BLOCK = 128

kernel_name = "hybrid_conv_sgu_natten_peer_dit"

def rmsnorm(x, g):
    xf = x.astype(jnp.float32)
    y = xf * lax.rsqrt(jnp.mean(xf * xf, axis=-1, keepdims=True) + EPS)
    return (y * g.astype(jnp.float32)).astype(x.dtype)

def group_rmsnorm(y, g, groups):
    shp = y.shape
    y = rmsnorm(y.reshape(*shp[:-1], groups, shp[-1] // groups), g.reshape(groups, -1))
    return y.reshape(shp)

def split_proj(p):
    a = p[..., :3 * CONV_W]
    s = p[..., 3 * CONV_W:3 * CONV_W + 2 * SGU_W]
    qkv = p[..., 3 * CONV_W + 2 * SGU_W:]
    return a, s, qkv

def to_heads(qkv):
    b, t, _ = qkv.shape
    q, k, v = jnp.split(qkv, 3, axis=-1)
    return (q.reshape(b, t, NA_HEADS, NA_HEAD_DIM), k.reshape(b, t, NA_HEADS, NA_HEAD_DIM),
            v.reshape(b, t, NA_HEADS, NA_HEAD_DIM))

def short_conv_mixer(p, w):
    gate_b, gate_c, xin = jnp.split(p, 3, axis=-1)
    z = jnp.pad(gate_c * xin, ((0, 0), (1, 1), (0, 0)))
    conv = z[:, :-2] * w[0] + z[:, 1:-1] * w[1] + z[:, 2:] * w[2]
    return gate_b * conv

def spatial_gating_mixer(p, w_s, b_s, g_v):
    b, t, _ = p.shape
    u, v = jnp.split(jax.nn.gelu(p), 2, axis=-1)
    v = group_rmsnorm(v, g_v, SGU_GROUPS)
    v = v.reshape(b, t // CHUNK, CHUNK, SGU_GROUPS, GROUP_DIM)
    mixed = jnp.einsum('gpq,bnqgc->bnpgc', w_s, v) + b_s.T[None, None, :, :, None]
    return u * mixed.reshape(b, t, SGU_W)

def neighbourhood_attention(q, k, v, kc, vc, rpb):
    b, t, h, dh = q.shape
    rows = t // GRID_W
    kh = min(NA_KH, rows)
    scale = dh ** -0.5
    qg = q.reshape(b, rows, GRID_W, h, dh)
    kg = k.reshape(b, rows, GRID_W, h, dh)
    vg = v.reshape(b, rows, GRID_W, h, dh)
    cols = jnp.arange(GRID_W)
    col_start = jnp.clip(cols - NA_KW // 2, 0, GRID_W - NA_KW)
    col_idx = col_start[:, None] + jnp.arange(NA_KW)[None, :]
    rpb_c = rpb[:, :, col_idx - cols[:, None] + (NA_KW - 1)]

    def row_step(r):
        rs = jnp.clip(r - kh // 2, 0, rows - kh)
        q_r = lax.dynamic_index_in_dim(qg, r, axis=1, keepdims=False)
        k_n = lax.dynamic_slice_in_dim(kg, rs, kh, axis=1)[:, :, col_idx]
        v_n = lax.dynamic_slice_in_dim(vg, rs, kh, axis=1)[:, :, col_idx]
        bias = rpb_c[:, rs + jnp.arange(kh) - r + (NA_KH - 1)]
        s_loc = jnp.einsum('bqhd,biqjhd->bhqij', q_r, k_n) * scale
        s_loc = s_loc + jnp.transpose(bias, (0, 2, 1, 3))[None]
        s_ctx = jnp.einsum('bqhd,bkhd->bhqk', q_r, kc) * scale
        s = jnp.concatenate([s_loc.reshape(b, h, GRID_W, kh * NA_KW), s_ctx], axis=-1)
        pr = jax.nn.softmax(s.astype(jnp.float32), axis=-1).astype(v.dtype)
        p_loc = pr[..., :kh * NA_KW].reshape(b, h, GRID_W, kh, NA_KW)
        p_ctx = pr[..., kh * NA_KW:]
        return (jnp.einsum('bhqij,biqjhd->bqhd', p_loc, v_n)
                + jnp.einsum('bhqk,bkhd->bqhd', p_ctx, vc))

    out = lax.map(row_step, jnp.arange(rows))
    return jnp.transpose(out, (1, 0, 2, 3, 4)).reshape(b, t, h * dh)

def context_attention(qc, kc, vc):
    s = jnp.einsum('bqhd,bkhd->bhqk', qc, kc) * (NA_HEAD_DIM ** -0.5)
    pr = jax.nn.softmax(s.astype(jnp.float32), axis=-1).astype(vc.dtype)
    return jnp.einsum('bhqk,bkhd->bqhd', pr, vc).reshape(qc.shape[0], qc.shape[1], NA_W)

def merge_heads(y_conv, y_sgu, y_na, out_norm_g, w_out):
    y = jnp.concatenate([y_conv, y_sgu, y_na], axis=-1)
    return group_rmsnorm(y, out_norm_g, MIX_W // GROUP_DIM) @ w_out

def peer_ffn(h, w_q, sub_keys, u_tab, v_tab):
    n, d = h.shape
    blocks = h.reshape(n // TOKEN_BLOCK, TOKEN_BLOCK, d)

    def block_step(hb):
        q = (hb @ w_q).reshape(TOKEN_BLOCK, PEER_HEADS, 2, PEER_DKEY // 2)
        s = jnp.einsum('thpd,hpkd->thpk', q, sub_keys).astype(jnp.float32)
        top_s, top_i = lax.top_k(s, PEER_TOPK)
        cand_s = (top_s[:, :, 0, :, None] + top_s[:, :, 1, None, :]).reshape(TOKEN_BLOCK, PEER_HEADS, -1)
        cand_i = (top_i[:, :, 0, :, None] * PEER_NKEYS + top_i[:, :, 1, None, :]).reshape(TOKEN_BLOCK, PEER_HEADS, -1)
        best_s, best_pos = lax.top_k(cand_s, PEER_TOPK)
        expert = jnp.take_along_axis(cand_i, best_pos, axis=-1)
        g = jax.nn.softmax(best_s, axis=-1)
        act = jax.nn.gelu(jnp.einsum('thkd,td->thk', u_tab[expert], hb))
        wgt = g.astype(act.dtype) * act
        return jnp.einsum('thk,thkd->td', wgt, v_tab[expert])

    return lax.map(block_step, blocks).reshape(n, d)

def setup_inputs(seed: int = 0) -> dict:
    key = jax.random.key(seed)
    ks = jax.random.split(key, 21)
    D = D_MODEL

    def nrm(k, shape, s):
        return jax.random.normal(k, shape, jnp.float32) * s

    return {
        "x": nrm(ks[0], (BATCH, SEQ, D), 1.0),
        "c": nrm(ks[1], (BATCH, D), 1.0),
        "ctx": nrm(ks[2], (BATCH, CTX_LEN, D), 1.0),
        "c_ctx": nrm(ks[3], (D,), 1.0),
        "ada_w": nrm(ks[4], (DEPTH, D, 6 * D), 0.5 * D ** -0.5),
        "ada_b": nrm(ks[5], (DEPTH, 6 * D), 0.02),
        "norm1_g": 1.0 + nrm(ks[6], (DEPTH, D), 0.05),
        "w_in": nrm(ks[7], (DEPTH, D, IN_W), D ** -0.5),
        "conv_w": nrm(ks[8], (DEPTH, CONV_K, CONV_W), CONV_K ** -0.5),
        "sgu_w": nrm(ks[9], (DEPTH, SGU_GROUPS, CHUNK, CHUNK), CHUNK ** -0.5),
        "sgu_b": 1.0 + nrm(ks[10], (DEPTH, SGU_GROUPS, CHUNK), 0.1),
        "sgu_norm_g": 1.0 + nrm(ks[11], (DEPTH, SGU_W), 0.05),
        "na_rpb": nrm(ks[12], (DEPTH, NA_HEADS, 2 * NA_KH - 1, 2 * NA_KW - 1), 0.2),
        "out_norm_g": 1.0 + nrm(ks[13], (DEPTH, MIX_W), 0.05),
        "w_out": nrm(ks[14], (DEPTH, MIX_W, D), MIX_W ** -0.5),
        "norm2_g": 1.0 + nrm(ks[15], (DEPTH, D), 0.05),
        "peer_wq": nrm(ks[16], (DEPTH, D, PEER_HEADS * PEER_DKEY), D ** -0.5),
        "peer_subkeys": nrm(ks[17], (DEPTH, PEER_HEADS, 2, PEER_NKEYS, PEER_DKEY // 2), (PEER_DKEY // 2) ** -0.5),
        "peer_u": nrm(ks[18], (DEPTH, PEER_N, D), D ** -0.5),
        "peer_v": nrm(ks[19], (DEPTH, PEER_N, D), 0.5),
        "final_norm_g": 1.0 + nrm(ks[20], (D,), 0.05),
    }

def reference(x, c, ctx, c_ctx, ada_w, ada_b, norm1_g, w_in, conv_w, sgu_w, sgu_b, sgu_norm_g,
              na_rpb, out_norm_g, w_out, norm2_g, peer_wq, peer_subkeys, peer_u, peer_v,
              final_norm_g):
    b, t, d = x.shape
    xc = ctx
    for l in range(DEPTH):
        last = l == DEPTH - 1
        sh1, sc1, g1, sh2, sc2, g2 = jnp.split((jax.nn.silu(c) @ ada_w[l] + ada_b[l])[:, None, :], 6, axis=-1)
        csh1, csc1, cg1, csh2, csc2, cg2 = jnp.split(jax.nn.silu(c_ctx) @ ada_w[l] + ada_b[l], 6, axis=-1)

        h = rmsnorm(x, norm1_g[l]) * (1.0 + sc1) + sh1
        hc = rmsnorm(xc, norm1_g[l]) * (1.0 + csc1) + csh1
        a_l, s_l, qkv_l = split_proj(h @ w_in[l])
        a_c, s_c, qkv_c = split_proj(hc @ w_in[l])
        q, k, v = to_heads(qkv_l)
        qc, kc, vc = to_heads(qkv_c)
        y = merge_heads(short_conv_mixer(a_l, conv_w[l]),
                        spatial_gating_mixer(s_l, sgu_w[l], sgu_b[l], sgu_norm_g[l]),
                        neighbourhood_attention(q, k, v, kc, vc, na_rpb[l]),
                        out_norm_g[l], w_out[l])
        x = x + g1 * y
        h2 = rmsnorm(x, norm2_g[l]) * (1.0 + sc2) + sh2

        if last:
            x = x + g2 * peer_ffn(h2.reshape(-1, d), peer_wq[l], peer_subkeys[l], peer_u[l], peer_v[l]).reshape(x.shape)
        else:
            yc = merge_heads(short_conv_mixer(a_c, conv_w[l]),
                             spatial_gating_mixer(s_c, sgu_w[l], sgu_b[l], sgu_norm_g[l]),
                             context_attention(qc, kc, vc),
                             out_norm_g[l], w_out[l])
            xc = xc + cg1 * yc
            hc2 = rmsnorm(xc, norm2_g[l]) * (1.0 + csc2) + csh2
            f = peer_ffn(jnp.concatenate([h2.reshape(-1, d), hc2.reshape(-1, d)], axis=0),
                         peer_wq[l], peer_subkeys[l], peer_u[l], peer_v[l])
            n_lat = b * t
            x = x + g2 * f[:n_lat].reshape(x.shape)
            xc = xc + cg2 * f[n_lat:].reshape(xc.shape)
    return rmsnorm(x, final_norm_g)


_drawn_inputs = setup_inputs


def setup_inputs(seed=0):
    import zlib

    import numpy as np

    out = dict(_drawn_inputs(seed))
    spreads = {}
    factors = {'sgu_b': 4.66, 'sgu_norm_g': 6.662, 'na_rpb': 4.662, 'out_norm_g': 2.932, 'norm2_g': 2.743}
    for name, (base, spread) in spreads.items():
        noise = np.random.default_rng([zlib.crc32(name.encode()), seed]).standard_normal(out[name].shape)
        drawn = base * np.exp(spread * noise) if base else spread * noise
        out[name] = __import__('jax').numpy.asarray(drawn.astype(out[name].dtype))
    for name, factor in factors.items():
        out[name] = (out[name] * factor).astype(out[name].dtype)
    return out
```

```python
from contextlib import ExitStack

import concourse.bass as bass
from concourse import mybir

F32 = mybir.dt.float32
F32R = mybir.dt.float32r
U32 = mybir.dt.uint32
ALU = mybir.AluOpType
ACT = mybir.ActivationFunctionType
AX = mybir.AxisListType

P = 128
D = 1024
KD = D // P
T = 256
TB = T // P
CTX = 256
KEYS = T + CTX
HEADS, HD = 8, 64
CONV_T = 2
SGU_G = 4
EPS = 1e-6
PH = 8
NK = 128
TOPK = 16
LISTS = 2 * PH
BLK = 256
RING = 4
NEG = -1.0e30
LOWEST = -3.0e38
SLOTS = 4
CHUNKS = NK
GT = 4
GROUPS = T // GT

TOPK_UNTIL = 4 * TB * PH
DECODE_UNTIL = TOPK_UNTIL + 16
SOFTMAX_UNTIL = DECODE_UNTIL + 4
TURN_AT = SOFTMAX_UNTIL + 8
SCRATCH_CHUNK = 96

COL_C = 0
COL_ADA_B = COL_C + 2 * KD
COL_N1 = COL_ADA_B + 6 * KD
COL_N2 = COL_N1 + KD
COL_OG = COL_N2 + KD
COL_CONV = COL_OG + KD
COLS = COL_CONV + 3 * CONV_T

SH1, SC1, G1, SH2, SC2, G2 = range(6)


def weight_blocks():
    first = [("ada", 4 * s + b) for s in (SH1, SC1) for b in range(4)]
    later = [("ada", 4 * s + b) for s in (G1, SH2, SC2) for b in range(4)]
    w_in = [("w_in", b) for b in (3, 4, 5, 6, 7, 8, 9, 10, 0, 1, 2)]
    order = first + [w_in[0]]
    for n, block in enumerate(later):
        order.append(block)
        if n + 1 < len(w_in):
            order.append(w_in[n + 1])
    order += [("w_out", b) for b in range(4)]
    order += [("w_q", b) for b in range(LISTS // 2)]
    order += [("ada", 4 * G2 + b) for b in range(4)]
    return order


def bank_uses(blocks):
    place, used = {}, [0] * 8

    def put(name, bank):
        place[name] = (bank, used[bank])
        used[bank] += 1

    n = 0

    def ring(name, banks=(0, 1, 2, 3)):
        nonlocal n
        put(name, banks[n % len(banks)])
        n += 1

    put("stat1", 7)
    for matrix, b in blocks:
        if matrix == "ada" and b // 4 < G2 and b % 4 == 0:
            put(("mod", b // 4), {SH1: 4, SC1: 5, G1: 6, SH2: 4, SC2: 5}[b // 4])
        if matrix == "w_in":
            for half in range(2 if b >= 7 else 1):
                ring((matrix, b, half))
        if (matrix, b) == ("w_in", 2):
            ring("sgu")
        if (matrix, b) == ("w_out", 0):
            for u in range(HEADS * TB + 2):
                if u < HEADS * TB:
                    put(("scores", u), 4 + u % 2)
                if u >= 2:
                    v = u - 2
                    put(("turned", v), 6 + v % 2)
                    if v % 4 == 0:
                        put(("attended", v // 4), v // 4)
            for j in range(4):
                put(("group", j), 4 + j)
        if matrix == "w_out":
            ring((matrix, b, 0))
        if (matrix, b) == ("w_out", 3):
            put("stat2", 4)
            for j in range(4):
                put(("x1_turned", j), 4 + (j + 1) % 4)
        if matrix == "w_q":
            ring((matrix, b, 0))
        if matrix == "ada" and b // 4 == G2 and b % 2 == 0:
            ring(("g2", b % 4 // 2))
    for tb in range(TB):
        for l4 in range(LISTS // 4):
            put(("keys", tb, l4), 4 + l4)
    return place, used


def build(nc, x_t, ctx_t, cols, rows, sgu_gain, final_gain, constants, sgu_wt, bias_mask, ada_w, w_in,
          w_out, w_q, subkeys_t, peer_u_t, peer_v, out):
    blocks = weight_blocks()
    place, used = bank_uses(blocks)
    ring_of = {block: n for n, block in enumerate(blocks)}
    sources = {"ada": ada_w, "w_in": w_in, "w_out": w_out, "w_q": w_q}
    v_rows = peer_v.rearrange("(a b) d -> b a d", b=CHUNKS)

    with ExitStack() as stack:
        def sbuf(name, shape, dtype=F32):
            return stack.enter_context(nc.sbuf_tensor(name, shape, dtype))

        def sem(name):
            return stack.enter_context(nc.semaphore(name))

        bank = [stack.enter_context(nc.psum_tensor(f"bank{b}", [P, 512], F32)) for b in range(8)]

        A = sbuf("A", [P, CHUNKS * T])
        A3 = A[:, :].rearrange("p (c t) -> p c t", t=T)

        at = [0]

        def part(size, start=None):
            if start is not None:
                at[0] = start
            at[0] += size
            return A[:, at[0] - size:at[0]]

        X1 = part(KD * T).rearrange("p (k t) -> p k t", k=KD)
        H = part(KD * KEYS).rearrange("p (k t) -> p k t", k=KD)
        C0 = part(KD * CTX).rearrange("p (k t) -> p k t", k=KD)
        YR = part(KD * T).rearrange("p (k t) -> p k t", k=KD)
        YS = part(KD * T).rearrange("p (k t) -> p k t", k=KD)
        CV = part(6 * T).rearrange("p (k t) -> p k t", k=6)
        Z = part(CONV_T * (T + 2)).rearrange("p (k t) -> p k t", k=CONV_T)
        SU = part(2 * T).rearrange("p (k t) -> p k t", k=2)
        SV = part(TB * BLK).rearrange("p (b c) -> p b c", b=TB)
        Q = part(4 * T).rearrange("p (k t) -> p k t", k=4)
        K = part(4 * KEYS).rearrange("p (k t) -> p k t", k=4)
        V = part(4 * 512).rearrange("p (c n) -> p c n", c=4)
        PR = part(3 * KEYS).rearrange("p (b n) -> p b n", b=3)
        PT = part(3 * KEYS).rearrange("p (b c n) -> p b c n", b=3, c=4)
        swt = part(SGU_G * P).rearrange("p (g n) -> p g n", g=SGU_G)
        sg_gain = part(BLK)
        assert at[0] <= 24576
        SVS = PT[:, 0, :, :].rearrange("p c n -> p (c n)").rearrange("p (b c) -> p b c", b=TB)
        sgb_row = PR[0:1, 0, :]
        g2_row = A[0:1, 12288:12288 + D]
        WR = part(RING * KD * BLK, 24576).rearrange("p (s k n) -> p s k n", s=RING, k=KD)
        SQ = part(KD * KEYS, 15364).rearrange("p (k t) -> p k t", k=KD)
        YN = A[:, 2048:4096].rearrange("p (k t) -> p k t", k=KD)
        H2 = A[:, 4096:6144].rearrange("p (k t) -> p k t", k=KD)
        SK = A[:, 6144:8192].rearrange("p (l n) -> p l n", l=LISTS)
        QP = A[:, 8192:12288].rearrange("p (l t) -> p l t", l=LISTS)
        S = A[:, 28672:32768].rearrange("p (b l n) -> p b l n", b=TB, l=LISTS)
        BIG = A[:, 24576:26624]
        LST = A[:, 26624:26880].rearrange("p (l n) -> p l n", l=2)
        LS2 = A[:, 26880:27136].rearrange("p (l n) -> p l n", l=2)
        CND = A[:, 27136:27392]
        CN2 = A[:, 27392:27648]
        all_i = A[:, 27648:28160].rearrange("p (n l k) -> p n l k", l=2, k=TOPK)
        all_v = A[:, 28160:28416].rearrange("p (n k) -> p n k", k=TOPK)
        all_p = A[:, 28416:28672].bitcast(U32).rearrange("p (n k) -> p n k", k=TOPK)
        digit = A[:, 26880:27136].bitcast(U32).rearrange("p (l n) -> p l n", l=2)
        assert 24576 == SCRATCH_CHUNK * T

        bias = sbuf("stage", [P, SLOTS, D])
        stage = bias
        BM = bias[:, :, :].rearrange("p s d -> p (s d)").rearrange("p (h b n) -> p h b n", h=HEADS, b=TB)
        hi = sbuf("hi", [P, 2, D], F32R)
        lo = sbuf("lo", [P, 2, D], F32R)
        h2_hi = sbuf("h2_hi", [P, KD, T], F32R)
        h2_lo = sbuf("h2_lo", [P, KD, T], F32R)
        w_hi = h2_hi[:, 0:2, :]
        w_lo = h2_lo[:, 0:2, :]
        x1n = sbuf("x1n", [P, TB, D])
        g2b = sbuf("g2b", [P, D])
        gate_buf = sbuf("gate_buf", [P, 4, GT, NK])
        ONE1 = gate_buf[:, 0:2]
        ONE2 = gate_buf[:, 2:4]
        crep = gate_buf[:, 0:2].rearrange("p a b c -> p (a b) c")
        rinv = gate_buf[:, 2, :, :].rearrange("p a b -> p (a b)")
        root = gate_buf[:, 3, :, :].rearrange("p a b -> p (a b)")
        fin = gate_buf[:, :, :, :].rearrange("p a b c -> p (a b c)")[:, 0:D]
        choice = sbuf("choice", [P, 3, TB, P])
        choice_t = sbuf("choice_t", [P, 3, T])
        con = sbuf("con", [P, 4, P])
        ident, ones, group_ones, iota = (con[:, n, :] for n in range(4))
        colv = sbuf("colv", [P, COLS])
        csil = sbuf("csil", [P, KD, 2])
        mod = sbuf("mod", [P, 5, KD, 2])
        gain1 = sbuf("gain1", [P, KD, 2])
        gain2 = sbuf("gain2", [P, KD])
        eps = sbuf("eps", [P, 1])
        gms = sbuf("gms", [P, 3, TB * SGU_G])
        nmax = sbuf("nmax", [P, HEADS * TB])
        psum_ = sbuf("psum_", [P, HEADS * TB])
        pinv = sbuf("pinv", [P, HEADS * TB])
        top_v = sbuf("top_v", [P, 2, TOPK])
        top_i = sbuf("top_i", [P, 2, TOPK], U32)
        best_v = sbuf("best_v", [P, TOPK])
        best_p = sbuf("best_p", [P, TOPK], U32)
        gsum = sbuf("gsum", [P, 2, TB * PH])
        fsum = sbuf("fsum", [P, 3, TB * 2])

        consts_in, x_in, cols_in, late_in, bias_in, g2_row_in = map(
            sem, ("consts_in", "x_in", "cols_in", "late_in", "bias_in", "g2_row_in"))
        ring_full = [sem(f"ring_full{s}") for s in range(RING)]
        ring_read = sem("ring_read")
        bank_full = [sem(f"bank_full{b}") for b in range(8)]
        bank_free = [sem(f"bank_free{b}") for b in range(8)]
        dve_done = sem("dve_done")
        act_done = sem("act_done")
        silu_ready, crep_ready, sq_ready, root_ready, h_ready = map(
            sem, ("silu_ready", "crep_ready", "sq_ready", "root_ready", "h_ready"))
        proj_ready, sv_ready, svroot_ready, svn_ready = map(
            sem, ("proj_ready", "sv_ready", "svroot_ready", "svn_ready"))
        nmax_ready, exp_ready, prob_ready, pt_ready = map(sem, ("nmax_ready", "exp_ready", "prob_ready", "pt_ready"))
        yr_ready, ys_ready, yroot_ready, yn_ready = map(sem, ("yr_ready", "ys_ready", "yroot_ready", "yn_ready"))
        x1_ready, x1s_ready, h2_ready, h2_hi_ready, h2_split = map(
            sem, ("x1_ready", "x1s_ready", "h2_ready", "h2_hi_ready", "h2_split"))
        qp_ready, keys_ready = map(sem, ("qp_ready", "keys_ready"))
        eps_ready, gms_ready = sem("eps_ready"), sem("gms_ready")
        stage_full = [sem(f"stage_full{s}") for s in range(SLOTS)]
        hi_made, lo_made, chunk_done, a_made = map(sem, ("hi_made", "lo_made", "chunk_done", "a_made"))
        topk_seen = sem("topk_seen")
        topk_step, shifted, exped, choice_ready, scratch_free, turned, choice_t_ready = map(
            sem, ("topk_step", "shifted", "exped", "choice_ready", "scratch_free", "turned", "choice_t_ready"))
        one1_made, one2_made, gates_done, gated = map(sem, ("one1_made", "one2_made", "gates_done", "gated"))
        whi_made, wlo_made = map(sem, ("whi_made", "wlo_made"))
        fin_in, res_ready, fsq_ready, froot_ready, out_ready, stored = map(
            sem, ("fin_in", "res_ready", "fsq_ready", "froot_ready", "out_ready", "stored"))

        block = stack.enter_context(nc.Block())

        def opened(eng, name):
            b, use = place[name]
            if use:
                eng.wait_ge(bank_free[b], use)
            return bank[b]

        def full(eng, name):
            b, use = place[name]
            eng.wait_ge(bank_full[b], use + 1)
            return bank[b]

        def fill_sem(name):
            return bank_full[place[name][0]]

        def free_sem(name):
            return bank_free[place[name][0]]

        @block.sync
        def _(sp):
            sp.dma_start(colv[:, :], cols).then_inc(cols_in, 16)
            sp.dma_start(X1, x_t).then_inc(x_in, 16)
            sp.dma_start(C0, ctx_t).then_inc(x_in, 16)
            sp.dma_start(con[:, :, :], constants).then_inc(consts_in, 16)
            for n, (matrix, b) in enumerate(blocks):
                if n >= RING:
                    sp.wait_ge(ring_read, n - RING + 1)
                sp.dma_start(WR[:, n % RING], sources[matrix][b]).then_inc(ring_full[n % RING], 16)
                if n == RING - 1:
                    sp.dma_start(sgb_row, rows[:, 0:SGU_G * P]).then_inc(late_in, 16)
                    sp.dma_start(sg_gain, sgu_gain).then_inc(late_in, 16)
                    sp.dma_start(swt, sgu_wt).then_inc(late_in, 16)
                if n == 10:
                    sp.dma_start(BM, bias_mask).then_inc(bias_in, 16)
                if (matrix, b) == ("w_out", 0):
                    sp.wait_ge(h_ready, 2)
                    sp.dma_start(SK, subkeys_t).then_inc(late_in, 16)
                if (matrix, b) == ("w_q", 0):
                    sp.wait_ge(yr_ready, 1)
                    sp.dma_start(g2_row, rows[:, SGU_G * P:]).then_inc(g2_row_in, 16)
            b, use = place[("scores", HEADS * TB - 1)]
            sp.wait_ge(bank_full[b], use + 1)
            b, use = place[("scores", HEADS * TB - 2)]
            sp.wait_ge(bank_full[b], use + 1)
            for j in range(SLOTS):
                sp.dma_start(stage[:, j, :], peer_u_t[j]).then_inc(stage_full[j], 16)
            with sp.Fori(1, CHUNKS // SLOTS) as i:
                for j in range(SLOTS):
                    sp.wait_ge(lo_made, i * SLOTS + (j + 1 - SLOTS))
                    sp.dma_start(stage[:, j, :], peer_u_t[i * SLOTS + j]).then_inc(stage_full[j], 16)
            with sp.Fori(0, CHUNKS // SLOTS) as i:
                for j in range(SLOTS):
                    sp.wait_ge(lo_made, i * SLOTS + (CHUNKS + j + 1 - SLOTS))
                    sp.dma_start(stage[:, j, :], v_rows[i * SLOTS + j]).then_inc(stage_full[j], 16)
            sp.wait_ge(gates_done, GROUPS)
            sp.dma_start(fin, final_gain).then_inc(fin_in, 16)
            for tb in range(TB):
                sp.wait_ge(out_ready, tb + 1)
                sp.dma_start(out[tb * P:(tb + 1) * P, :], x1n[:, tb, :]).then_inc(stored, 16)
            sp.wait_ge(stored, 16 * TB)

        def spatial_gating(pe):
            o = opened(pe, "sgu")
            pe.wait_ge(svn_ready, 1)
            pe.wait_ge(late_in, 48)
            for g in range(SGU_G):
                for tb in range(TB):
                    half = slice(HD * (g % 2), HD * (g % 2) + HD)
                    oo = o[half, (g // 2) * T + tb * P:(g // 2) * T + (tb + 1) * P]
                    pe.matmul(oo, SV[:, tb, g * HD:(g + 1) * HD], swt[:, g, :], start=True, stop=False)
                    mm = pe.matmul(oo, ones[0:1, 0:HD], sgb_row[:, g * P:(g + 1) * P], start=False, stop=True)
            mm.then_inc(fill_sem("sgu"), 1)

        def attention(pe):
            pe.wait_ge(bias_in, 16)
            pe.wait_ge(proj_ready, 7)
            for u in range(HEADS * TB + 2):
                if u < HEADS * TB:
                    h, tb = u // 2, u % 2
                    o = opened(pe, ("scores", u))
                    pp = slice(HD * (h % 2), HD * (h % 2) + HD)
                    qq = Q[pp, h // 2, tb * P:(tb + 1) * P]
                    pe.matmul(o[:, 0:T], ident, BM[:, h, tb, :], start=True, stop=False)
                    pe.matmul(o[:, 0:T], qq, K[pp, h // 2, 0:T], start=False, stop=True)
                    pe.matmul(o[:, T:KEYS], qq, K[pp, h // 2, T:KEYS], start=True, stop=True)\
                      .then_inc(fill_sem(("scores", u)), 1)
                if u >= 2:
                    v = u - 2
                    h, tb = v // 2, v % 2
                    o = opened(pe, ("turned", v))
                    pe.wait_ge(prob_ready, v + 1)
                    for c in range(4):
                        mm = pe.transpose(o[:, c * P:(c + 1) * P], PR[:, v % 3, c * P:(c + 1) * P], ident)
                    mm.then_inc(fill_sem(("turned", v)), 1)
                    name = ("attended", v // 4)
                    o = opened(pe, name) if v % 4 == 0 else bank[place[name][0]]
                    pe.wait_ge(pt_ready, v + 1)
                    for c in range(4):
                        mm = pe.matmul(o[HD * (h % 2):HD * (h % 2) + HD, tb * P:(tb + 1) * P],
                                       V[:, c, h * HD:(h + 1) * HD], PT[:, v % 3, c, :],
                                       start=(c == 0), stop=(c == 3))
                    if v % 4 == 3:
                        mm.then_inc(fill_sem(name), 1)

        def group_sums(pe):
            for j in range(4):
                o = opened(pe, ("group", j))
                pe.wait_ge(ys_ready, j + 1)
                pe.matmul(o[:, :], group_ones, YS[:, 2 * j:2 * j + 2, :], start=True, stop=True)\
                  .then_inc(fill_sem(("group", j)), 1)

        @block.tensor
        def _(pe):
            def weights(block_name):
                n = ring_of[block_name]
                pe.wait_ge(ring_full[n % RING], 16 * (n // RING + 1))
                return WR[:, n % RING]

            def contract(o, lhs, rhs, n=KD):
                for k in range(n):
                    mm = pe.matmul(o, lhs(k), rhs(k), start=(k == 0), stop=(k == n - 1))
                return mm

            def modulation(b):
                s = b // 4
                o = bank[place[("mod", s)][0]]
                if b % 4 == 0:
                    o = opened(pe, ("mod", s))
                w = weights(("ada", b))
                for m in range(2):
                    c = 2 * (2 * (b % 4) + m)
                    mm = contract(o[:, c:c + 2], lambda k: w[:, k, m * P:(m + 1) * P], lambda k: csil[:, k, :])
                mm.then_inc(ring_read, 1)
                return mm, s

            def in_projection(b):
                w = weights(("w_in", b))
                if b in (0, 1, 2, 3, 5, 6):
                    o = opened(pe, ("w_in", b, 0))
                    for m in range(2):
                        mm = contract(o[:, m * T:(m + 1) * T], lambda k: w[:, k, m * P:(m + 1) * P],
                                      lambda k: H[:, k, 0:T])
                    mms = [mm]
                elif b == 4:
                    o = opened(pe, ("w_in", b, 0))
                    for t in range(TB):
                        mm = contract(o[:, t * BLK:(t + 1) * BLK], lambda k: H[:, k, t * P:(t + 1) * P],
                                      lambda k: w[:, k, :])
                    mms = [mm]
                elif b in (7, 8):
                    mms = []
                    for m in range(2):
                        o = opened(pe, ("w_in", b, m))
                        mms.append(contract(o[:, :], lambda k: w[:, k, m * P:(m + 1) * P], lambda k: H[:, k, :]))
                else:
                    mms = []
                    for m in range(2):
                        o = opened(pe, ("w_in", b, m))
                        for c in range(2):
                            t = 2 * m + c
                            mm = contract(o[:, c * BLK:(c + 1) * BLK], lambda k: H[:, k, t * P:(t + 1) * P],
                                          lambda k: w[:, k, :])
                        mms.append(mm)
                return mms

            pe.wait_ge(consts_in, 16)
            pe.wait_ge(sq_ready, 2)
            o = opened(pe, "stat1")
            contract(o[:, :], lambda k: ones, lambda k: SQ[:, k, :]).then_inc(fill_sem("stat1"), 1)
            pe.wait_ge(silu_ready, 1)
            for matrix, b in blocks:
                if matrix == "ada" and b // 4 < G2:
                    mm, s = modulation(b)
                    if b % 4 == 3:
                        pe.wait_ge(ring_read, ring_of[("ada", b)] + 1)
                        pe.sem_inc(fill_sem(("mod", s)), 1)
                elif matrix == "w_in":
                    if b == 3:
                        pe.wait_ge(h_ready, 2)
                    mms = in_projection(b)
                    for half, mm in enumerate(mms):
                        mm.then_inc(fill_sem(("w_in", b, half)), 1)
                    pe.wait_ge(bank_full[place[("w_in", b, len(mms) - 1)][0]],
                               place[("w_in", b, len(mms) - 1)][1] + 1)
                    pe.sem_inc(ring_read, 1)
                    if b == 2:
                        spatial_gating(pe)
                elif matrix == "w_out":
                    if b == 0:
                        attention(pe)
                        group_sums(pe)
                        pe.wait_ge(yn_ready, KD)
                    w = weights((matrix, b))
                    o = opened(pe, (matrix, b, 0))
                    for m in range(2):
                        mm = contract(o[:, m * T:(m + 1) * T], lambda k: w[:, k, m * P:(m + 1) * P],
                                      lambda k: YN[:, k, :])
                    mm.then_inc(fill_sem((matrix, b, 0)), 1)
                    pe.wait_ge(bank_full[place[(matrix, b, 0)][0]], place[(matrix, b, 0)][1] + 1)
                    pe.sem_inc(ring_read, 1)
                    if b == 3:
                        o = opened(pe, "stat2")
                        for m in range(KD):
                            if m % 2 == 0:
                                pe.wait_ge(x1s_ready, m // 2 + 1)
                            mm = pe.matmul(o[:, 0:T], ones, YS[:, m, :], start=(m == 0), stop=(m == KD - 1))
                        mm.then_inc(fill_sem("stat2"), 1)
                        for j in range(4):
                            o = opened(pe, ("x1_turned", j))
                            for m in range(4):
                                mm = pe.transpose(o[:, m * P:(m + 1) * P],
                                                  X1[:, 4 * (j % 2) + m, (j // 2) * P:(j // 2 + 1) * P], ident)
                            mm.then_inc(fill_sem(("x1_turned", j)), 1)
                elif matrix == "w_q":
                    if b == 0:
                        pe.wait_ge(h2_ready, KD)
                    w = weights((matrix, b))
                    o = opened(pe, (matrix, b, 0))
                    for m in range(2):
                        mm = contract(o[:, m * T:(m + 1) * T], lambda k: w[:, k, m * P:(m + 1) * P],
                                      lambda k: H2[:, k, :])
                    mm.then_inc(fill_sem((matrix, b, 0)), 1)
                    pe.wait_ge(bank_full[place[(matrix, b, 0)][0]], place[(matrix, b, 0)][1] + 1)
                    pe.sem_inc(ring_read, 1)
                else:
                    if b % 4 == 0:
                        pe.wait_ge(crep_ready, 1)
                        pe.wait_ge(g2_row_in, 16)
                    name, half = ("g2", b % 4 // 2), b % 2
                    w = weights(("ada", b))
                    o = opened(pe, name) if half == 0 else bank[place[name][0]]
                    c = b % 4 * BLK
                    for k in range(KD):
                        pe.matmul(o[:, half * BLK:(half + 1) * BLK], crep[:, k, :], w[:, k, :],
                                  start=(k == 0), stop=False)
                    mm = pe.matmul(o[:, half * BLK:(half + 1) * BLK], ones[0:1, :],
                                   g2_row[:, c:c + BLK], start=False, stop=True)
                    mm.then_inc(ring_read, 1)
                    if half == 1:
                        pe.wait_ge(ring_read, ring_of[("ada", b)] + 1)
                        pe.sem_inc(fill_sem(name), 1)

            pe.wait_ge(late_in, 64)
            for tb in range(TB):
                for l4 in range(LISTS // 4):
                    name = ("keys", tb, l4)
                    o = opened(pe, name)
                    pe.wait_ge(qp_ready, 2 * l4 + 2)
                    for m in range(4):
                        lst = 4 * l4 + m
                        mm = pe.matmul(o[:, m * P:(m + 1) * P], QP[:, lst, tb * P:(tb + 1) * P], SK[:, lst, :],
                                       start=True, stop=True)
                    mm.then_inc(fill_sem(name), 1)

            def u_chunk(j, c):
                pe.wait_ge(lo_made, c + 1)
                o = bank[j][:, 0:T]
                for k in range(KD):
                    kk = slice(k * P, (k + 1) * P)
                    pe.matmul(o, hi[:, j % 2, kk], h2_hi[:, k, :], start=(k == 0), stop=False)
                    pe.matmul(o, hi[:, j % 2, kk], h2_lo[:, k, :], start=False, stop=False)
                    mm = pe.matmul(o, lo[:, j % 2, kk], h2_hi[:, k, :], start=False, stop=(k == KD - 1))
                mm.then_inc(chunk_done, 1)

            pe.wait_ge(h2_split, KD)
            for b in range(SLOTS):
                pe.wait_ge(bank_free[b], used[b])
            for j in range(SLOTS):
                u_chunk(j, j)
            with pe.Fori(1, TURN_AT // SLOTS) as i:
                for j in range(SLOTS):
                    pe.wait_ge(a_made, i * SLOTS + (j + 1 - SLOTS))
                    u_chunk(j, i * SLOTS + j)
            pe.wait_ge(choice_ready, TB)
            for tb in range(TB):
                pe.wait_ge(bank_free[4 + tb], used[4 + tb])
                for n in range(3):
                    mm = pe.transpose(bank[4 + tb][:, n * P:(n + 1) * P], choice[:, n, tb, :], ident)
                mm.then_inc(turned, 1)
            with pe.Fori(TURN_AT // SLOTS, CHUNKS // SLOTS) as i:
                for j in range(SLOTS):
                    pe.wait_ge(a_made, i * SLOTS + (j + 1 - SLOTS))
                    u_chunk(j, i * SLOTS + j)

            def gates(j, g):
                pe.wait_ge(one1_made, g + 1)
                pe.wait_ge(one2_made, g + 1)
                for t in range(GT):
                    mm = pe.matmul(bank[j][:, t * NK:(t + 1) * NK], ONE1[:, j, t, :], ONE2[:, j, t, :],
                                   start=True, stop=True)
                mm.then_inc(gates_done, 1)

            pe.wait_ge(a_made, CHUNKS)
            for j in range(2):
                gates(j, j)
            with pe.Fori(1, GROUPS // 2) as i:
                for j in range(2):
                    pe.wait_ge(gated, i * 2 + (j - 1))
                    gates(j, i * 2 + j)

            def v_chunk(j, v, first=False, last=False):
                pe.wait_ge(lo_made, v + (CHUNKS + 1))
                pe.wait_ge(wlo_made, v + 1)
                for tb in range(TB):
                    for half in range(2):
                        o = bank[4 + 2 * tb + half][:, :]
                        tt = slice(tb * P, (tb + 1) * P)
                        dd = slice(half * 512, half * 512 + 512)
                        pe.matmul(o, w_hi[:, j, tt], hi[:, j, dd], start=first, stop=False)
                        pe.matmul(o, w_hi[:, j, tt], lo[:, j, dd], start=False, stop=False)
                        mm = pe.matmul(o, w_lo[:, j, tt], hi[:, j, dd], start=False, stop=last)
                mm.then_inc(chunk_done, 1)

            pe.wait_ge(choice_t_ready, TB)
            for b in (6, 7):
                pe.wait_ge(bank_free[b], used[b])
            v_chunk(0, 0, first=True)
            v_chunk(1, 1)
            with pe.Fori(1, CHUNKS // 2 - 1) as i:
                for j in range(2):
                    v_chunk(j, i * 2 + j)
            v_chunk(0, CHUNKS - 2)
            v_chunk(1, CHUNKS - 1, last=True)

        @block.scalar
        def _(act):
            act.wait_ge(cols_in, 16)
            act.activation(csil[:, :, :].rearrange("p k v -> p (k v)"), colv[:, COL_C:COL_C + 2 * KD],
                           ACT.Silu).then_inc(silu_ready, 1)
            act.wait_ge(x_in, 32)
            act.activation(SQ[:, :, 0:T], X1, ACT.Square).then_inc(sq_ready, 1)
            act.activation(SQ[:, :, T:KEYS], C0, ACT.Square).then_inc(sq_ready, 1)
            act.wait_ge(eps_ready, 1)
            o = full(act, "stat1")
            act.activation(root, o[:, :], ACT.Sqrt, bias=eps[:, :], scale=1.0 / D).then_inc(root_ready, 1)
            for matrix, b in blocks:
                if matrix != "w_in":
                    continue
                for half in range(2 if b >= 7 else 1):
                    name = (matrix, b, half)
                    o = full(act, name)
                    two = o[:, :].rearrange("p (m t) -> p m t", m=2)
                    if b == 3:
                        act.activation(SU, two, ACT.Gelu_apprx_tanh).then_inc(bank_free[place[name][0]], 1)
                    elif b == 4:
                        act.activation(SV, two, ACT.Gelu_apprx_tanh).then_inc(bank_free[place[name][0]], 1)
                        act.wait_ge(bank_free[place[name][0]], place[name][1] + 1)
                        act.activation(SVS, SV, ACT.Square).then_inc(sv_ready, 1)
                    elif b in (5, 6):
                        act.activation(Q[:, 2 * (b - 5):2 * (b - 5) + 2, :], two, ACT.Copy, scale=HD ** -0.5)\
                           .then_inc(bank_free[place[name][0]], 1)
                    elif b in (7, 8):
                        act.activation(K[:, 2 * (b - 7) + half, :], o[:, :], ACT.Copy)\
                           .then_inc(bank_free[place[name][0]], 1)
                    elif b in (9, 10):
                        act.activation(V[:, 2 * half:2 * half + 2, (b - 9) * BLK:(b - 8) * BLK], two, ACT.Copy)\
                           .then_inc(bank_free[place[name][0]], 1)
                    else:
                        act.activation(CV[:, 2 * b:2 * b + 2, :], two, ACT.Copy)\
                           .then_inc(bank_free[place[name][0]], 1)
                    act.wait_ge(bank_free[place[name][0]], place[name][1] + 1)
                    if half == (1 if b >= 7 else 0):
                        act.sem_inc(proj_ready, 1)
                if b == 5:
                    act.wait_ge(gms_ready, 1)
                    act.activation(gms[:, 1, :], gms[:, 0, :], ACT.Sqrt, bias=eps[:, :], scale=1.0 / HD)\
                       .then_inc(svroot_ready, 1)

            def exp_unit(u):
                o = full(act, ("scores", u))
                act.wait_ge(nmax_ready, u + 1)
                if u >= 3:
                    name = ("turned", u - 3)
                    act.wait_ge(bank_full[place[name][0]], place[name][1] + 1)
                act.activation(PR[:, u % 3, :], o[:, :], ACT.Exp, bias=nmax[:, u:u + 1],
                               accum_out=psum_[:, u:u + 1]).then_inc(exp_ready, 1)

            for u in range(HEADS * TB + 2):
                if u < HEADS * TB:
                    exp_unit(u)
                if u >= 2:
                    v = u - 2
                    name = ("turned", v)
                    o = full(act, name)
                    if v >= 3:
                        act.wait_ge(bank_full[place[("turned", v - 2)][0]], place[("turned", v - 2)][1] + 1)
                    act.activation(PT[:, v % 3, :, :].rearrange("p c n -> p (c n)"), o[:, :], ACT.Copy)\
                       .then_inc(pt_ready, 1)
                    act.wait_ge(pt_ready, v + 1)
                    act.sem_inc(free_sem(name), 1)

            for j in range(4):
                act.wait_ge(yr_ready, j + 1)
                act.activation(YS[:, 2 * j:2 * j + 2, :], YR[:, 2 * j:2 * j + 2, :], ACT.Square)\
                   .then_inc(ys_ready, 1)
            for j in range(4):
                o = full(act, ("group", j))
                if j:
                    act.wait_ge(yn_ready, 2 * j)
                act.activation(root, o[:, :], ACT.Sqrt, bias=eps[:, :], scale=1.0 / HD)\
                   .then_inc(yroot_ready, 1)
            for b in range(4):
                act.wait_ge(x1_ready, b + 1)
                act.activation(YS[:, 2 * b:2 * b + 2, :], X1[:, 2 * b:2 * b + 2, :], ACT.Square)\
                   .then_inc(x1s_ready, 1)
            o = full(act, "stat2")
            act.activation(root[:, 0:T], o[:, 0:T], ACT.Sqrt, bias=eps[:, :], scale=1.0 / D)\
               .then_inc(root_ready, 1)
            for j in range(4):
                name = ("x1_turned", j)
                o = full(act, name)
                act.activation(x1n[:, j // 2, (j % 2) * 512:(j % 2) * 512 + 512], o[:, :], ACT.Copy)\
                   .then_inc(free_sem(name), 1)
            for k in range(KD):
                act.wait_ge(h2_ready, k + 1)
                act.activation(h2_hi[:, k, :], H2[:, k, :], ACT.Copy).then_inc(h2_hi_ready, 1)
            for b in range(LISTS // 2):
                name = ("w_q", b, 0)
                o = full(act, name)
                act.activation(QP[:, 2 * b:2 * b + 2, :].rearrange("p l t -> p (l t)"), o[:, :], ACT.Copy)\
                   .then_inc(qp_ready, 1)
                act.wait_ge(qp_ready, b + 1)
                act.sem_inc(free_sem(name), 1)
            for half in range(2):
                o = full(act, ("g2", half))
                act.activation(g2b[:, half * 512:half * 512 + 512], o[:, :], ACT.Copy)\
                   .then_inc(free_sem(("g2", half)), 1)
            for tb in range(TB):
                for l4 in range(LISTS // 4):
                    name = ("keys", tb, l4)
                    o = full(act, name)
                    act.activation(S[:, tb, 4 * l4:4 * l4 + 4, :].rearrange("p l n -> p (l n)"), o[:, :],
                                   ACT.Copy).then_inc(keys_ready, 1)
                    act.wait_ge(keys_ready, tb * (LISTS // 4) + l4 + 1)
                    act.sem_inc(free_sem(name), 1)

            def round_chunk(j, use):
                act.wait_ge(stage_full[j], use)
                act.activation(hi[:, j % 2, :], stage[:, j, :], ACT.Copy).then_inc(hi_made, 1)

            def gelu_chunk(j, c):
                act.activation(A3[:, c, :], bank[j][:, 0:T], ACT.Gelu_apprx_tanh).then_inc(a_made, 1)

            def u_steps(i, j):
                act.wait_ge(chunk_done, i * SLOTS + (j - 1))
                round_chunk(j, i * (16 * SLOTS // 4) + 16)
                gelu_chunk((j - 2) % SLOTS, i * SLOTS + (j - 2))

            for c in range(SLOTS):
                if c >= 2:
                    act.wait_ge(chunk_done, c - 1)
                round_chunk(c, 16)
                if c >= 2:
                    gelu_chunk(c - 2, c - 2)
            with act.Fori(1, DECODE_UNTIL // SLOTS) as i:
                for j in range(SLOTS):
                    u_steps(i, j)
            act.wait_ge(shifted, TB)
            act.activation(choice[:, 2, :, :], choice[:, 2, :, :], ACT.Exp).then_inc(exped, 1)
            with act.Fori(DECODE_UNTIL // SLOTS, SCRATCH_CHUNK // SLOTS) as i:
                for j in range(SLOTS):
                    u_steps(i, j)
            act.wait_ge(scratch_free, 1)
            with act.Fori(SCRATCH_CHUNK // SLOTS, CHUNKS // SLOTS) as i:
                for j in range(SLOTS):
                    u_steps(i, j)
            for j in range(2):
                act.wait_ge(chunk_done, CHUNKS - 1 + j)
                round_chunk(j, 16 * (CHUNKS // SLOTS) + 16)
                gelu_chunk(2 + j, CHUNKS - 2 + j)

            def v_steps(i, j, table=True):
                act.activation(w_hi[:, j % 2, :], A3[:, i * SLOTS + j, :], ACT.Copy).then_inc(whi_made, 1)
                if table:
                    act.wait_ge(chunk_done, i * SLOTS + (CHUNKS + j + 1))
                    round_chunk((j + 2) % SLOTS, i * 16 + (16 * (CHUNKS // SLOTS) + (16 if j < 2 else 32)))

            act.wait_ge(gated, GROUPS)
            v_first = CHUNKS // SLOTS - 1
            with act.Fori(0, 1) as i:
                for j in range(2):
                    act.activation(w_hi[:, j, :], A3[:, i + j, :], ACT.Copy).then_inc(whi_made, 1)
            for j in range(2):
                act.wait_ge(chunk_done, CHUNKS + j + 1)
                round_chunk(j + 2, 16 * (CHUNKS // SLOTS) + 16)
                act.activation(w_hi[:, j, :], A3[:, 2 + j, :], ACT.Copy).then_inc(whi_made, 1)
            with act.Fori(1, CHUNKS // SLOTS) as i:
                for j in range(SLOTS):
                    act.wait_ge(chunk_done, i * SLOTS + (CHUNKS + j - 1))
                    round_chunk(j, i * 16 + (16 * (CHUNKS // SLOTS) + 16))
                    act.activation(w_hi[:, j % 2, :], A3[:, i * SLOTS + j, :], ACT.Copy).then_inc(whi_made, 1)

            for n in range(2 * TB):
                tb, half = n // 2, n % 2
                act.wait_ge(res_ready, n + 1)
                act.activation(A[:, n * 512:n * 512 + 512], x1n[:, tb, half * 512:half * 512 + 512], ACT.Square,
                               accum_out=fsum[:, 0, n:n + 1]).then_inc(fsq_ready, 1)
            act.wait_ge(fsq_ready, 2 * TB + 1)
            act.activation(fsum[:, 2, 0:TB], fsum[:, 1, 0:TB], ACT.Sqrt, bias=eps[:, :], scale=1.0 / D)\
               .then_inc(froot_ready, 1)

        @block.vector
        def _(dve):
            chain = [0]

            def link(ins):
                chain[0] += 1
                ins.then_inc(dve_done, 1)
                dve.wait_ge(dve_done, chain[0])

            dve.memset(eps[:, :], EPS).then_inc(eps_ready, 1)
            dve.memset(Z[:, :, 0:1], 0.0)
            link(dve.memset(Z[:, :, T + 1:T + 2], 0.0))
            dve.wait_ge(silu_ready, 1)
            dve.tensor_copy(crep, csil[:, :, 0:1].broadcast_to([P, KD, P])).then_inc(crep_ready, 1)
            dve.wait_ge(root_ready, 1)
            link(dve.reciprocal(rinv, root))
            dve.sem_inc(free_sem("stat1"), 1)
            rb = lambda a, b: rinv[:, a:b].unsqueeze(1).broadcast_to([P, KD, b - a])
            dve.tensor_tensor(H[:, :, 0:T], X1, rb(0, T), ALU.mult)
            link(dve.tensor_tensor(H[:, :, T:KEYS], C0, rb(T, KEYS), ALU.mult))

            def modulation(s):
                o = full(dve, ("mod", s))
                b = colv[:, COL_ADA_B + s * KD:COL_ADA_B + (s + 1) * KD].unsqueeze(2).broadcast_to([P, KD, 2])
                link(dve.tensor_tensor(mod[:, s, :, :], o[:, 0:2 * KD].rearrange("p (k v) -> p k v", v=2), b, ALU.add))
                dve.sem_inc(free_sem(("mod", s)), 1)

            modulation(SH1)
            modulation(SC1)
            link(dve.scalar_tensor_tensor(gain1[:, :, :], mod[:, SC1, :, :], 1.0,
                                          colv[:, COL_N1:COL_N1 + KD].unsqueeze(2).broadcast_to([P, KD, 2]),
                                          ALU.add, ALU.mult))
            for v in range(2):
                for k in range(KD):
                    h = H[:, k, v * T:(v + 1) * T]
                    ins = dve.tensor_scalar(h, h, gain1[:, k, v:v + 1], mod[:, SH1, k, v:v + 1], ALU.mult, ALU.add)
                ins.then_inc(h_ready, 1)

            dve.wait_ge(sv_ready, 1)
            dve.wait_ge(late_in, 48)
            groups = "p b (g c) -> p (b g) c"
            dve.tensor_reduce(gms[:, 0, :], SVS.rearrange(groups, c=HD), AX.X, ALU.add).then_inc(gms_ready, 1)
            dve.wait_ge(svroot_ready, 1)
            link(dve.reciprocal(gms[:, 2, :], gms[:, 1, :]))
            link(dve.tensor_tensor(SV.rearrange(groups, c=HD), SV.rearrange(groups, c=HD),
                                   gms[:, 2, :].unsqueeze(2).broadcast_to([P, TB * SGU_G, HD]), ALU.mult))
            dve.tensor_tensor(SV, SV, sg_gain.unsqueeze(1).broadcast_to([P, TB, BLK]), ALU.mult)\
               .then_inc(svn_ready, 1)
            for s in (G1, SH2, SC2):
                modulation(s)
            link(dve.scalar_tensor_tensor(gain2[:, :], mod[:, SC2, :, 0], 1.0, colv[:, COL_N2:COL_N2 + KD],
                                          ALU.add, ALU.mult))

            dve.wait_ge(proj_ready, 11)
            link(dve.tensor_tensor(Z[:, :, 1:T + 1], CV[:, 2:4, :], CV[:, 4:6, :], ALU.mult))
            for tap in range(3):
                for m in range(CONV_T):
                    w = colv[:, COL_CONV + 3 * m + tap:COL_CONV + 3 * m + tap + 1]
                    z = Z[:, m, tap:tap + T]
                    if tap == 0:
                        ins = dve.tensor_scalar(YR[:, m, :], z, w, None, ALU.mult)
                    else:
                        ins = dve.scalar_tensor_tensor(YR[:, m, :], z, w, YR[:, m, :], ALU.mult, ALU.add)
                link(ins)
            dve.tensor_tensor(YR[:, 0:2, :], YR[:, 0:2, :], CV[:, 0:2, :], ALU.mult).then_inc(yr_ready, 1)
            o = full(dve, "sgu")
            link(dve.tensor_tensor(YR[:, 2:4, :], SU, o[:, :].rearrange("p (m t) -> p m t", m=2), ALU.mult))
            dve.sem_inc(yr_ready, 1)
            dve.sem_inc(free_sem("sgu"), 1)

            for u in range(HEADS * TB + 3):
                if u < HEADS * TB:
                    o = full(dve, ("scores", u))
                    dve.tensor_reduce(nmax[:, u:u + 1], o[:, :], AX.X, ALU.max, negate=True).then_inc(nmax_ready, 1)
                if 1 <= u <= HEADS * TB:
                    v = u - 1
                    dve.wait_ge(exp_ready, v + 1)
                    dve.sem_inc(free_sem(("scores", v)), 1)
                    link(dve.reciprocal(pinv[:, v:v + 1], psum_[:, v:v + 1]))
                    dve.tensor_scalar(PR[:, v % 3, :], PR[:, v % 3, :], pinv[:, v:v + 1], None, ALU.mult)\
                       .then_inc(prob_ready, 1)
                if u >= 3 and (u - 3) % 4 == 3:
                    j = (u - 3) // 4
                    o = full(dve, ("attended", j))
                    link(dve.tensor_copy(YR[:, 4 + j, :], o[:, 0:T]))
                    dve.sem_inc(free_sem(("attended", j)), 1)
                    if j % 2:
                        dve.sem_inc(yr_ready, 1)
            for j in range(4):
                dve.wait_ge(yroot_ready, j + 1)
                dve.sem_inc(free_sem(("group", j)), 1)
                link(dve.reciprocal(rinv, root))
                for m in range(2):
                    k = 2 * j + m
                    dve.scalar_tensor_tensor(YN[:, k, :], YR[:, k, :], colv[:, COL_OG + k:COL_OG + k + 1],
                                             rinv[:, m * T:(m + 1) * T], ALU.mult, ALU.mult).then_inc(yn_ready, 1)
                dve.wait_ge(yn_ready, 2 * j + 2)
            for b in range(4):
                name = ("w_out", b, 0)
                o = full(dve, name)
                for m in range(2):
                    k = 2 * b + m
                    ins = dve.scalar_tensor_tensor(X1[:, k, :], o[:, m * T:(m + 1) * T], mod[:, G1, k, 0:1],
                                                   X1[:, k, :], ALU.mult, ALU.add)
                ins.then_inc(x1_ready, 1)
                dve.wait_ge(x1_ready, b + 1)
                dve.sem_inc(free_sem(name), 1)
            dve.wait_ge(root_ready, 2)
            dve.sem_inc(free_sem("stat2"), 1)
            link(dve.reciprocal(rinv[:, 0:T], root[:, 0:T]))
            link(dve.tensor_tensor(H2, X1, rb(0, T), ALU.mult))
            for k in range(KD):
                dve.tensor_scalar(H2[:, k, :], H2[:, k, :], gain2[:, k:k + 1], mod[:, SH2, k, 0:1], ALU.mult,
                                  ALU.add).then_inc(h2_ready, 1)
            for k in range(KD):
                dve.wait_ge(h2_hi_ready, k + 1)
                dve.tensor_tensor(h2_lo[:, k, :], H2[:, k, :], h2_hi[:, k, :].bitcast(F32), ALU.subtract)\
                   .then_inc(h2_split, 1)

            def rest(j, c):
                dve.wait_ge(hi_made, c + 1)
                dve.tensor_tensor(lo[:, j % 2, :], stage[:, j, :], hi[:, j % 2, :].bitcast(F32), ALU.subtract)\
                   .then_inc(lo_made, 1)

            dve.wait_ge(keys_ready, TB * LISTS // 4)
            SN = A[:, 28672:32768].rearrange("p (n l k) -> p n l k", l=2, k=NK)
            STEPS = 11
            with dve.Fori(0, TB * PH) as n:
                def step(k):
                    dve.wait_ge(topk_step, n * STEPS + k)
                    dve.sem_inc(topk_seen, 1)

                dve.tensor_copy(LST, SN[:, n, :, :]).then_inc(topk_step, 1)
                rest(0, n * 4)
                step(1)
                for p in range(2):
                    last = dve.max(top_v[:, p, 0:8], LST[:, p, :])
                last.then_inc(topk_step, 1)
                step(2)
                for p in range(2):
                    dve.max_index(top_i[:, p, 0:8], top_v[:, p, 0:8], LST[:, p, :])
                    last = dve.match_replace(LS2[:, p, :], top_v[:, p, 0:8], LST[:, p, :], LOWEST)
                last.then_inc(topk_step, 1)
                rest(1, n * 4 + 1)
                step(3)
                for p in range(2):
                    last = dve.max(top_v[:, p, 8:16], LS2[:, p, :])
                last.then_inc(topk_step, 1)
                step(4)
                for p in range(2):
                    last = dve.max_index(top_i[:, p, 8:16], top_v[:, p, 8:16], LS2[:, p, :])
                last.then_inc(topk_step, 1)
                dve.tensor_tensor(CND.rearrange("p (a b) -> p a b", b=TOPK),
                                  top_v[:, 0, :].unsqueeze(2).broadcast_to([P, TOPK, TOPK]),
                                  top_v[:, 1, :].unsqueeze(1).broadcast_to([P, TOPK, TOPK]),
                                  ALU.add).then_inc(topk_step, 1)
                rest(2, n * 4 + 2)
                step(6)
                dve.tensor_copy(all_i[:, n, :, :], top_i[:, :, :])
                dve.max(best_v[:, 0:8], CND).then_inc(topk_step, 1)
                step(7)
                dve.max_index(best_p[:, 0:8], best_v[:, 0:8], CND)
                dve.match_replace(CN2, best_v[:, 0:8], CND, LOWEST).then_inc(topk_step, 1)
                step(8)
                dve.max(best_v[:, 8:16], CN2).then_inc(topk_step, 1)
                rest(3, n * 4 + 3)
                step(9)
                dve.max_index(best_p[:, 8:16], best_v[:, 8:16], CN2).then_inc(topk_step, 1)
                step(10)
                dve.tensor_copy(all_v[:, n, :], best_v[:, :])
                dve.tensor_copy(all_p[:, n, :], best_p[:, :]).then_inc(topk_step, 1)
                step(11)

            chunk = [TOPK_UNTIL]

            def another():
                rest(chunk[0] % SLOTS, chunk[0])
                chunk[0] += 1

            iota16 = iota[:, 0:TOPK].unsqueeze(1).broadcast_to([P, PH * TOPK, TOPK])
            for tb in range(TB):
                heads = slice(tb * PH, (tb + 1) * PH)
                dve.tensor_tensor(choice[:, 2, tb, :].rearrange("p (h k) -> p h k", k=TOPK), all_v[:, heads, :],
                                  all_v[:, heads, 0:1].broadcast_to([P, PH, TOPK]), ALU.subtract)\
                   .then_inc(shifted, 1)
                places = all_p[:, heads, :].rearrange("p h k -> p (h k)")
                dve.tensor_scalar(digit[:, 0, :], places, 4, None, ALU.logical_shift_right)
                link(dve.tensor_scalar(digit[:, 1, :], places, TOPK - 1, None, ALU.bitwise_and))
                for p in range(2):
                    b3 = BIG.rearrange("p (m a) -> p m a", a=TOPK)
                    another()
                    link(dve.tensor_tensor(b3, digit[:, p, :].unsqueeze(2).broadcast_to([P, PH * TOPK, TOPK]),
                                           iota16, ALU.is_equal))
                    another()
                    b4 = BIG.rearrange("p (h k a) -> p h k a", k=TOPK, a=TOPK)
                    link(dve.tensor_tensor(b4, b4, all_i[:, heads, p, :].unsqueeze(2)
                                           .broadcast_to([P, PH, TOPK, TOPK]), ALU.mult))
                    another()
                    link(dve.tensor_reduce(choice[:, p, tb, :], b3, AX.X, ALU.add))
                another()
                another()
            while chunk[0] < DECODE_UNTIL:
                another()
            dve.sem_inc(scratch_free, 1)
            another()
            dve.wait_ge(exped, 1)
            e3 = choice[:, 2, :, :].rearrange("p b (h k) -> p (b h) k", k=TOPK)
            link(dve.tensor_reduce(gsum[:, 0, :], e3, AX.X, ALU.add))
            another()
            link(dve.reciprocal(gsum[:, 1, :], gsum[:, 0, :]))
            another()
            dve.tensor_tensor(e3, e3, gsum[:, 1, :].unsqueeze(2).broadcast_to([P, TB * PH, TOPK]), ALU.mult)\
               .then_inc(choice_ready, TB)
            another()
            with dve.Fori(SOFTMAX_UNTIL // SLOTS, TURN_AT // SLOTS + 1) as i:
                for j in range(SLOTS):
                    rest(j, i * SLOTS + j)
            for tb in range(TB):
                dve.wait_ge(turned, tb + 1)
                dve.tensor_copy(choice_t[:, :, tb * P:(tb + 1) * P],
                                bank[4 + tb][:, 0:3 * P].rearrange("p (n t) -> p n t", n=3))\
                   .then_inc(choice_t_ready, 1)
            with dve.Fori(TURN_AT // SLOTS + 1, CHUNKS // SLOTS) as i:
                for j in range(SLOTS):
                    rest(j, i * SLOTS + j)
            for j in range(2):
                rest(j, CHUNKS + j)

            def one1(j, g):
                dve.tensor_tensor(ONE1[:, j], iota.unsqueeze(1).broadcast_to([P, GT, NK]),
                                  choice_t[:, 0, bass.ds(g * GT, GT)].unsqueeze(2).broadcast_to([P, GT, NK]),
                                  ALU.is_equal).then_inc(one1_made, 1)

            def one2(j, g):
                for t in range(GT):
                    tt = g * GT + t
                    last = dve.tensor_scalar(ONE2[:, j, t, :], iota, choice_t[:, 1, bass.ds(tt, 1)],
                                             choice_t[:, 2, bass.ds(tt, 1)], ALU.is_equal, ALU.mult)
                last.then_inc(one2_made, 1)

            def gate(j, g):
                dve.wait_ge(gates_done, g + 1)
                a = A3[:, :, bass.ds(g * GT, GT)]
                dve.tensor_tensor(a, a, bank[j][:, :].rearrange("p (t c) -> p c t", t=GT), ALU.mult)\
                   .then_inc(gated, 1)

            dve.wait_ge(choice_t_ready, TB)
            for j in range(2):
                one1(j, j)
                one2(j, j)
            dve.wait_ge(a_made, CHUNKS)
            with dve.Fori(1, GROUPS // 2) as i:
                for j in range(2):
                    gate(j, i * 2 + (j - 2))
                    one1(j, i * 2 + j)
                    one2(j, i * 2 + j)
            for j in range(2):
                gate(j, GROUPS - 2 + j)

            def w_rest(j, v):
                dve.wait_ge(whi_made, v + 1)
                dve.tensor_tensor(w_lo[:, j % 2, :], A3[:, v, :], w_hi[:, j % 2, :].bitcast(F32), ALU.subtract)\
                   .then_inc(wlo_made, 1)

            dve.wait_ge(gated, GROUPS)
            with dve.Fori(0, 1) as i:
                for j in range(2):
                    w_rest(j, i + j)
            for j in (2, 3):
                rest(j, CHUNKS + j)
                w_rest(j, j)
            with dve.Fori(1, CHUNKS // SLOTS) as i:
                for j in range(SLOTS):
                    rest(j, i * SLOTS + (CHUNKS + j))
                    w_rest(j, i * SLOTS + j)

            dve.wait_ge(chunk_done, 2 * CHUNKS)
            for n in range(2 * TB):
                tb, half = n // 2, slice(n % 2 * 512, n % 2 * 512 + 512)
                tmp = A[:, 4096 + n * 512:4096 + n * 512 + 512]
                link(dve.tensor_tensor(tmp, bank[4 + n][:, :], g2b[:, half], ALU.mult))
                dve.tensor_tensor(x1n[:, tb, half], x1n[:, tb, half], tmp, ALU.add).then_inc(res_ready, 1)
            dve.wait_ge(fsq_ready, 2 * TB)
            dve.tensor_reduce(fsum[:, 1, 0:TB], fsum[:, 0, :].rearrange("p (b h) -> p b h", h=2), AX.X, ALU.add)\
               .then_inc(fsq_ready, 1)
            dve.wait_ge(froot_ready, 1)
            link(dve.reciprocal(fsum[:, 1, TB:2 * TB], fsum[:, 2, 0:TB]))
            dve.wait_ge(fin_in, 16)
            dve.wait_ge(res_ready, 2 * TB)
            for tb in range(TB):
                dve.scalar_tensor_tensor(x1n[:, tb, :], x1n[:, tb, :], fsum[:, 1, TB + tb:TB + tb + 1], fin,
                                         ALU.mult, ALU.mult).then_inc(out_ready, 1)


def bias_places():
    import numpy as np

    grid_w, kh, kw = 64, 8, 16
    q = np.arange(T)
    r, c = q // grid_w, q % grid_w
    start = np.clip(c - kw // 2, 0, grid_w - kw)
    inside = (c[None, :] >= start[:, None]) & (c[None, :] < start[:, None] + kw)
    dr = r[None, :] - r[:, None] + kh - 1
    dc = np.where(inside, c[None, :] - c[:, None] + kw - 1, 0)
    return inside, dr, dc


def kernel(**inputs):
    import numpy as np
    import concourse.bacc as bacc
    from concourse.bass_utils import run_bass_kernel_spmd

    f = {k: np.asarray(v) for k, v in inputs.items()}
    one = {k: f[k][0] for k in f if k not in ("c", "c_ctx", "final_norm_g")}

    def tiles(a):
        return np.ascontiguousarray(a.reshape(-1, P, a.shape[-1]).transpose(1, 0, 2))

    def column(a):
        return a.reshape(-1, P).T

    def in_blocks(a):
        return np.ascontiguousarray(a.reshape(KD, P, -1, BLK).transpose(2, 1, 0, 3))

    c2 = np.stack([column(f["c"][0]), column(f["c_ctx"])], axis=-1).reshape(P, 2 * KD)
    conv = one["conv_w"].reshape(3, CONV_T, P).transpose(2, 1, 0).reshape(P, 3 * CONV_T)
    cols = np.concatenate([c2, column(one["ada_b"]), column(one["norm1_g"]), column(one["norm2_g"]),
                           column(one["out_norm_g"]), conv], axis=1)
    rows = np.concatenate([one["sgu_b"].reshape(-1), one["ada_b"][G2 * D:]])[None]
    constants = np.zeros((P, 4, P), np.float32)
    constants[:, 0] = np.eye(P)
    constants[:, 1] = 1.0
    constants[:, 2] = np.kron(np.eye(2), np.ones((HD, HD)))
    constants[:, 3] = np.arange(P)
    inside, dr, dc = bias_places()
    bias_mask = np.full((HEADS, T, T), NEG, np.float32)
    bias_mask[:, inside] = one["na_rpb"][:, dr[inside], dc[inside]]
    bias_mask = bias_mask.reshape(HEADS, TB, P, T).transpose(2, 0, 1, 3)
    arrays = {
        "x_t": tiles(one["x"].T),
        "ctx_t": tiles(one["ctx"].T),
        "cols": cols,
        "rows": rows,
        "sgu_gain": np.broadcast_to(one["sgu_norm_g"], (P, BLK)),
        "final_gain": np.broadcast_to(f["final_norm_g"], (P, D)),
        "constants": constants,
        "sgu_wt": one["sgu_w"].transpose(2, 0, 1),
        "bias_mask": bias_mask,
        "ada_w": in_blocks(one["ada_w"]),
        "w_in": in_blocks(one["w_in"]),
        "w_out": in_blocks(one["w_out"]),
        "w_q": in_blocks(one["peer_wq"]),
        "subkeys_t": one["peer_subkeys"].transpose(3, 0, 1, 2).reshape(P, LISTS, NK),
        "peer_u_t": one["peer_u"].reshape(NK, NK, KD, P).transpose(1, 3, 2, 0).reshape(NK, P, D),
        "peer_v": one["peer_v"],
    }
    nc = bacc.Bacc("TRN2", target_bir_lowering=False, num_devices=1)
    arrays = {f"in_{k}": np.ascontiguousarray(v) for k, v in arrays.items()}
    args = [nc.dram_tensor(k, v.shape, mybir.dt.from_np(v.dtype), kind="ExternalInput").ap()
            for k, v in arrays.items()]
    result = nc.dram_tensor("out_x", (T, D), F32, kind="ExternalOutput").ap()
    build(nc, *args, result)
    r = run_bass_kernel_spmd(nc, [arrays], core_ids=[0])
    return r.results[0]["out_x"].reshape(1, T, D)
```

```python
from contextlib import ExitStack

import concourse.bass as bass
from concourse import mybir

F32 = mybir.dt.float32
F32R = mybir.dt.float32r
U32 = mybir.dt.uint32
ALU = mybir.AluOpType
ACT = mybir.ActivationFunctionType
AX = mybir.AxisListType

P = 128
D = 1024
KD = D // P
T = 256
TB = T // P
CTX = 256
KEYS = T + CTX
HEADS, HD = 8, 64
CONV_T = 2
SGU_G = 4
EPS = 1e-6
PH = 8
NK = 128
TOPK = 16
LISTS = 2 * PH
BLK = 256
RING = 4
NEG = -1.0e30
LOWEST = -3.0e38
SLOTS = 4
CHUNKS = NK
PIECE = D // 2
PIECES = 4
GT = 4
GROUPS = T // GT

TOPK_UNTIL = 4 * TB * PH
DECODE_UNTIL = TOPK_UNTIL + 16
SOFTMAX_UNTIL = DECODE_UNTIL + 4
TURN_AT = SOFTMAX_UNTIL + 4
MERGE = 96
assert (CHUNKS - MERGE) * 2 == GROUPS

COL_C = 0
COL_ADA_B = COL_C + 2 * KD
COL_N1 = COL_ADA_B + 6 * KD
COL_N2 = COL_N1 + KD
COL_OG = COL_N2 + KD
COL_CONV = COL_OG + KD
COLS = COL_CONV + 3 * CONV_T

SH1, SC1, G1, SH2, SC2, G2 = range(6)


def schedule():
    steps = [("stat1", 0)]
    behind = []

    def ada(b):
        steps.append(("ada", b))
        behind.append(b)

    def turn():
        if behind:
            b = behind.pop(0)
            steps.append(("spread" if b // 4 == G2 else "column", b))

    for s in (SC1, SH1):
        for b in range(4):
            ada(4 * s + b)
            if len(behind) > 1:
                turn()
    turn()
    later = [4 * s + b for s in (G1, SH2, SC2) for b in range(4)]
    for n, b in enumerate((4, 3, 1, 2, 0, 5, 6, 7, 8, 9, 10)):
        steps.append(("w_in", b))
        turn()
        if b == 0:
            steps.append(("gating", 0))
        if b == 9:
            steps += [("squares", 0), ("squares", 1)]
        ada(later.pop(0))
    turn()
    ada(later.pop(0))
    steps += [("group", 0), ("group", 1)]
    units = HEADS * TB
    for u in range(units + 3):
        if u < units:
            steps.append(("scores", u))
        if u == 0:
            turn()
        if 0 <= u - 2 < units:
            steps.append(("turned", u - 2))
        if u >= 3:
            steps.append(("attend", u - 3))
        if u == 13:
            steps.append(("squares", 2))
    steps += [("squares", 3), ("group", 2), ("group", 3), ("w_out", 0), ("stat2", 0), ("x1_turned", 0)]
    for b in range(LISTS // 2):
        steps.append(("w_q", b))
        turn()
        if b >= 4:
            ada(4 * G2 + b - 4)
    turn()
    return steps + [("keys", tb * 4 + l4) for tb in range(TB) for l4 in range(LISTS // 4)]


def blocks_of(steps):
    out = []
    for kind, b in steps:
        if kind == "w_out":
            out += [("w_out", n) for n in range(4)]
        elif kind in ("ada", "w_in", "w_q"):
            out.append((kind, b))
    return out


def bank_uses(steps):
    place, used, turn = {}, [0] * 8, [0]

    def put(name, b):
        place[name] = (b, used[b])
        used[b] += 1

    def ring(name, banks=(0, 1, 2, 3)):
        put(name, banks[turn[0] % len(banks)])
        turn[0] += 1

    sections = {SC1: 4, SH1: 5, G1: 6, SH2: 7, SC2: 6}
    for kind, n in steps:
        if kind == "stat1":
            put((kind, 0), 7)
        elif kind == "w_in" and n >= 7:
            ring((kind, n, 0))
            ring((kind, n, 1))
        elif kind == "w_in":
            ring((kind, n, 0))
        elif kind == "column":
            if n % 4 == 0:
                put(("mod", n // 4), sections[n // 4])
        elif kind == "scores":
            put((kind, n), 4 + n % 2)
        elif kind == "turned":
            put((kind, n), 6 + n % 2)
        elif kind == "attend":
            if n % 4 == 0:
                put((kind, n // 4), n // 4 % 2)
        elif kind == "group":
            put((kind, n), 2 + n % 2)
        elif kind == "w_out":
            for m in range(4):
                put((kind, m), 4 + m)
        elif kind == "stat2":
            put((kind, 0), 0)
        elif kind == "x1_turned":
            for j in range(4):
                put((kind, j), (1, 2, 3, 7)[j])
        elif kind == "squares":
            pass
        elif kind == "keys":
            put((kind, n), 4 + n % 4)
        else:
            ring((kind, n))
    return place, used


def build(nc, x_t, ctx_t, cols, rows, sgu_gain, final_gain, constants, sgu_wt, bias_mask, ada_w, w_in,
          w_out, w_q, subkeys_t, peer_u_t, peer_v, out):
    steps = schedule()
    blocks = blocks_of(steps)
    place, used = bank_uses(steps)
    ring_of = {block: n for n, block in enumerate(blocks)}
    sources = {"ada": ada_w, "w_in": w_in, "w_out": w_out, "w_q": w_q}
    v_rows = peer_v.rearrange("(a b) d -> b a d", b=CHUNKS)

    def last_read(block_name):
        kind, b = block_name
        if kind == "w_in":
            return ("w_in", b, 1 if b >= 7 else 0)
        return ("w_out", 3) if kind == "w_out" else block_name

    with ExitStack() as stack:
        def sbuf(name, shape, dtype=F32):
            return stack.enter_context(nc.sbuf_tensor(name, shape, dtype))

        def sem(name):
            return stack.enter_context(nc.semaphore(name))

        bank = [stack.enter_context(nc.psum_tensor(f"bank{b}", [P, 512], F32)) for b in range(8)]

        A = sbuf("A", [P, CHUNKS * T])
        A3 = A[:, :].rearrange("p (c t) -> p c t", t=T)

        at = [0]

        def part(size, start=None):
            if start is not None:
                at[0] = start
            at[0] += size
            return A[:, at[0] - size:at[0]]

        X1 = part(KD * T).rearrange("p (k t) -> p k t", k=KD)
        H = part(KD * KEYS).rearrange("p (k t) -> p k t", k=KD)
        C0 = part(KD * CTX).rearrange("p (k t) -> p k t", k=KD)
        YR = part(KD * T).rearrange("p (k t) -> p k t", k=KD)
        YS = part(KD * T).rearrange("p (k t) -> p k t", k=KD)
        CV = part(6 * T).rearrange("p (k t) -> p k t", k=6)
        Z = part(CONV_T * (T + 2)).rearrange("p (k t) -> p k t", k=CONV_T)
        SU = part(2 * T).rearrange("p (k t) -> p k t", k=2)
        SV = part(TB * BLK).rearrange("p (b c) -> p b c", b=TB)
        Q = part(4 * T).rearrange("p (k t) -> p k t", k=4)
        K = part(4 * KEYS).rearrange("p (k t) -> p k t", k=4)
        V = part(4 * 512).rearrange("p (c n) -> p c n", c=4)
        PR = part(3 * KEYS).rearrange("p (b n) -> p b n", b=3)
        PT = part(3 * KEYS).rearrange("p (b c n) -> p b c n", b=3, c=4)
        swt = part(SGU_G * P).rearrange("p (g n) -> p g n", g=SGU_G)
        sg_gain = part(BLK)
        assert at[0] <= 24576
        SVS = PT[:, 0, :, :].rearrange("p c n -> p (c n)").rearrange("p (b c) -> p b c", b=TB)
        sgb_row = PR[0:1, 0, :]
        g2_row = A[0:1, 12288:12288 + D]
        WR = part(RING * KD * BLK, 24576).rearrange("p (s k n) -> p s k n", s=RING, k=KD)
        SQ = part(KD * KEYS, 15364).rearrange("p (k t) -> p k t", k=KD)
        YN = A[:, 2048:4096].rearrange("p (k t) -> p k t", k=KD)
        H2 = A[:, 4096:6144].rearrange("p (k t) -> p k t", k=KD)
        SK = A[:, 6144:8192].rearrange("p (l n) -> p l n", l=LISTS)
        QP = A[:, 8192:12288].rearrange("p (l t) -> p l t", l=LISTS)
        S = A[:, 28672:32768].rearrange("p (b l n) -> p b l n", b=TB, l=LISTS)
        BIG = A[:, 24576:26624]
        LST = A[:, 26624:26880].rearrange("p (l n) -> p l n", l=2)
        LS2 = A[:, 26880:27136].rearrange("p (l n) -> p l n", l=2)
        CND = A[:, 27136:27392]
        CN2 = A[:, 27392:27648]
        all_i = A[:, 27648:28160].rearrange("p (n l k) -> p n l k", l=2, k=TOPK)
        all_v = A[:, 28160:28416].rearrange("p (n k) -> p n k", k=TOPK)
        all_p = A[:, 28416:28672].bitcast(U32).rearrange("p (n k) -> p n k", k=TOPK)
        digit = A[:, 26880:27136].bitcast(U32).rearrange("p (l n) -> p l n", l=2)
        assert 24576 == MERGE * T

        bias = sbuf("stage", [P, SLOTS, D])
        stage = bias
        BM = bias[:, :, :].rearrange("p s d -> p (s d)").rearrange("p (h b n) -> p h b n", h=HEADS, b=TB)
        hi = sbuf("hi", [P, PIECES, PIECE], F32R)
        lo = sbuf("lo", [P, PIECES, PIECE], F32R)
        h2_hi = sbuf("h2_hi", [P, KD, T], F32R)
        h2_lo = sbuf("h2_lo", [P, KD, T], F32R)
        w_hi = h2_hi[:, 0:2, :]
        w_lo = h2_lo[:, 0:2, :]
        x1n = sbuf("x1n", [P, TB, D])
        g2b = sbuf("g2b", [P, D])
        gate_buf = sbuf("gate_buf", [P, 4, GT, NK])
        ONE1 = gate_buf[:, 0:2]
        ONE2 = gate_buf[:, 2:4]
        mrow = gate_buf[:, 0, :, :].rearrange("p (n a) b -> p n (a b)", n=2)
        rinv = gate_buf[:, 2, :, :].rearrange("p a b -> p (a b)")
        root = gate_buf[:, 3, :, :].rearrange("p a b -> p (a b)")
        fin = gate_buf[:, :, :, :].rearrange("p a b c -> p (a b c)")[:, 0:D]
        choice = sbuf("choice", [P, 3, TB, P])
        choice_t = sbuf("choice_t", [P, 3, T])
        gelu_buf = choice[:, 0:2, :, :].rearrange("p n b t -> p n (b t)")
        con = sbuf("con", [P, 5 * P + 2])
        ident, ones, group_ones, iota, row_ones = (con[:, n * P:(n + 1) * P] for n in range(5))
        row_pick = con[:, 5 * P:5 * P + 2]
        colv = sbuf("colv", [P, COLS])
        csil = sbuf("csil", [P, KD, 32])
        mod = sbuf("mod", [P, 5, KD, 2])
        gain1 = sbuf("gain1", [P, KD, 2])
        gain2 = sbuf("gain2", [P, KD])
        eps = sbuf("eps", [P, 1])
        gms = sbuf("gms", [P, 3, TB * SGU_G])
        nmax = sbuf("nmax", [P, HEADS * TB])
        psum_ = sbuf("psum_", [P, HEADS * TB])
        pinv = sbuf("pinv", [P, HEADS * TB])
        top_v = sbuf("top_v", [P, 2, TOPK])
        top_i = sbuf("top_i", [P, 2, TOPK], U32)
        best_v = sbuf("best_v", [P, TOPK])
        best_p = sbuf("best_p", [P, TOPK], U32)
        gsum = sbuf("gsum", [P, 2, TB * PH])
        fsum = sbuf("fsum", [P, 3, TB * 2])

        consts_in, x_in, cols_in, gating_in, bias_in, subkeys_in, g2_row_in = map(
            sem, ("consts_in", "x_in", "cols_in", "gating_in", "bias_in", "subkeys_in", "g2_row_in"))
        ring_full = [sem(f"ring_full{s}") for s in range(RING)]
        bank_full = [sem(f"bank_full{b}") for b in range(8)]
        bank_free = [sem(f"bank_free{b}") for b in range(8)]
        dve_done = sem("dve_done")
        silu_zero, silu_ready, sq_ready, root_ready, h_ready, mrow_ready = map(
            sem, ("silu_zero", "silu_ready", "sq_ready", "root_ready", "h_ready", "mrow_ready"))
        proj_ready, sv_ready, svroot_ready, svn_ready = map(
            sem, ("proj_ready", "sv_ready", "svroot_ready", "svn_ready"))
        nmax_ready, exp_ready, prob_ready, pt_ready = map(sem, ("nmax_ready", "exp_ready", "prob_ready", "pt_ready"))
        yr_ready, ys_ready, yroot_ready, yn_ready = map(sem, ("yr_ready", "ys_ready", "yroot_ready", "yn_ready"))
        h2_scaled = sem("h2_scaled")
        x1_ready, x1s_ready, h2_ready, h2_hi_ready, h2_split = map(
            sem, ("x1_ready", "x1s_ready", "h2_ready", "h2_hi_ready", "h2_split"))
        qp_ready, keys_ready = map(sem, ("qp_ready", "keys_ready"))
        eps_ready, gms_ready = sem("eps_ready"), sem("gms_ready")
        stage_full = [sem(f"stage_full{s}") for s in range(SLOTS)]
        hi_made, lo_made, piece_done, a_made = map(sem, ("hi_made", "lo_made", "piece_done", "a_made"))
        ones_made, multiplied, one1_square = map(sem, ("ones_made", "multiplied", "one1_square"))
        topk_seen = sem("topk_seen")
        topk_step, shifted, exped, choice_ready, scratch_free, turned, choice_t_ready = map(
            sem, ("topk_step", "shifted", "exped", "choice_ready", "scratch_free", "turned", "choice_t_ready"))
        one1_made, one2_made, gates_done, gated = map(sem, ("one1_made", "one2_made", "gates_done", "gated"))
        whi_made, wlo_made = map(sem, ("whi_made", "wlo_made"))
        fin_in, res_ready, fsq_ready, froot_ready, out_ready, stored = map(
            sem, ("fin_in", "res_ready", "fsq_ready", "froot_ready", "out_ready", "stored"))

        block = stack.enter_context(nc.Block())

        def opened(eng, name):
            b, use = place[name]
            if use:
                eng.wait_ge(bank_free[b], use)
            return bank[b]

        def full(eng, name):
            b, use = place[name]
            eng.wait_ge(bank_full[b], use + 1)
            return bank[b]

        def fill_sem(name):
            return bank_full[place[name][0]]

        def free_sem(name):
            return bank_free[place[name][0]]

        @block.sync
        def _(sp):
            sp.dma_start(colv[:, :], cols).then_inc(cols_in, 16)
            sp.dma_start(X1, x_t).then_inc(x_in, 16)
            sp.dma_start(C0, ctx_t).then_inc(x_in, 16)
            sp.dma_start(con[:, :], constants).then_inc(consts_in, 16)
            for n, (matrix, b) in enumerate(blocks):
                if n >= RING:
                    old = place[last_read(blocks[n - RING])]
                    sp.wait_ge(bank_full[old[0]], old[1] + 1)
                sp.dma_start(WR[:, n % RING], sources[matrix][b]).then_inc(ring_full[n % RING], 16)
                if n == RING - 1:
                    sp.dma_start(sgb_row, rows[:, 0:SGU_G * P]).then_inc(gating_in, 16)
                    sp.dma_start(sg_gain, sgu_gain).then_inc(gating_in, 16)
                    sp.dma_start(swt, sgu_wt).then_inc(gating_in, 16)
                if n == 16:
                    sp.dma_start(BM, bias_mask).then_inc(bias_in, 16)
                    sp.wait_ge(h_ready, KD)
                    sp.dma_start(SK, subkeys_t).then_inc(subkeys_in, 16)
                if (matrix, b) == ("w_q", 0):
                    sp.wait_ge(yr_ready, 1)
                    sp.dma_start(g2_row, rows[:, SGU_G * P:]).then_inc(g2_row_in, 16)
            for u in (HEADS * TB - 2, HEADS * TB - 1):
                b, use = place[("scores", u)]
                sp.wait_ge(bank_full[b], use + 1)
            for j in range(SLOTS):
                sp.dma_start(stage[:, j, :], peer_u_t[j]).then_inc(stage_full[j], 16)
            with sp.Fori(1, CHUNKS // SLOTS) as i:
                for j in range(SLOTS):
                    sp.wait_ge(lo_made, i * (2 * SLOTS) + (2 * (j + 1 - SLOTS)))
                    sp.dma_start(stage[:, j, :], peer_u_t[i * SLOTS + j]).then_inc(stage_full[j], 16)
            with sp.Fori(0, CHUNKS // SLOTS) as i:
                for j in range(SLOTS):
                    sp.wait_ge(lo_made, i * (2 * SLOTS) + (2 * (CHUNKS + j + 1 - SLOTS)))
                    sp.dma_start(stage[:, j, :], v_rows[i * SLOTS + j]).then_inc(stage_full[j], 16)
            sp.wait_ge(gates_done, GROUPS)
            sp.dma_start(fin, final_gain).then_inc(fin_in, 16)
            for tb in range(TB):
                sp.wait_ge(out_ready, tb + 1)
                sp.dma_start(out[tb * P:(tb + 1) * P, :], x1n[:, tb, :]).then_inc(stored, 16)
            sp.wait_ge(stored, 16 * TB)

        @block.tensor
        def _(pe):
            def weights(block_name):
                n = ring_of[block_name]
                pe.wait_ge(ring_full[n % RING], 16 * (n // RING + 1))
                return WR[:, n % RING]

            def contract(o, lhs, rhs, ready=None):
                for k in range(KD):
                    if ready is not None:
                        pe.wait_ge(ready, k + 1)
                    mm = pe.matmul(o, lhs(k), rhs(k), start=(k == 0), stop=(k == KD - 1))
                return mm

            def ada(b):
                o = opened(pe, ("ada", b))
                w = weights(("ada", b))
                for k in range(KD):
                    q = slice(32 * (k % 4), 32 * (k % 4) + 32)
                    mm = pe.matmul(o[q, 0:BLK], csil[:, k, :], w[:, k, :], start=(k < 4), stop=(k >= 4),
                                   tile_position=(0, 32 * (k % 4)))
                mm.then_inc(fill_sem(("ada", b)), 1)

            ada_blocks = [b for kind, b in steps if kind == "ada"]

            def column(b):
                s, n = b // 4, ada_blocks.index(b)
                o = opened(pe, ("mod", s)) if b % 4 == 0 else bank[place[("mod", s)][0]]
                pe.wait_ge(mrow_ready, n + 1)
                for m in range(2):
                    c = 2 * (2 * (b % 4) + m)
                    mm = pe.matmul(o[:, c:c + 2], mrow[:, n % 2, m * P:(m + 1) * P], row_pick, start=True, stop=True)
                if b % 4 == 3:
                    mm.then_inc(fill_sem(("mod", s)), 1)

            def spread(b):
                n, c = ada_blocks.index(b), b % 4 * BLK
                o = opened(pe, ("spread", b))
                pe.wait_ge(mrow_ready, n + 1)
                pe.wait_ge(g2_row_in, 16)
                pe.matmul(o[:, 0:BLK], row_ones, mrow[:, n % 2, :], start=True, stop=False)
                pe.matmul(o[:, 0:BLK], ones[0:1, :], g2_row[:, c:c + BLK], start=False, stop=True)\
                  .then_inc(fill_sem(("spread", b)), 1)

            def in_projection(b):
                w = weights(("w_in", b))
                if b in (0, 1, 2, 3, 5, 6):
                    o = opened(pe, ("w_in", b, 0))
                    for m in range(2):
                        mm = contract(o[:, m * T:(m + 1) * T], lambda k: w[:, k, m * P:(m + 1) * P],
                                      lambda k: H[:, k, 0:T])
                    mm.then_inc(fill_sem(("w_in", b, 0)), 1)
                elif b == 4:
                    o = opened(pe, ("w_in", b, 0))
                    for t in range(TB):
                        mm = contract(o[:, t * BLK:(t + 1) * BLK], lambda k: H[:, k, t * P:(t + 1) * P],
                                      lambda k: w[:, k, :], h_ready if t == 0 else None)
                    mm.then_inc(fill_sem(("w_in", b, 0)), 1)
                elif b in (7, 8):
                    for m in range(2):
                        o = opened(pe, ("w_in", b, m))
                        contract(o[:, :], lambda k: w[:, k, m * P:(m + 1) * P], lambda k: H[:, k, :])\
                            .then_inc(fill_sem(("w_in", b, m)), 1)
                else:
                    for m in range(2):
                        o = opened(pe, ("w_in", b, m))
                        for c in range(2):
                            t = 2 * m + c
                            mm = contract(o[:, c * BLK:(c + 1) * BLK], lambda k: H[:, k, t * P:(t + 1) * P],
                                          lambda k: w[:, k, :])
                        mm.then_inc(fill_sem(("w_in", b, m)), 1)

            def gating():
                o = opened(pe, ("gating", 0))
                pe.wait_ge(svn_ready, 1)
                pe.wait_ge(gating_in, 48)
                for g in range(SGU_G):
                    for tb in range(TB):
                        half = slice(HD * (g % 2), HD * (g % 2) + HD)
                        oo = o[half, (g // 2) * T + tb * P:(g // 2) * T + (tb + 1) * P]
                        pe.matmul(oo, SV[:, tb, g * HD:(g + 1) * HD], swt[:, g, :], start=True, stop=False)
                        mm = pe.matmul(oo, ones[0:1, 0:HD], sgb_row[:, g * P:(g + 1) * P], start=False, stop=True)
                mm.then_inc(fill_sem(("gating", 0)), 1)

            def scores(u):
                h, tb = u // 2, u % 2
                if u == 0:
                    pe.wait_ge(bias_in, 16)
                    pe.wait_ge(proj_ready, 11)
                o = opened(pe, ("scores", u))
                pp = slice(HD * (h % 2), HD * (h % 2) + HD)
                qq = Q[pp, h // 2, tb * P:(tb + 1) * P]
                pe.matmul(o[:, 0:T], ident, BM[:, h, tb, :], start=True, stop=False)
                pe.matmul(o[:, 0:T], qq, K[pp, h // 2, 0:T], start=False, stop=True)
                pe.matmul(o[:, T:KEYS], qq, K[pp, h // 2, T:KEYS], start=True, stop=True)\
                  .then_inc(fill_sem(("scores", u)), 1)

            def turned_probs(v):
                o = opened(pe, ("turned", v))
                pe.wait_ge(prob_ready, v + 1)
                for c in range(4):
                    mm = pe.transpose(o[:, c * P:(c + 1) * P], PR[:, v % 3, c * P:(c + 1) * P], ident)
                mm.then_inc(fill_sem(("turned", v)), 1)

            def attend(v):
                h, tb = v // 2, v % 2
                name = ("attend", v // 4)
                o = opened(pe, name) if v % 4 == 0 else bank[place[name][0]]
                pe.wait_ge(pt_ready, v + 1)
                for c in range(4):
                    mm = pe.matmul(o[HD * (h % 2):HD * (h % 2) + HD, tb * P:(tb + 1) * P],
                                   V[:, c, h * HD:(h + 1) * HD], PT[:, v % 3, c, :],
                                   start=(c == 0), stop=(c == 3))
                if v % 4 == 3:
                    mm.then_inc(fill_sem(name), 1)

            def group_sums(j):
                o = opened(pe, ("group", j))
                pe.wait_ge(ys_ready, j + 1)
                pe.matmul(o[:, :], group_ones, YS[:, 2 * j:2 * j + 2, :], start=True, stop=True)\
                  .then_inc(fill_sem(("group", j)), 1)

            def out_projection():
                w = [weights(("w_out", b)) for b in range(4)]
                for k in range(KD):
                    pe.wait_ge(yn_ready, k + 1)
                    for m in range(KD):
                        o = opened(pe, ("w_out", m // 2)) if k == 0 and m % 2 == 0 else bank[place[("w_out", m // 2)][0]]
                        mm = pe.matmul(o[:, m % 2 * T:m % 2 * T + T], w[m // 2][:, k, m % 2 * P:m % 2 * P + P],
                                       YN[:, k, :], start=(k == 0 and m % 2 == 0), stop=(k == KD - 1),
                                       skip_group_check=True)
                        if k == KD - 1 and m % 2 == 1:
                            mm.then_inc(fill_sem(("w_out", m // 2)), 1)

            def second_stat():
                o = opened(pe, ("stat2", 0))
                for m in range(KD):
                    if m % 2 == 0:
                        pe.wait_ge(x1s_ready, m // 2 + 1)
                    mm = pe.matmul(o[:, 0:T], ones, YS[:, m, :], start=(m == 0), stop=(m == KD - 1))
                mm.then_inc(fill_sem(("stat2", 0)), 1)

            def turned_x1():
                for j in range(4):
                    o = opened(pe, ("x1_turned", j))
                    for m in range(4):
                        mm = pe.transpose(o[:, m * P:(m + 1) * P],
                                          X1[:, 4 * (j % 2) + m, (j // 2) * P:(j // 2 + 1) * P], ident)
                    mm.then_inc(fill_sem(("x1_turned", j)), 1)

            def queries(b):
                w = weights(("w_q", b))
                o = opened(pe, ("w_q", b))
                for m in range(2):
                    mm = contract(o[:, m * T:(m + 1) * T], lambda k: w[:, k, m * P:(m + 1) * P],
                                  lambda k: H2[:, k, :], h2_ready if b == 0 and m == 0 else None)
                mm.then_inc(fill_sem(("w_q", b)), 1)

            def keys(n):
                tb, l4 = n // 4, n % 4
                if n == 0:
                    pe.wait_ge(subkeys_in, 16)
                o = opened(pe, ("keys", n))
                pe.wait_ge(qp_ready, 2 * l4 + 2)
                for m in range(4):
                    lst = 4 * l4 + m
                    mm = pe.matmul(o[:, m * P:(m + 1) * P], QP[:, lst, tb * P:(tb + 1) * P], SK[:, lst, :],
                                   start=True, stop=True)
                mm.then_inc(fill_sem(("keys", n)), 1)

            for kind, n in steps:
                if kind == "stat1":
                    pe.wait_ge(consts_in, 16)
                    pe.wait_ge(sq_ready, 2)
                    o = opened(pe, ("stat1", 0))
                    contract(o[:, :], lambda k: ones, lambda k: SQ[:, k, :]).then_inc(fill_sem(("stat1", 0)), 1)
                    pe.wait_ge(silu_ready, 1)
                elif kind == "ada":
                    ada(n)
                elif kind == "column":
                    column(n)
                elif kind == "spread":
                    spread(n)
                elif kind == "w_in":
                    in_projection(n)
                elif kind == "gating":
                    gating()
                elif kind == "scores":
                    scores(n)
                elif kind == "turned":
                    turned_probs(n)
                elif kind == "attend":
                    attend(n)
                elif kind == "squares":
                    pass
                elif kind == "group":
                    group_sums(n)
                elif kind == "w_out":
                    out_projection()
                elif kind == "stat2":
                    second_stat()
                elif kind == "x1_turned":
                    turned_x1()
                elif kind == "w_q":
                    queries(n)
                else:
                    keys(n)

            def u_chunk(j, c):
                o = bank[j % SLOTS][:, 0:T]
                for h in range(2):
                    pe.wait_ge(lo_made, c * 2 + (h + 1))
                    for n in range(KD // 2):
                        k, p, kk = KD // 2 * h + n, (2 * j + h) % PIECES, slice(n * P, (n + 1) * P)
                        pe.matmul(o, hi[:, p, kk], h2_hi[:, k, :], start=(k == 0), stop=False)
                        pe.matmul(o, hi[:, p, kk], h2_lo[:, k, :], start=False, stop=False)
                        mm = pe.matmul(o, lo[:, p, kk], h2_hi[:, k, :], start=False, stop=(k == KD - 1))
                    mm.then_inc(piece_done, 1)

            def gates(j, g):
                pe.wait_ge(one1_made, g + 1)
                pe.wait_ge(one2_made, g + 1)
                for t in range(GT):
                    mm = pe.matmul(bank[4 + j][:, t * NK:(t + 1) * NK], ONE1[:, j, t, :], ONE2[:, j, t, :],
                                   start=True, stop=True)
                mm.then_inc(gates_done, 1)

            pe.wait_ge(h2_split, KD)
            for b in range(SLOTS):
                pe.wait_ge(bank_free[b], used[b])
            for j in range(2 * SLOTS):
                if j >= SLOTS:
                    pe.wait_ge(a_made, j + 1 - SLOTS)
                u_chunk(j, j)
            with pe.Fori(1, TURN_AT // (2 * SLOTS)) as i:
                for j in range(2 * SLOTS):
                    pe.wait_ge(a_made, i * (2 * SLOTS) + (j + 1 - SLOTS))
                    u_chunk(j, i * (2 * SLOTS) + j)
            pe.wait_ge(choice_ready, TB)
            for tb in range(TB):
                pe.wait_ge(bank_free[6 + tb], used[6 + tb])
                for n in range(3):
                    mm = pe.transpose(bank[6 + tb][:, n * P:(n + 1) * P], choice[:, n, tb, :], ident)
                mm.then_inc(turned, 1)
            for c in range(TURN_AT, MERGE):
                pe.wait_ge(a_made, c + 1 - SLOTS)
                u_chunk(c % SLOTS, c)
            for b in (4, 5):
                pe.wait_ge(bank_free[b], used[b])
            for j in range(SLOTS):
                pe.wait_ge(a_made, MERGE + j + 1 - SLOTS)
                u_chunk(j, MERGE + j)
                for q in range(2):
                    if j:
                        pe.wait_ge(gated, 2 * j + q - 1)
                    gates(q, 2 * j + q)
            with pe.Fori(1, (CHUNKS - MERGE) // SLOTS) as i:
                for j in range(SLOTS):
                    pe.wait_ge(a_made, i * SLOTS + (MERGE + j + 1 - SLOTS))
                    u_chunk(j, i * SLOTS + (MERGE + j))
                    for q in range(2):
                        pe.wait_ge(gated, i * (2 * SLOTS) + (2 * j + q - 1))
                        gates(q, i * (2 * SLOTS) + (2 * j + q))

            def v_chunk(j, v, first=False, last=False):
                pe.wait_ge(wlo_made, v + 1)
                for half in range(2):
                    pe.wait_ge(lo_made, v * 2 + (2 * CHUNKS + half + 1))
                    p = (2 * j + half) % PIECES
                    for tb in range(TB):
                        o = bank[4 + 2 * tb + half][:, :]
                        tt = slice(tb * P, (tb + 1) * P)
                        pe.matmul(o, w_hi[:, j % 2, tt], hi[:, p, :], start=first, stop=False)
                        pe.matmul(o, w_hi[:, j % 2, tt], lo[:, p, :], start=False, stop=False)
                        mm = pe.matmul(o, w_lo[:, j % 2, tt], hi[:, p, :], start=False, stop=last)
                    mm.then_inc(piece_done, 1)

            pe.wait_ge(gated, GROUPS)
            pe.wait_ge(choice_t_ready, 2 * TB)
            for j in range(4):
                v_chunk(j, j, first=(j == 0))
            with pe.Fori(1, CHUNKS // 4 - 1) as i:
                for j in range(4):
                    v_chunk(j, i * 4 + j)
            for j in range(4):
                v_chunk(j, CHUNKS - 4 + j, last=(j == 3))

        def probs_out(act, v):
            name = ("turned", v)
            o = full(act, name)
            act.activation(PT[:, v % 3, :, :].rearrange("p c n -> p (c n)"), o[:, :], ACT.Copy)\
               .then_inc(pt_ready, 1)
            act.wait_ge(pt_ready, v + 1)
            act.sem_inc(free_sem(name), 1)

        def group_root(act, m):
            name = ("group", m)
            o = full(act, name)
            if m:
                act.wait_ge(yn_ready, 2 * m)
            act.activation(root, o[:, :], ACT.Sqrt, bias=eps[:, :], scale=1.0 / HD).then_inc(yroot_ready, 1)

        @block.scalar
        def _(act):
            act.wait_ge(cols_in, 16)
            act.wait_ge(silu_zero, 1)
            act.activation(csil[:, :, 0:2], colv[:, COL_C:COL_C + 2 * KD].rearrange("p (k v) -> p k v", v=2),
                           ACT.Silu).then_inc(silu_ready, 1)
            act.wait_ge(x_in, 32)
            act.activation(SQ[:, :, 0:T], X1, ACT.Square).then_inc(sq_ready, 1)
            act.activation(SQ[:, :, T:KEYS], C0, ACT.Square).then_inc(sq_ready, 1)
            act.wait_ge(eps_ready, 1)

            def projection(b):
                for half in range(2 if b >= 7 else 1):
                    name = ("w_in", b, half)
                    o = full(act, name)
                    two = o[:, :].rearrange("p (m t) -> p m t", m=2)
                    if b == 3:
                        ins = act.activation(SU, two, ACT.Gelu_apprx_tanh)
                    elif b == 4:
                        ins = act.activation(SV, two, ACT.Gelu_apprx_tanh)
                    elif b in (5, 6):
                        ins = act.activation(Q[:, 2 * (b - 5):2 * (b - 5) + 2, :], two, ACT.Copy, scale=HD ** -0.5)
                    elif b in (7, 8):
                        ins = act.activation(K[:, 2 * (b - 7) + half, :], o[:, :], ACT.Copy)
                    elif b in (9, 10):
                        ins = act.activation(V[:, 2 * half:2 * half + 2, (b - 9) * BLK:(b - 8) * BLK], two, ACT.Copy)
                    else:
                        ins = act.activation(CV[:, 2 * b:2 * b + 2, :], two, ACT.Copy)
                    ins.then_inc(free_sem(name), 1)
                act.wait_ge(free_sem(name), place[name][1] + 1)
                act.sem_inc(proj_ready, 1)
                if b == 4:
                    act.activation(SVS, SV, ACT.Square).then_inc(sv_ready, 1)
                if b == 3:
                    act.wait_ge(gms_ready, 1)
                    act.activation(gms[:, 1, :], gms[:, 0, :], ACT.Sqrt, bias=eps[:, :], scale=1.0 / HD)\
                       .then_inc(svroot_ready, 1)

            ada_seen = 0
            for kind, n in steps:
                if kind == "stat1":
                    o = full(act, (kind, n))
                    act.activation(root, o[:, :], ACT.Sqrt, bias=eps[:, :], scale=1.0 / D).then_inc(root_ready, 1)
                elif kind == "ada":
                    o = full(act, (kind, n))
                    act.activation(mrow[:, ada_seen % 2, :], o[:, 0:BLK], ACT.Copy).then_inc(mrow_ready, 1)
                    ada_seen += 1
                    act.wait_ge(mrow_ready, ada_seen)
                    act.sem_inc(free_sem((kind, n)), 1)
                elif kind == "spread":
                    o = full(act, (kind, n))
                    act.activation(g2b[:, n % 4 * BLK:(n % 4 + 1) * BLK], o[:, 0:BLK], ACT.Copy)\
                       .then_inc(free_sem((kind, n)), 1)
                elif kind == "w_in":
                    projection(n)
                elif kind == "scores":
                    if n >= 2:
                        probs_out(act, n - 2)
                    o = full(act, (kind, n))
                    act.wait_ge(nmax_ready, n + 1)
                    if n >= 3:
                        act.wait_ge(pt_ready, n - 2)
                    act.activation(PR[:, n % 3, :], o[:, :], ACT.Exp, bias=nmax[:, n:n + 1],
                                   accum_out=psum_[:, n:n + 1]).then_inc(exp_ready, 1)
                    if n == HEADS * TB - 1:
                        probs_out(act, n - 1)
                        probs_out(act, n)
                elif kind == "squares":
                    act.wait_ge(yr_ready, n + 1)
                    act.activation(YS[:, 2 * n:2 * n + 2, :], YR[:, 2 * n:2 * n + 2, :], ACT.Square)\
                       .then_inc(ys_ready, 1)
                elif kind == "group":
                    group_root(act, n)
                elif kind == "w_out":
                    for b in range(4):
                        act.wait_ge(x1_ready, b + 1)
                        act.activation(YS[:, 2 * b:2 * b + 2, :], X1[:, 2 * b:2 * b + 2, :], ACT.Square)\
                           .then_inc(x1s_ready, 1)
                elif kind == "stat2":
                    o = full(act, (kind, n))
                    act.activation(root[:, 0:T], o[:, 0:T], ACT.Sqrt, bias=eps[:, :], scale=1.0 / D)\
                       .then_inc(root_ready, 1)
                elif kind == "x1_turned":
                    for k in range(KD):
                        act.wait_ge(h2_scaled, k + 1)
                        act.activation(H2[:, k, :], H2[:, k, :], ACT.Identity, bias=mod[:, SH2, k, 0:1])\
                           .then_inc(h2_ready, 1)
                    for j in range(4):
                        name = (kind, j)
                        o = full(act, name)
                        act.activation(x1n[:, j // 2, (j % 2) * 512:(j % 2) * 512 + 512], o[:, :], ACT.Copy)\
                           .then_inc(free_sem(name), 1)
                    for k in range(KD):
                        act.wait_ge(h2_ready, k + 1)
                        act.activation(h2_hi[:, k, :], H2[:, k, :], ACT.Copy).then_inc(h2_hi_ready, 1)
                elif kind == "w_q":
                    o = full(act, (kind, n))
                    act.activation(QP[:, 2 * n:2 * n + 2, :].rearrange("p l t -> p (l t)"), o[:, :], ACT.Copy)\
                       .then_inc(qp_ready, 1)
                    act.wait_ge(qp_ready, n + 1)
                    act.sem_inc(free_sem((kind, n)), 1)
                elif kind == "keys":
                    o = full(act, (kind, n))
                    act.activation(S[:, n // 4, 4 * (n % 4):4 * (n % 4) + 4, :].rearrange("p l n -> p (l n)"), o[:, :],
                                   ACT.Copy).then_inc(keys_ready, 1)
                    act.wait_ge(keys_ready, n + 1)
                    act.sem_inc(free_sem((kind, n)), 1)

            def round_chunk(j, use, done=None):
                for h in range(2):
                    if done is not None:
                        act.wait_ge(piece_done, done + h)
                    if h == 0:
                        act.wait_ge(stage_full[j], use)
                    act.activation(hi[:, (2 * j + h) % PIECES, :], stage[:, j, h * PIECE:(h + 1) * PIECE], ACT.Copy)\
                       .then_inc(hi_made, 1)

            def gelu_chunk(j, c):
                act.activation(A3[:, c, :], bank[j % SLOTS][:, 0:T], ACT.Gelu_apprx_tanh).then_inc(a_made, 1)

            def gelu_beside(j, n, reused=True):
                if reused:
                    act.wait_ge(multiplied, n - 1)
                act.activation(gelu_buf[:, j % 2, :], bank[j % SLOTS][:, 0:T], ACT.Gelu_apprx_tanh)\
                   .then_inc(a_made, 1)

            def u_steps(i, j):
                round_chunk(j, i * 16 + 16, i * (2 * SLOTS) + (2 * j - 3))
                gelu_chunk(j - 2, i * SLOTS + (j - 2))

            def one1(i, j, reused=True):
                for q in range(2):
                    if reused:
                        act.wait_ge(gates_done, i * (2 * SLOTS) + (2 * j + q - 1))
                    for t in range(GT):
                        tt = i * (2 * SLOTS * GT) + ((2 * j + q) * GT + t)
                        last = act.activation(ONE1[:, q, t, :], iota, ACT.Square, bias=choice_t[:, 0, bass.ds(tt, 1)])
                    last.then_inc(one1_square, 1)
                for q in range(2):
                    act.wait_ge(one1_square, i * (2 * SLOTS) + (2 * j + q + 1))
                    act.activation(ONE1[:, q], ONE1[:, q], ACT.Relu, bias=1.0, scale=-1.0).then_inc(one1_made, 1)

            for c in range(SLOTS):
                round_chunk(c, 16, 2 * c - 3 if c >= 2 else None)
                if c >= 2:
                    gelu_chunk(c - 2, c - 2)
            with act.Fori(1, DECODE_UNTIL // SLOTS) as i:
                for j in range(SLOTS):
                    u_steps(i, j)
            act.wait_ge(shifted, TB)
            act.activation(choice[:, 2, :, :], choice[:, 2, :, :], ACT.Exp).then_inc(exped, 1)
            with act.Fori(DECODE_UNTIL // SLOTS, MERGE // SLOTS) as i:
                for j in range(SLOTS):
                    u_steps(i, j)
            act.wait_ge(choice_t_ready, 2 * TB)
            for j in range(SLOTS):
                c = MERGE + j
                round_chunk(j, 16 * (c // SLOTS) + 16, 2 * c - 3)
                if j < 2:
                    gelu_chunk(j + 2, c - 2)
                else:
                    gelu_beside(j + 2, j - 2, reused=False)
                one1(0, j, reused=j > 0)
            with act.Fori(1, (CHUNKS - MERGE) // SLOTS) as i:
                for j in range(SLOTS):
                    round_chunk(j, i * 16 + (16 * (MERGE // SLOTS) + 16), i * (2 * SLOTS) + (2 * (MERGE + j) - 3))
                    gelu_beside(j + 2, i * SLOTS + (j - 2))
                    one1(i, j)
            for j in range(2):
                n = CHUNKS + j
                round_chunk(j, 16 * (n // SLOTS) + 16, 2 * n - 3)
                gelu_beside(j + 2, n - 2 - MERGE)

            def w_round(j, v):
                act.activation(w_hi[:, j % 2, :], A3[:, v, :], ACT.Copy).then_inc(whi_made, 1)

            act.wait_ge(gated, GROUPS)
            act.wait_ge(multiplied, CHUNKS - MERGE)
            act.wait_ge(piece_done, 2 * CHUNKS)
            for v in range(2):
                w_round(v, v)
            for v in (2, 3):
                act.wait_ge(piece_done, 2 * (CHUNKS + v - 1))
                w_round(v, v)
                round_chunk(v, 16 * (CHUNKS // SLOTS) + 16, 2 * (CHUNKS + v) - 3)
            with act.Fori(1, CHUNKS // SLOTS) as i:
                for j in range(SLOTS):
                    act.wait_ge(piece_done, i * (2 * SLOTS) + 2 * (CHUNKS + j - 1))
                    w_round(j, i * SLOTS + j)
                    round_chunk(j, i * 16 + (16 * (CHUNKS // SLOTS) + 16), i * (2 * SLOTS) + (2 * (CHUNKS + j) - 3))

            for n in range(2 * TB):
                tb, half = n // 2, n % 2
                act.wait_ge(res_ready, n + 1)
                act.activation(A[:, n * 512:n * 512 + 512], x1n[:, tb, half * 512:half * 512 + 512], ACT.Square,
                               accum_out=fsum[:, 0, n:n + 1]).then_inc(fsq_ready, 1)
            act.wait_ge(fsq_ready, 2 * TB + 1)
            act.activation(fsum[:, 2, 0:TB], fsum[:, 1, 0:TB], ACT.Sqrt, bias=eps[:, :], scale=1.0 / D)\
               .then_inc(froot_ready, 1)

        @block.vector
        def _(dve):
            chain = [0]

            def link(ins):
                chain[0] += 1
                ins.then_inc(dve_done, 1)
                dve.wait_ge(dve_done, chain[0])

            dve.memset(csil[:, :, :], 0.0).then_inc(silu_zero, 1)
            dve.memset(eps[:, :], EPS).then_inc(eps_ready, 1)
            dve.memset(Z[:, :, 0:1], 0.0)
            link(dve.memset(Z[:, :, T + 1:T + 2], 0.0))
            dve.wait_ge(root_ready, 1)
            link(dve.reciprocal(rinv, root))
            dve.sem_inc(free_sem(("stat1", 0)), 1)
            rb = lambda a, b: rinv[:, a:b].unsqueeze(1).broadcast_to([P, KD, b - a])
            dve.tensor_tensor(H[:, :, 0:T], X1, rb(0, T), ALU.mult)
            link(dve.tensor_tensor(H[:, :, T:KEYS], C0, rb(T, KEYS), ALU.mult))

            def modulation(s):
                o = full(dve, ("mod", s))
                b = colv[:, COL_ADA_B + s * KD:COL_ADA_B + (s + 1) * KD].unsqueeze(2).broadcast_to([P, KD, 2])
                link(dve.tensor_tensor(mod[:, s, :, :], o[:, 0:2 * KD].rearrange("p (k v) -> p k v", v=2), b, ALU.add))
                dve.sem_inc(free_sem(("mod", s)), 1)

            modulation(SC1)
            link(dve.scalar_tensor_tensor(gain1[:, :, :], mod[:, SC1, :, :], 1.0,
                                          colv[:, COL_N1:COL_N1 + KD].unsqueeze(2).broadcast_to([P, KD, 2]),
                                          ALU.add, ALU.mult))
            modulation(SH1)
            for k in range(KD):
                for v in range(2):
                    h = H[:, k, v * T:(v + 1) * T]
                    ins = dve.tensor_scalar(h, h, gain1[:, k, v:v + 1], mod[:, SH1, k, v:v + 1], ALU.mult, ALU.add)
                ins.then_inc(h_ready, 1)

            dve.wait_ge(sv_ready, 1)
            dve.wait_ge(gating_in, 48)
            groups = "p b (g c) -> p (b g) c"
            dve.tensor_reduce(gms[:, 0, :], SVS.rearrange(groups, c=HD), AX.X, ALU.add).then_inc(gms_ready, 1)
            dve.wait_ge(svroot_ready, 1)
            link(dve.reciprocal(gms[:, 2, :], gms[:, 1, :]))
            link(dve.tensor_tensor(SV.rearrange(groups, c=HD), SV.rearrange(groups, c=HD),
                                   gms[:, 2, :].unsqueeze(2).broadcast_to([P, TB * SGU_G, HD]), ALU.mult))
            dve.tensor_tensor(SV, SV, sg_gain.unsqueeze(1).broadcast_to([P, TB, BLK]), ALU.mult)\
               .then_inc(svn_ready, 1)

            dve.wait_ge(proj_ready, 5)
            link(dve.tensor_tensor(Z[:, :, 1:T + 1], CV[:, 2:4, :], CV[:, 4:6, :], ALU.mult))
            for tap in range(3):
                for m in range(CONV_T):
                    w = colv[:, COL_CONV + 3 * m + tap:COL_CONV + 3 * m + tap + 1]
                    z = Z[:, m, tap:tap + T]
                    if tap == 0:
                        ins = dve.tensor_scalar(YR[:, m, :], z, w, None, ALU.mult)
                    else:
                        ins = dve.scalar_tensor_tensor(YR[:, m, :], z, w, YR[:, m, :], ALU.mult, ALU.add)
                link(ins)
            dve.tensor_tensor(YR[:, 0:2, :], YR[:, 0:2, :], CV[:, 0:2, :], ALU.mult).then_inc(yr_ready, 1)
            o = full(dve, ("gating", 0))
            link(dve.tensor_tensor(YR[:, 2:4, :], SU, o[:, :].rearrange("p (m t) -> p m t", m=2), ALU.mult))
            dve.sem_inc(yr_ready, 1)
            dve.sem_inc(free_sem(("gating", 0)), 1)

            def group_norm(j):
                dve.wait_ge(yroot_ready, j + 1)
                dve.sem_inc(free_sem(("group", j)), 1)
                link(dve.reciprocal(rinv, root))
                for m in range(2):
                    k = 2 * j + m
                    dve.scalar_tensor_tensor(YN[:, k, :], YR[:, k, :], colv[:, COL_OG + k:COL_OG + k + 1],
                                             rinv[:, m * T:(m + 1) * T], ALU.mult, ALU.mult).then_inc(yn_ready, 1)
                dve.wait_ge(yn_ready, 2 * j + 2)

            modulation(G1)
            dve.wait_ge(proj_ready, 11)
            group_norm(0)
            group_norm(1)
            modulation(SH2)

            for u in range(HEADS * TB + 1):
                if u < HEADS * TB:
                    o = full(dve, ("scores", u))
                    dve.tensor_reduce(nmax[:, u:u + 1], o[:, :], AX.X, ALU.max, negate=True).then_inc(nmax_ready, 1)
                if u >= 1:
                    v = u - 1
                    dve.wait_ge(exp_ready, v + 1)
                    dve.sem_inc(free_sem(("scores", v)), 1)
                    link(dve.reciprocal(pinv[:, v:v + 1], psum_[:, v:v + 1]))
                    dve.tensor_scalar(PR[:, v % 3, :], PR[:, v % 3, :], pinv[:, v:v + 1], None, ALU.mult)\
                       .then_inc(prob_ready, 1)
                if u == 1:
                    modulation(SC2)
                    link(dve.scalar_tensor_tensor(gain2[:, :], mod[:, SC2, :, 0], 1.0, colv[:, COL_N2:COL_N2 + KD],
                                                  ALU.add, ALU.mult))
                for j in ([(u - 7) // 4] if u >= 7 and u % 4 == 3 else [3] if u == HEADS * TB else []):
                    o = full(dve, ("attend", j))
                    link(dve.tensor_copy(YR[:, 4 + j, :], o[:, 0:T]))
                    dve.sem_inc(free_sem(("attend", j)), 1)
                    if j % 2:
                        dve.sem_inc(yr_ready, 1)
            group_norm(2)
            group_norm(3)
            for b in range(4):
                name = ("w_out", b)
                o = full(dve, name)
                for m in range(2):
                    k = 2 * b + m
                    ins = dve.scalar_tensor_tensor(X1[:, k, :], o[:, m * T:(m + 1) * T], mod[:, G1, k, 0:1],
                                                   X1[:, k, :], ALU.mult, ALU.add)
                ins.then_inc(x1_ready, 1)
                dve.wait_ge(x1_ready, b + 1)
                dve.sem_inc(free_sem(name), 1)
            dve.wait_ge(root_ready, 2)
            dve.sem_inc(free_sem(("stat2", 0)), 1)
            link(dve.reciprocal(rinv[:, 0:T], root[:, 0:T]))
            for k in range(KD):
                dve.scalar_tensor_tensor(H2[:, k, :], X1[:, k, :], gain2[:, k:k + 1], rinv[:, 0:T], ALU.mult,
                                         ALU.mult).then_inc(h2_scaled, 1)
            for k in range(KD):
                dve.wait_ge(h2_hi_ready, k + 1)
                dve.tensor_tensor(h2_lo[:, k, :], H2[:, k, :], h2_hi[:, k, :].bitcast(F32), ALU.subtract)\
                   .then_inc(h2_split, 1)

            def rest(j, c):
                for h in range(2):
                    p = (2 * j + h) % PIECES
                    dve.wait_ge(hi_made, c * 2 + (h + 1))
                    dve.tensor_tensor(lo[:, p, :], stage[:, j, h * PIECE:(h + 1) * PIECE], hi[:, p, :].bitcast(F32),
                                      ALU.subtract).then_inc(lo_made, 1)

            dve.wait_ge(keys_ready, TB * LISTS // 4)
            SN = A[:, 28672:32768].rearrange("p (n l k) -> p n l k", l=2, k=NK)
            STEPS = 11
            with dve.Fori(0, TB * PH) as n:
                def step(k):
                    dve.wait_ge(topk_step, n * STEPS + k)
                    dve.sem_inc(topk_seen, 1)

                dve.tensor_copy(LST, SN[:, n, :, :]).then_inc(topk_step, 1)
                rest(0, n * 4)
                step(1)
                for p in range(2):
                    last = dve.max(top_v[:, p, 0:8], LST[:, p, :])
                last.then_inc(topk_step, 1)
                step(2)
                for p in range(2):
                    dve.max_index(top_i[:, p, 0:8], top_v[:, p, 0:8], LST[:, p, :])
                    last = dve.match_replace(LS2[:, p, :], top_v[:, p, 0:8], LST[:, p, :], LOWEST)
                last.then_inc(topk_step, 1)
                rest(1, n * 4 + 1)
                step(3)
                for p in range(2):
                    last = dve.max(top_v[:, p, 8:16], LS2[:, p, :])
                last.then_inc(topk_step, 1)
                step(4)
                for p in range(2):
                    last = dve.max_index(top_i[:, p, 8:16], top_v[:, p, 8:16], LS2[:, p, :])
                last.then_inc(topk_step, 1)
                dve.tensor_tensor(CND.rearrange("p (a b) -> p a b", b=TOPK),
                                  top_v[:, 0, :].unsqueeze(2).broadcast_to([P, TOPK, TOPK]),
                                  top_v[:, 1, :].unsqueeze(1).broadcast_to([P, TOPK, TOPK]),
                                  ALU.add).then_inc(topk_step, 1)
                rest(2, n * 4 + 2)
                step(6)
                dve.tensor_copy(all_i[:, n, :, :], top_i[:, :, :])
                dve.max(best_v[:, 0:8], CND).then_inc(topk_step, 1)
                step(7)
                dve.max_index(best_p[:, 0:8], best_v[:, 0:8], CND)
                dve.match_replace(CN2, best_v[:, 0:8], CND, LOWEST).then_inc(topk_step, 1)
                step(8)
                dve.max(best_v[:, 8:16], CN2).then_inc(topk_step, 1)
                rest(3, n * 4 + 3)
                step(9)
                dve.max_index(best_p[:, 8:16], best_v[:, 8:16], CN2).then_inc(topk_step, 1)
                step(10)
                dve.tensor_copy(all_v[:, n, :], best_v[:, :])
                dve.tensor_copy(all_p[:, n, :], best_p[:, :]).then_inc(topk_step, 1)
                step(11)

            chunk = [TOPK_UNTIL]

            def another():
                rest(chunk[0] % SLOTS, chunk[0])
                chunk[0] += 1

            iota16 = iota[:, 0:TOPK].unsqueeze(1).broadcast_to([P, PH * TOPK, TOPK])
            for tb in range(TB):
                heads = slice(tb * PH, (tb + 1) * PH)
                dve.tensor_tensor(choice[:, 2, tb, :].rearrange("p (h k) -> p h k", k=TOPK), all_v[:, heads, :],
                                  all_v[:, heads, 0:1].broadcast_to([P, PH, TOPK]), ALU.subtract)\
                   .then_inc(shifted, 1)
                places = all_p[:, heads, :].rearrange("p h k -> p (h k)")
                dve.tensor_scalar(digit[:, 0, :], places, 4, None, ALU.logical_shift_right)
                link(dve.tensor_scalar(digit[:, 1, :], places, TOPK - 1, None, ALU.bitwise_and))
                for p in range(2):
                    b3 = BIG.rearrange("p (m a) -> p m a", a=TOPK)
                    another()
                    link(dve.tensor_tensor(b3, digit[:, p, :].unsqueeze(2).broadcast_to([P, PH * TOPK, TOPK]),
                                           iota16, ALU.is_equal))
                    another()
                    b4 = BIG.rearrange("p (h k a) -> p h k a", k=TOPK, a=TOPK)
                    link(dve.tensor_tensor(b4, b4, all_i[:, heads, p, :].unsqueeze(2)
                                           .broadcast_to([P, PH, TOPK, TOPK]), ALU.mult))
                    another()
                    link(dve.tensor_reduce(choice[:, p, tb, :], b3, AX.X, ALU.add))
                another()
                another()
            while chunk[0] < DECODE_UNTIL:
                another()
            dve.sem_inc(scratch_free, 1)
            another()
            dve.wait_ge(exped, 1)
            e3 = choice[:, 2, :, :].rearrange("p b (h k) -> p (b h) k", k=TOPK)
            link(dve.tensor_reduce(gsum[:, 0, :], e3, AX.X, ALU.add))
            another()
            link(dve.reciprocal(gsum[:, 1, :], gsum[:, 0, :]))
            another()
            dve.tensor_tensor(e3, e3, gsum[:, 1, :].unsqueeze(2).broadcast_to([P, TB * PH, TOPK]), ALU.mult)\
               .then_inc(choice_ready, TB)
            another()
            for c in range(SOFTMAX_UNTIL, TURN_AT + 2):
                rest(c % SLOTS, c)
            for tb in range(TB):
                dve.wait_ge(turned, tb + 1)
                tt = slice(tb * P, (tb + 1) * P)
                dve.tensor_scalar(choice_t[:, 0, tt], bank[6 + tb][:, 0:P], -1.0, None, ALU.mult)\
                   .then_inc(choice_t_ready, 1)
                dve.tensor_copy(choice_t[:, 1:3, tt], bank[6 + tb][:, P:3 * P].rearrange("p (n t) -> p n t", n=2))\
                   .then_inc(choice_t_ready, 1)
            for c in range(TURN_AT + 2, MERGE):
                rest(c % SLOTS, c)

            def one2(q, g):
                for t in range(GT):
                    tt = g * GT + t
                    last = dve.tensor_scalar(ONE2[:, q, t, :], iota, choice_t[:, 1, bass.ds(tt, 1)],
                                             choice_t[:, 2, bass.ds(tt, 1)], ALU.is_equal, ALU.mult)
                last.then_inc(one2_made, 1)

            def gate(q, g):
                dve.wait_ge(gates_done, g + 1)
                a = A3[:, :, bass.ds(g * GT, GT)]
                dve.tensor_tensor(a, a, bank[4 + q][:, :].rearrange("p (t c) -> p c t", t=GT), ALU.mult)\
                   .then_inc(gated, 1)

            def multiply(j, n):
                dve.wait_ge(a_made, n + (MERGE + 1))
                dve.tensor_tensor(A3[:, n + MERGE, :], A3[:, n + MERGE, :], gelu_buf[:, j % 2, :], ALU.mult)\
                   .then_inc(multiplied, 1)

            dve.wait_ge(choice_t_ready, 2 * TB)
            for j in range(SLOTS):
                rest(j, MERGE + j)
                if j >= 2:
                    dve.wait_ge(gated, 2 * (j - 1))
                    multiply(j, j - 2)
                    dve.wait_ge(multiplied, j - 1)
                for q in range(2):
                    if j == 1 and q == 0:
                        dve.wait_ge(ones_made, 1)
                        dve.wait_ge(a_made, MERGE)
                    if j:
                        gate(q, 2 * (j - 1) + q)
                    one2(q, 2 * j + q)
            with dve.Fori(1, (CHUNKS - MERGE) // SLOTS) as i:
                for j in range(SLOTS):
                    rest(j, i * SLOTS + (MERGE + j))
                    dve.wait_ge(gated, i * (2 * SLOTS) + 2 * (j - 1))
                    multiply(j, i * SLOTS + (j - 2))
                    one2_at = i * (2 * SLOTS) + 2 * j
                    dve.wait_ge(multiplied, i * SLOTS + (j - 1))
                    for q in range(2):
                        gate(q, one2_at + (q - 2))
                        one2(q, one2_at + q)
            for j in range(2):
                rest(j, CHUNKS + j)
                if j == 0:
                    dve.wait_ge(gated, GROUPS - 2)
                multiply(j, CHUNKS - MERGE - 2 + j)
            dve.wait_ge(multiplied, CHUNKS - MERGE)
            for q in range(2):
                gate(q, GROUPS - 2 + q)

            def w_rest(j, v):
                dve.wait_ge(whi_made, v + 1)
                dve.tensor_tensor(w_lo[:, j % 2, :], A3[:, v, :], w_hi[:, j % 2, :].bitcast(F32), ALU.subtract)\
                   .then_inc(wlo_made, 1)

            dve.wait_ge(gated, GROUPS)
            for v in range(2):
                w_rest(v, v)
            for v in (2, 3):
                w_rest(v, v)
                rest(v, CHUNKS + v)
            with dve.Fori(1, CHUNKS // SLOTS) as i:
                for j in range(SLOTS):
                    w_rest(j, i * SLOTS + j)
                    rest(j, i * SLOTS + (CHUNKS + j))

            dve.wait_ge(piece_done, 4 * CHUNKS)
            for n in range(2 * TB):
                tb, half = n // 2, slice(n % 2 * 512, n % 2 * 512 + 512)
                tmp = A[:, 4096 + n * 512:4096 + n * 512 + 512]
                link(dve.tensor_tensor(tmp, bank[4 + n][:, :], g2b[:, half], ALU.mult))
                dve.tensor_tensor(x1n[:, tb, half], x1n[:, tb, half], tmp, ALU.add).then_inc(res_ready, 1)
            dve.wait_ge(fsq_ready, 2 * TB)
            dve.tensor_reduce(fsum[:, 1, 0:TB], fsum[:, 0, :].rearrange("p (b h) -> p b h", h=2), AX.X, ALU.add)\
               .then_inc(fsq_ready, 1)
            dve.wait_ge(froot_ready, 1)
            link(dve.reciprocal(fsum[:, 1, TB:2 * TB], fsum[:, 2, 0:TB]))
            dve.wait_ge(fin_in, 16)
            dve.wait_ge(res_ready, 2 * TB)
            for tb in range(TB):
                dve.scalar_tensor_tensor(x1n[:, tb, :], x1n[:, tb, :], fsum[:, 1, TB + tb:TB + tb + 1], fin,
                                         ALU.mult, ALU.mult).then_inc(out_ready, 1)

        @block.gpsimd
        def _(pool):
            pool.wait_ge(scratch_free, 1)
            pool.memset(A3[:, MERGE:CHUNKS, :], 1.0).then_inc(ones_made, 1)


def bias_places():
    import numpy as np

    grid_w, kh, kw = 64, 8, 16
    q = np.arange(T)
    r, c = q // grid_w, q % grid_w
    start = np.clip(c - kw // 2, 0, grid_w - kw)
    inside = (c[None, :] >= start[:, None]) & (c[None, :] < start[:, None] + kw)
    dr = r[None, :] - r[:, None] + kh - 1
    dc = np.where(inside, c[None, :] - c[:, None] + kw - 1, 0)
    return inside, dr, dc


def kernel(**inputs):
    import numpy as np
    import concourse.bacc as bacc
    from concourse.bass_utils import run_bass_kernel_spmd

    f = {k: np.asarray(v) for k, v in inputs.items()}
    one = {k: f[k][0] for k in f if k not in ("c", "c_ctx", "final_norm_g")}

    def tiles(a):
        return np.ascontiguousarray(a.reshape(-1, P, a.shape[-1]).transpose(1, 0, 2))

    def column(a):
        return a.reshape(-1, P).T

    def in_blocks(a):
        return np.ascontiguousarray(a.reshape(KD, P, -1, BLK).transpose(2, 1, 0, 3))

    c2 = np.stack([column(f["c"][0]), column(f["c_ctx"])], axis=-1).reshape(P, 2 * KD)
    conv = one["conv_w"].reshape(3, CONV_T, P).transpose(2, 1, 0).reshape(P, 3 * CONV_T)
    cols = np.concatenate([c2, column(one["ada_b"]), column(one["norm1_g"]), column(one["norm2_g"]),
                           column(one["out_norm_g"]), conv], axis=1)
    rows = np.concatenate([one["sgu_b"].reshape(-1), one["ada_b"][G2 * D:]])[None]
    pick = np.kron(np.ones((4, 1)), np.eye(32))
    constants = np.concatenate([np.eye(P), np.ones((P, P)), np.kron(np.eye(2), np.ones((HD, HD))),
                                np.tile(np.arange(P), (P, 1)), np.tile(pick[:, 0:1], (1, P)), pick[:, 0:2]],
                               axis=1).astype(np.float32)
    inside, dr, dc = bias_places()
    bias_mask = np.full((HEADS, T, T), NEG, np.float32)
    bias_mask[:, inside] = one["na_rpb"][:, dr[inside], dc[inside]]
    bias_mask = bias_mask.reshape(HEADS, TB, P, T).transpose(2, 0, 1, 3)
    arrays = {
        "x_t": tiles(one["x"].T),
        "ctx_t": tiles(one["ctx"].T),
        "cols": cols,
        "rows": rows,
        "sgu_gain": np.broadcast_to(one["sgu_norm_g"], (P, BLK)),
        "final_gain": np.broadcast_to(f["final_norm_g"], (P, D)),
        "constants": constants,
        "sgu_wt": one["sgu_w"].transpose(2, 0, 1),
        "bias_mask": bias_mask,
        "ada_w": in_blocks(one["ada_w"]),
        "w_in": in_blocks(one["w_in"]),
        "w_out": in_blocks(one["w_out"]),
        "w_q": in_blocks(one["peer_wq"]),
        "subkeys_t": one["peer_subkeys"].transpose(3, 0, 1, 2).reshape(P, LISTS, NK),
        "peer_u_t": one["peer_u"].reshape(NK, NK, KD, P).transpose(1, 3, 2, 0).reshape(NK, P, D),
        "peer_v": one["peer_v"],
    }
    nc = bacc.Bacc("TRN2", target_bir_lowering=False, num_devices=1)
    arrays = {f"in_{k}": np.ascontiguousarray(v) for k, v in arrays.items()}
    args = [nc.dram_tensor(k, v.shape, mybir.dt.from_np(v.dtype), kind="ExternalInput").ap()
            for k, v in arrays.items()]
    result = nc.dram_tensor("out_x", (T, D), F32, kind="ExternalOutput").ap()
    build(nc, *args, result)
    r = run_bass_kernel_spmd(nc, [arrays], core_ids=[0])
    return r.results[0]["out_x"].reshape(1, T, D)
```

```python
from contextlib import ExitStack

import concourse.bass as bass
from concourse import mybir

F32 = mybir.dt.float32
F32R = mybir.dt.float32r
U32 = mybir.dt.uint32
ALU = mybir.AluOpType
ACT = mybir.ActivationFunctionType
AX = mybir.AxisListType

P = 128
D = 1024
KD = D // P
T = 256
TB = T // P
CTX = 256
KEYS = T + CTX
HEADS, HD = 8, 64
CONV_T = 2
SGU_G = 4
EPS = 1e-6
PH = 8
NK = 128
TOPK = 16
LISTS = 2 * PH
BLK = 256
RING = 4
NEG = -1.0e30
LOWEST = -3.0e38
SLOTS = 4
CHUNKS = NK
PIECE = D // 2
PIECES = 4
GT = 4
GROUPS = T // GT

EARLY = 4
BESIDE = 8
TOPK_UNTIL = BESIDE * (PH - EARLY)
DECODE_UNTIL = TOPK_UNTIL + 24
SOFTMAX_UNTIL = DECODE_UNTIL + 4
TURN_AT = SOFTMAX_UNTIL
MERGE = 64
SCRATCH = 96
assert CHUNKS - MERGE == GROUPS and TURN_AT + 4 <= MERGE

COL_C = 0
COL_ADA_B = COL_C + 2 * KD
COL_N1 = COL_ADA_B + 6 * KD
COL_N2 = COL_N1 + KD
COL_OG = COL_N2 + KD
COL_CONV = COL_OG + KD
COLS = COL_CONV + 3 * CONV_T

SH1, SC1, G1, SH2, SC2, G2 = range(6)
W_IN_BLOCKS = 11


def schedule():
    steps = [("stat1", 0)]
    behind = []
    splits = []

    def ada(b):
        steps.append(("ada", b))
        behind.append(b)

    def turn():
        if behind:
            b = behind.pop(0)
            steps.append(("spread" if b // 4 == G2 else "column", b))

    for s in (SC1, SH1):
        for b in range(4):
            ada(4 * s + b)
            if len(behind) > 1:
                turn()
    steps.append(("split", 0))
    turn()
    steps.append(("split", 1))
    later = [4 * s + b for s in (G1, SH2, SC2) for b in range(4)]
    for b in (4, 3, 1, 2, 0, 5, 6, 7, 8, 9, 10):
        steps.append(("w_in", b))
        splits.append(("w_in", b))
        if b == 3:
            steps.append(("ctx_squares", 0))
        if b == 1:
            steps.append(("stat1", 1))
        if b == 2:
            steps.append(("context", 0))
        if len(splits) + 1 < W_IN_BLOCKS:
            steps.append(("split", len(splits) + 1))
        turn()
        if b == 0:
            steps.append(("gating", 0))
        if b == 9:
            steps += [("squares", 0), ("squares", 1)]
        ada(later.pop(0))
        if b == 9:
            steps += [("group", 0), ("group", 1)] + [("quarter", q) for q in range(4)]
    turn()
    ada(later.pop(0))
    splits += [("w_out", b) for b in range(4)]
    units = HEADS * TB
    for u in range(units + 3):
        if u < units:
            steps.append(("scores", u))
        if u == 0:
            turn()
        if 0 <= u - 2 < units:
            steps.append(("turned", u - 2))
        if u >= 3:
            steps.append(("attend", u - 3))
        if 1 <= u <= 12:
            steps.append(("quarter", 3 + u))
        if u in (7, 11):
            steps.append(("yn", u // 4 - 1))
        if u == 13:
            steps.append(("squares", 2))
    q0 = len(splits)
    steps += [("squares", 3), ("group", 2), ("group", 3), ("yn", 2), ("yn", 3)]
    steps += [("split", q0), ("split", q0 + 1), ("split", q0 + 2), ("w_out", 0), ("stat2", 0), ("x1_turned", 0)]
    ada(4 * G2)
    ada(4 * G2 + 1)
    steps.append(("split", q0 + 3))
    splits += [("w_q", b) for b in range(PH)]
    for b in range(PH):
        steps.append(("w_q", b))
        turn()
        if b == 6:
            steps.append(("first_chunks", 0))
        if b == 0:
            steps.append(("keys", 0))
        if b == 0:
            steps.append(("split", q0 + 4))
        elif b >= 3 and b < 6:
            steps.append(("split", q0 + b + 2))
        if b >= 2:
            steps.append(("keys", b - 1))
        if b in (4, 5):
            ada(4 * G2 + b - 2)
    turn()
    steps.append(("keys", PH - 1))
    return steps, splits


def blocks_of(steps):
    out = []
    for kind, b in steps:
        if kind == "w_out":
            out += [("w_out", n) for n in range(4)]
        elif kind in ("ada", "w_in", "w_q"):
            out.append((kind, b))
    waiting = [("ada", 4 * G2), ("ada", 4 * G2 + 1)]
    out = [b for b in out if b not in waiting]
    at = out.index(("w_q", RING - 1)) + 1
    out[at:at] = waiting
    first = out.index(("w_q", 0))
    second = [b for b in out[first:] if b not in waiting]
    return out, [[b for b in out if b not in second], second]


def bank_uses(steps):
    place, used, turn = {}, [0] * 8, [0]

    def put(name, b):
        place[name] = (b, used[b])
        used[b] += 1

    def ring(name, banks=(0, 1, 2, 3)):
        put(name, banks[turn[0] % len(banks)])
        turn[0] += 1

    sections = {SC1: 4, SH1: 5, G1: 6, SH2: 7, SC2: 6}
    for kind, n in steps:
        if kind == "stat1":
            put((kind, n), 7)
        elif kind == "w_in" and n >= 7:
            ring((kind, n, 0))
            ring((kind, n, 1))
        elif kind == "w_in":
            ring((kind, n, 0))
        elif kind == "column":
            if n % 4 == 0:
                put(("mod", n // 4), sections[n // 4])
        elif kind == "scores":
            put((kind, n), 4 + n % 2)
        elif kind == "turned":
            put((kind, n), 6 + n % 2)
        elif kind == "attend":
            if n % 4 == 0:
                put((kind, n // 4), n // 4 % 2)
        elif kind == "group":
            put((kind, n), 2 + n % 2)
        elif kind == "w_out":
            for m in range(4):
                put((kind, m), 4 + m)
        elif kind == "stat2":
            put((kind, 0), 0)
        elif kind == "x1_turned":
            for j in range(4):
                put((kind, j), (1, 2, 3, 7)[j])
        elif kind in ("squares", "split", "context", "ctx_squares", "yn", "quarter", "first_chunks"):
            pass
        elif kind == "keys":
            put((kind, n), 4 + n % 4)
        elif kind == "ada" and n in (4 * G2, 4 * G2 + 1):
            put((kind, n), 4 + n % 2)
        else:
            ring((kind, n))
    return place, used


def build(nc, x_t, ctx_t, cols, rows, sgu_gain, final_gain, constants, sgu_wt, bias_mask, ada_w, w_in,
          w_out, w_q, subkeys_t, peer_u_t, peer_v, out):
    steps, splits = schedule()
    blocks, rings = blocks_of(steps)
    place, used = bank_uses(steps)
    ring_of = {block: n for ring in rings for n, block in enumerate(ring)}
    sources = {"ada": ada_w, "w_in": w_in, "w_out": w_out, "w_q": w_q}
    v_rows = peer_v.rearrange("(a b) d -> b a d", b=CHUNKS)

    q0 = splits.index(("w_q", 0))

    def whole(n):
        return sum(kind != "w_out" for kind, _ in splits[:n + 1])

    def last_read(block_name):
        kind, b = block_name
        if kind == "w_in":
            return ("w_in", b, 1 if b >= 7 else 0)
        return ("w_out", 3) if kind == "w_out" else block_name

    with ExitStack() as stack:
        def sbuf(name, shape, dtype=F32):
            return stack.enter_context(nc.sbuf_tensor(name, shape, dtype))

        def sem(name):
            return stack.enter_context(nc.semaphore(name))

        bank = [stack.enter_context(nc.psum_tensor(f"bank{b}", [P, 512], F32)) for b in range(8)]

        with ExitStack() as views:
            def view(name, size):
                return views.enter_context(nc.sbuf_tensor(name, [P, size], F32R))

            view("below_h", 2048)
            h_low = view("h_low", KD * KEYS)
            view("above_h", 13312 - 6144)
            query_hi0 = view("query_hi0", KD * BLK)
            view("below_ring2", 1024)
            ring2_low = view("ring2_low", RING * KD * BLK)
            ring_low = view("ring_low", RING * KD * BLK)
        with ExitStack() as views:
            view("below_yn", 2048)
            yn_low = view("yn_low", KD * T)
            out_hi2 = view("out_hi2", KD * BLK)
        A = sbuf("A", [P, CHUNKS * T])
        A3 = A[:, :].rearrange("p (c t) -> p c t", t=T)

        at = [0]

        def part(size, start=None):
            if start is not None:
                at[0] = start
            at[0] += size
            return A[:, at[0] - size:at[0]]

        X1 = part(KD * T).rearrange("p (k t) -> p k t", k=KD)
        H = part(KD * KEYS).rearrange("p (k t) -> p k t", k=KD)
        H_lo = h_low[:, :].rearrange("p (k t) -> p k t", k=KD)
        C0 = part(KD * CTX).rearrange("p (k t) -> p k t", k=KD)
        YR = part(KD * T).rearrange("p (k t) -> p k t", k=KD)
        YS = part(KD * T).rearrange("p (k t) -> p k t", k=KD)
        CV = part(6 * T).rearrange("p (k t) -> p k t", k=6)
        Z = part(CONV_T * (T + 2)).rearrange("p (k t) -> p k t", k=CONV_T)
        SU = part(2 * T).rearrange("p (k t) -> p k t", k=2)
        SV = part(TB * BLK).rearrange("p (b c) -> p b c", b=TB)
        Q = part(4 * T).rearrange("p (k t) -> p k t", k=4)
        K = part(4 * KEYS).rearrange("p (k t) -> p k t", k=4)
        V = part(4 * 512).rearrange("p (c n) -> p c n", c=4)
        PR = part(3 * KEYS).rearrange("p (b n) -> p b n", b=3)
        PT = part(3 * KEYS).rearrange("p (b c n) -> p b c n", b=3, c=4)
        swt = part(SGU_G * P).rearrange("p (g n) -> p g n", g=SGU_G)
        sg_gain = part(BLK)
        assert at[0] <= 24576
        SVS = PT[:, 0, :, :].rearrange("p c n -> p (c n)").rearrange("p (b c) -> p b c", b=TB)
        sgb_row = PR[0:1, 0, :]
        g2_row = A[0:1, 12288:12288 + D]
        WR = part(RING * KD * BLK, 24576).rearrange("p (s k n) -> p s k n", s=RING, k=KD)
        WR_lo = ring_low[:, :].rearrange("p (s k n) -> p s k n", s=RING, k=KD)
        WR2_lo = ring2_low[:, :].rearrange("p (s k n) -> p s k n", s=RING, k=KD)
        WR2 = A[:, 16384:24576].rearrange("p (s k n) -> p s k n", s=RING, k=KD)
        SQ = part(KD * KEYS, 15364).rearrange("p (k t) -> p k t", k=KD)
        YN = A[:, 2048:4096].rearrange("p (k t) -> p k t", k=KD)
        H2 = A[:, 4096:6144].rearrange("p (k t) -> p k t", k=KD)
        SK = A[:, 6144:8192].rearrange("p (l n) -> p l n", l=LISTS)
        QP = A[:, 8192:12288].rearrange("p (l t) -> p l t", l=LISTS)
        S = A[:, 28672:32768].rearrange("p (b l n) -> p b l n", b=TB, l=LISTS)
        BIG = A[:, 24576:26624]
        LS2 = A[:, 25088:25600].rearrange("p (b l n) -> p b l n", b=TB, l=2)
        CND, CN2 = (A[:, a:a + 512].rearrange("p (b n) -> p b n", b=TB) for a in (25600, 26112))
        all_i = A[:, 27648:28160].rearrange("p (n l k) -> p n l k", l=2, k=TOPK)
        all_v = A[:, 28160:28416].rearrange("p (n k) -> p n k", k=TOPK)
        all_p = A[:, 28416:28672].bitcast(U32).rearrange("p (n k) -> p n k", k=TOPK)
        digit = A[:, 26880:27136].bitcast(U32).rearrange("p (l n) -> p l n", l=2)
        assert 24576 == SCRATCH * T

        with ExitStack() as views:
            query_hi2 = view("query_hi2", KD * BLK)
            query_hi3 = view("query_hi3", KD * BLK)
        bias = sbuf("stage", [P, SLOTS, D])
        stage = bias
        BM = bias[:, :, :].rearrange("p s d -> p (s d)").rearrange("p (h b n) -> p h b n", h=HEADS, b=TB)
        hi = sbuf("hi", [P, PIECES, PIECE], F32R)
        lo = sbuf("lo", [P, PIECES, PIECE], F32R)
        h2_hi = sbuf("h2_hi", [P, KD, T], F32R)
        h2_lo = sbuf("h2_lo", [P, KD, T], F32R)
        with ExitStack() as views:
            out_hi3 = view("out_hi3", KD * BLK)
        x1n = sbuf("x1n", [P, TB, D])
        YN_lo = yn_low[:, :].rearrange("p (k t) -> p k t", k=KD)
        yn_hi = h2_hi
        tile_hi = [t[:, :, :].rearrange("p a b -> p (a b)").rearrange("p (k n) -> p k n", k=KD)
                   for t in (hi, lo)]
        place_hi = [t[:, :].rearrange("p (k n) -> p k n", k=KD) for t in (query_hi0, yn_low, query_hi2, query_hi3)]
        weight_hi = [tile_hi[n % 2] for n in range(13)]
        weight_hi += [t[:, :].rearrange("p (k n) -> p k n", k=KD) for t in (out_hi2, out_hi3)]
        weight_hi += [place_hi[n] for n in (0, 2, 3, 1, 0, 1, 0, 1)]
        hi_free = [None, None] + splits[:W_IN_BLOCKS] + [("w_in", 10), ("w_in", 10)]
        hi_free += [None, ("scores", HEADS * TB - 1), ("scores", HEADS * TB - 1), ("w_out", 3)]
        hi_free += [("w_q", 0), ("w_q", 3), ("w_q", 4), ("w_q", 5)]
        h_hi = (h2_hi, h2_lo)
        w_hi = h2_hi[:, 0:2, :]
        w_lo = h2_lo[:, 0:2, :]
        g2b = sbuf("g2b", [P, D])
        gate_buf = sbuf("gate_buf", [P, 4, GT, NK])
        ONE1 = gate_buf[:, 0:2]
        ONE2 = gate_buf[:, 2:4]
        mrow = gate_buf[:, 0, :, :].rearrange("p (n a) b -> p n (a b)", n=2)
        rinv = gate_buf[:, 2, :, :].rearrange("p a b -> p (a b)")
        root = gate_buf[:, 3, :, :].rearrange("p a b -> p (a b)")
        roots = [root, gate_buf[:, 1, :, :].rearrange("p a b -> p (a b)")]
        fin = gate_buf[:, :, :, :].rearrange("p a b c -> p (a b c)")[:, 0:D]
        choice = sbuf("choice", [P, 3, TB, P])
        choice_t = sbuf("choice_t", [P, 3, T])
        gelu_buf = choice[:, 0:2, :, :].rearrange("p n b t -> p n (b t)")
        con = sbuf("con", [P, 5 * P + 2])
        ident, ones, group_ones, iota, row_ones = (con[:, n * P:(n + 1) * P] for n in range(5))
        row_pick = con[:, 5 * P:5 * P + 2]
        colv = sbuf("colv", [P, COLS])
        csil = sbuf("csil", [P, KD, 32])
        mod = sbuf("mod", [P, 5, KD, 2])
        gain1 = sbuf("gain1", [P, KD, 2])
        gain2 = sbuf("gain2", [P, KD])
        eps = sbuf("eps", [P, 1])
        gms = sbuf("gms", [P, 3, TB * SGU_G])
        nmax = sbuf("nmax", [P, HEADS * TB])
        psum_ = sbuf("psum_", [P, HEADS * TB])
        pinv = sbuf("pinv", [P, HEADS * TB])
        top_v = sbuf("top_v", [P, TB, 2, TOPK])
        top_i = sbuf("top_i", [P, TB, 2, TOPK], U32)
        gsum = sbuf("gsum", [P, 2, TB * PH])
        fsum = sbuf("fsum", [P, 3, TB * 2])

        consts_in, x_in, ctx_in, cols_in, gating_in, bias_in, subkeys_in, g2_row_in = map(
            sem, ("consts_in", "x_in", "ctx_in", "cols_in", "gating_in", "bias_in", "subkeys_in", "g2_row_in"))
        ring_full = [[sem(f"ring{r}_full{s}") for s in range(RING)] for r in range(2)]
        bank_full = [sem(f"bank_full{b}") for b in range(8)]
        bank_free = [sem(f"bank_free{b}") for b in range(8)]
        dve_done = sem("dve_done")
        weight_rounded, weight_split, h_full, h_rounded, ctx_ready = map(
            sem, ("weight_rounded", "weight_split", "h_full", "h_rounded", "ctx_ready"))
        query_split = sem("query_split")
        quarter_rounded, quarter_split = sem("quarter_rounded"), sem("quarter_split")
        yn_rounded, yn_split = sem("yn_rounded"), sem("yn_split")
        silu_zero, silu_ready, sq_ready, root_ready, h_ready, mrow_ready = map(
            sem, ("silu_zero", "silu_ready", "sq_ready", "root_ready", "h_ready", "mrow_ready"))
        proj_ready, sv_ready, svroot_ready, svn_ready = map(
            sem, ("proj_ready", "sv_ready", "svroot_ready", "svn_ready"))
        nmax_ready, exp_ready, prob_ready, pt_ready = map(sem, ("nmax_ready", "exp_ready", "prob_ready", "pt_ready"))
        yr_ready, ys_ready, yroot_ready, yn_ready = map(sem, ("yr_ready", "ys_ready", "yroot_ready", "yn_ready"))
        h2_scaled = sem("h2_scaled")
        x1_ready, x1s_ready, h2_ready, h2_hi_ready, h2_split = map(
            sem, ("x1_ready", "x1s_ready", "h2_ready", "h2_hi_ready", "h2_split"))
        qp_ready, keys_ready = map(sem, ("qp_ready", "keys_ready"))
        eps_ready, gms_ready = sem("eps_ready"), sem("gms_ready")
        stage_full = [sem(f"stage_full{s}") for s in range(SLOTS)]
        hi_made, lo_made, piece_done, a_made = map(sem, ("hi_made", "lo_made", "piece_done", "a_made"))
        ones_made, multiplied, one1_square = map(sem, ("ones_made", "multiplied", "one1_square"))
        topk_step, shifted, exped, choice_ready, scratch_free, turned, choice_t_ready = map(
            sem, ("topk_step", "shifted", "exped", "choice_ready", "scratch_free", "turned", "choice_t_ready"))
        one1_made, one2_made, gates_done, gated = map(sem, ("one1_made", "one2_made", "gates_done", "gated"))
        whi_made, wlo_made, out_full, fsum_ready = map(
            sem, ("whi_made", "wlo_made", "out_full", "fsum_ready"))
        fin_in, res_ready, fsq_ready, froot_ready, out_ready, stored = map(
            sem, ("fin_in", "res_ready", "fsq_ready", "froot_ready", "out_ready", "stored"))

        block = stack.enter_context(nc.Block())

        def opened(eng, name):
            b, use = place[name]
            if use:
                eng.wait_ge(bank_free[b], use)
            return bank[b]

        def full(eng, name):
            b, use = place[name]
            eng.wait_ge(bank_full[b], use + 1)
            return bank[b]

        def fill_sem(name):
            return bank_full[place[name][0]]

        def free_sem(name):
            return bank_free[place[name][0]]

        @block.sync
        def _(sp):
            sp.dma_start(colv[:, :], cols).then_inc(cols_in, 16)
            sp.dma_start(X1, x_t).then_inc(x_in, 16)
            sp.dma_start(con[:, :], constants).then_inc(consts_in, 16)
            for n, (matrix, b) in enumerate(blocks):
                late = (matrix, b) in rings[1]
                slot = ring_of[(matrix, b)]
                if slot >= RING:
                    old = place[last_read(rings[late][slot - RING])]
                    sp.wait_ge(bank_full[old[0]], old[1] + 1)
                elif late:
                    old = place[("attend", 3)]
                    sp.wait_ge(bank_full[old[0]], old[1] + 1)
                sp.dma_start((WR2 if late else WR)[:, slot % RING], sources[matrix][b])\
                  .then_inc(ring_full[late][slot % RING], 16)
                if n == 2 * RING + 1:
                    sp.dma_start(C0, ctx_t).then_inc(ctx_in, 16)
                if n == RING - 1:
                    sp.dma_start(sgb_row, rows[:, 0:SGU_G * P]).then_inc(gating_in, 16)
                    sp.dma_start(sg_gain, sgu_gain).then_inc(gating_in, 16)
                    sp.dma_start(swt, sgu_wt).then_inc(gating_in, 16)
                if (matrix, b) == ("w_q", PH - 1):
                    old, use = place[("w_q", 2)]
                    sp.wait_ge(bank_full[old], use + 1)
                    for j in range(SLOTS):
                        sp.dma_start(stage[:, j, :], peer_u_t[j]).then_inc(stage_full[j], 16)
                if n == 27:
                    sp.dma_start(BM, bias_mask).then_inc(bias_in, 16)
                    sp.wait_ge(h_ready, KD)
                    sp.dma_start(SK, subkeys_t).then_inc(subkeys_in, 16)
                if (matrix, b) == ("w_q", 0):
                    sp.wait_ge(yr_ready, 1)
                    sp.dma_start(g2_row, rows[:, SGU_G * P:]).then_inc(g2_row_in, 16)
            with sp.Fori(1, CHUNKS // SLOTS) as i:
                for j in range(SLOTS):
                    sp.wait_ge(lo_made, i * (2 * SLOTS) + (2 * (j + 1 - SLOTS)))
                    sp.dma_start(stage[:, j, :], peer_u_t[i * SLOTS + j]).then_inc(stage_full[j], 16)
            with sp.Fori(0, CHUNKS // SLOTS) as i:
                for j in range(SLOTS):
                    sp.wait_ge(lo_made, i * (2 * SLOTS) + (2 * (CHUNKS + j + 1 - SLOTS)))
                    sp.dma_start(stage[:, j, :], v_rows[i * SLOTS + j]).then_inc(stage_full[j], 16)
            sp.wait_ge(gates_done, GROUPS)
            sp.dma_start(fin, final_gain).then_inc(fin_in, 16)
            for n in range(2 * TB):
                tb, half = n // 2, slice(n % 2 * 512, n % 2 * 512 + 512)
                sp.wait_ge(out_ready, n + 1)
                sp.dma_start(out[tb * P:(tb + 1) * P, half], x1n[:, tb, half]).then_inc(stored, 16)
            sp.wait_ge(stored, 16 * 2 * TB)

        @block.tensor
        def _(pe):
            def weights(block_name):
                n, late = ring_of[block_name], block_name in rings[1]
                pe.wait_ge(ring_full[late][n % RING], 16 * (n // RING + 1))
                return (WR2 if late else WR)[:, n % RING]

            def split_weights(block_name):
                n = splits.index(block_name)
                if n < q0 + 3:
                    pe.wait_ge(weight_split, whole(n))
                else:
                    pe.wait_ge(query_split, n - q0 - 2)
                return weight_hi[n], (WR2_lo if block_name[0] == "w_q" else WR_lo)[:, ring_of[block_name] % RING]

            def contract3(o, lhs, rhs, ready=None):
                for k in range(KD):
                    if ready is not None:
                        pe.wait_ge(ready, k + 1)
                    (a_hi, a_lo), (b_hi, b_lo) = lhs(k), rhs(k)
                    pe.matmul(o, a_hi, b_hi, start=(k == 0), stop=False)
                    pe.matmul(o, a_hi, b_lo, start=False, stop=False)
                    mm = pe.matmul(o, a_lo, b_hi, start=False, stop=(k == KD - 1))
                return mm

            def contract(o, lhs, rhs, ready=None):
                for k in range(KD):
                    if ready is not None:
                        pe.wait_ge(ready, k + 1)
                    mm = pe.matmul(o, lhs(k), rhs(k), start=(k == 0), stop=(k == KD - 1))
                return mm

            def ada(b):
                o = opened(pe, ("ada", b))
                w = weights(("ada", b))
                for k in range(KD):
                    q = slice(32 * (k % 4), 32 * (k % 4) + 32)
                    mm = pe.matmul(o[q, 0:BLK], csil[:, k, :], w[:, k, :], start=(k < 4), stop=(k >= 4),
                                   tile_position=(0, 32 * (k % 4)))
                mm.then_inc(fill_sem(("ada", b)), 1)

            ada_blocks = [b for kind, b in steps if kind == "ada"]

            def column(b):
                s, n = b // 4, ada_blocks.index(b)
                o = opened(pe, ("mod", s)) if b % 4 == 0 else bank[place[("mod", s)][0]]
                pe.wait_ge(mrow_ready, n + 1)
                for m in range(2):
                    c = 2 * (2 * (b % 4) + m)
                    mm = pe.matmul(o[:, c:c + 2], mrow[:, n % 2, m * P:(m + 1) * P], row_pick, start=True, stop=True)
                if b % 4 == 3:
                    mm.then_inc(fill_sem(("mod", s)), 1)

            def spread(b):
                n, c = ada_blocks.index(b), b % 4 * BLK
                o = opened(pe, ("spread", b))
                pe.wait_ge(mrow_ready, n + 1)
                pe.wait_ge(g2_row_in, 16)
                pe.matmul(o[:, 0:BLK], row_ones, mrow[:, n % 2, :], start=True, stop=False)
                pe.matmul(o[:, 0:BLK], ones[0:1, :], g2_row[:, c:c + BLK], start=False, stop=True)\
                  .then_inc(fill_sem(("spread", b)), 1)

            def in_projection(b):
                w_hi, w_lo = split_weights(("w_in", b))

                def w(m):
                    return lambda k: (w_hi[:, k, m * P:(m + 1) * P], w_lo[:, k, m * P:(m + 1) * P])

                def all_w(k):
                    return w_hi[:, k, :], w_lo[:, k, :]

                def h(t, size=P):
                    return lambda k: (h_hi[t // T][:, k, t % T:t % T + size], H_lo[:, k, t:t + size])

                if b in (0, 1, 2, 3, 5, 6):
                    o = opened(pe, ("w_in", b, 0))
                    for m in range(2):
                        mm = contract3(o[:, m * T:(m + 1) * T], w(m), h(0, T))
                    mm.then_inc(fill_sem(("w_in", b, 0)), 1)
                elif b == 4:
                    o = opened(pe, ("w_in", b, 0))
                    for t in range(TB):
                        mm = contract3(o[:, t * BLK:(t + 1) * BLK], h(t * P), all_w, h_ready if t == 0 else None)
                    mm.then_inc(fill_sem(("w_in", b, 0)), 1)
                elif b in (7, 8):
                    pe.wait_ge(ctx_ready, KD)
                    for m in range(2):
                        o = opened(pe, ("w_in", b, m))
                        for t in (0, T):
                            mm = contract3(o[:, t:t + T], w(m), h(t, T))
                        mm.then_inc(fill_sem(("w_in", b, m)), 1)
                else:
                    for m in range(2):
                        o = opened(pe, ("w_in", b, m))
                        for c in range(2):
                            mm = contract3(o[:, c * BLK:(c + 1) * BLK], h((2 * m + c) * P), all_w)
                        mm.then_inc(fill_sem(("w_in", b, m)), 1)

            def gating():
                o = opened(pe, ("gating", 0))
                pe.wait_ge(svn_ready, 1)
                pe.wait_ge(gating_in, 48)
                for g in range(SGU_G):
                    for tb in range(TB):
                        half = slice(HD * (g % 2), HD * (g % 2) + HD)
                        oo = o[half, (g // 2) * T + tb * P:(g // 2) * T + (tb + 1) * P]
                        pe.matmul(oo, SV[:, tb, g * HD:(g + 1) * HD], swt[:, g, :], start=True, stop=False)
                        mm = pe.matmul(oo, ones[0:1, 0:HD], sgb_row[:, g * P:(g + 1) * P], start=False, stop=True)
                mm.then_inc(fill_sem(("gating", 0)), 1)

            def scores(u):
                h, tb = u // 2, u % 2
                if u == 0:
                    pe.wait_ge(bias_in, 16)
                    pe.wait_ge(proj_ready, W_IN_BLOCKS)
                o = opened(pe, ("scores", u))
                pp = slice(HD * (h % 2), HD * (h % 2) + HD)
                qq = Q[pp, h // 2, tb * P:(tb + 1) * P]
                pe.matmul(o[:, 0:T], ident, BM[:, h, tb, :], start=True, stop=False)
                pe.matmul(o[:, 0:T], qq, K[pp, h // 2, 0:T], start=False, stop=True)
                pe.matmul(o[:, T:KEYS], qq, K[pp, h // 2, T:KEYS], start=True, stop=True)\
                  .then_inc(fill_sem(("scores", u)), 1)

            def turned_probs(v):
                o = opened(pe, ("turned", v))
                pe.wait_ge(prob_ready, v + 1)
                for c in range(4):
                    mm = pe.transpose(o[:, c * P:(c + 1) * P], PR[:, v % 3, c * P:(c + 1) * P], ident)
                mm.then_inc(fill_sem(("turned", v)), 1)

            def attend(v):
                h, tb = v // 2, v % 2
                name = ("attend", v // 4)
                o = opened(pe, name) if v % 4 == 0 else bank[place[name][0]]
                pe.wait_ge(pt_ready, v + 1)
                for c in range(4):
                    mm = pe.matmul(o[HD * (h % 2):HD * (h % 2) + HD, tb * P:(tb + 1) * P],
                                   V[:, c, h * HD:(h + 1) * HD], PT[:, v % 3, c, :],
                                   start=(c == 0), stop=(c == 3))
                if v % 4 == 3:
                    mm.then_inc(fill_sem(name), 1)

            def group_sums(j):
                o = opened(pe, ("group", j))
                pe.wait_ge(ys_ready, j + 1)
                pe.matmul(o[:, :], group_ones, YS[:, 2 * j:2 * j + 2, :], start=True, stop=True)\
                  .then_inc(fill_sem(("group", j)), 1)

            def out_projection():
                pe.wait_ge(quarter_split, 16)
                w = [(weight_hi[splits.index(("w_out", b))], WR_lo[:, ring_of[("w_out", b)] % RING]) for b in range(4)]
                for k in range(KD):
                    pe.wait_ge(yn_split, k + 1)
                    for m in range(KD):
                        name = ("w_out", m // 2)
                        o = opened(pe, name) if k == 0 and m % 2 == 0 else bank[place[name][0]]
                        oo, cc = o[:, m % 2 * T:m % 2 * T + T], slice(m % 2 * P, m % 2 * P + P)
                        a_hi, a_lo = w[m // 2]
                        pe.matmul(oo, a_hi[:, k, cc], yn_hi[:, k, :], start=(k == 0 and m % 2 == 0), stop=False,
                                  skip_group_check=True)
                        pe.matmul(oo, a_hi[:, k, cc], YN_lo[:, k, :], start=False, stop=False, skip_group_check=True)
                        mm = pe.matmul(oo, a_lo[:, k, cc], yn_hi[:, k, :], start=False, stop=(k == KD - 1),
                                       skip_group_check=True)
                        if k == KD - 1 and m % 2 == 1:
                            mm.then_inc(fill_sem(("w_out", m // 2)), 1)

            def second_stat():
                o = opened(pe, ("stat2", 0))
                for m in range(KD):
                    if m % 2 == 0:
                        pe.wait_ge(x1s_ready, m // 2 + 1)
                    mm = pe.matmul(o[:, 0:T], ones, YS[:, m, :], start=(m == 0), stop=(m == KD - 1))
                mm.then_inc(fill_sem(("stat2", 0)), 1)

            def turned_x1():
                for j in range(4):
                    o = opened(pe, ("x1_turned", j))
                    for m in range(4):
                        mm = pe.transpose(o[:, m * P:(m + 1) * P],
                                          X1[:, 4 * (j % 2) + m, (j // 2) * P:(j // 2 + 1) * P], ident)
                    mm.then_inc(fill_sem(("x1_turned", j)), 1)

            def queries(b):
                w_hi, w_lo = split_weights(("w_q", b))
                o = opened(pe, ("w_q", b))
                for m in range(2):
                    mm = contract3(o[:, m * T:(m + 1) * T],
                                   lambda k: (w_hi[:, k, m * P:(m + 1) * P], w_lo[:, k, m * P:(m + 1) * P]),
                                   lambda k: (h2_hi[:, k, :], h2_lo[:, k, :]), h2_split if b == 0 and m == 0 else None)
                mm.then_inc(fill_sem(("w_q", b)), 1)

            def keys(h):
                if h == 0:
                    pe.wait_ge(subkeys_in, 16)
                o = opened(pe, ("keys", h))
                pe.wait_ge(qp_ready, h + 1)
                for tb in range(TB):
                    for l in range(2):
                        m = 2 * tb + l
                        mm = pe.matmul(o[:, m * P:(m + 1) * P], QP[:, 2 * h + l, tb * P:(tb + 1) * P],
                                       SK[:, 2 * h + l, :], start=True, stop=True)
                mm.then_inc(fill_sem(("keys", h)), 1)

            for kind, n in steps:
                if kind == "stat1":
                    pe.wait_ge(consts_in, 16)
                    pe.wait_ge(sq_ready, n + 1)
                    o = opened(pe, (kind, n))
                    contract(o[:, 0:T], lambda k: ones, lambda k: SQ[:, k, n * T:(n + 1) * T])\
                        .then_inc(fill_sem((kind, n)), 1)
                elif kind == "ada":
                    if n == 4 * SC1:
                        pe.wait_ge(silu_ready, 1)
                    ada(n)
                elif kind == "column":
                    column(n)
                elif kind == "spread":
                    spread(n)
                elif kind == "w_in":
                    in_projection(n)
                elif kind == "gating":
                    gating()
                elif kind == "scores":
                    scores(n)
                elif kind == "turned":
                    turned_probs(n)
                elif kind == "attend":
                    attend(n)
                elif kind in ("squares", "split", "context", "ctx_squares", "yn", "quarter", "first_chunks"):
                    pass
                elif kind == "group":
                    group_sums(n)
                elif kind == "w_out":
                    out_projection()
                elif kind == "stat2":
                    second_stat()
                elif kind == "x1_turned":
                    turned_x1()
                elif kind == "w_q":
                    queries(n)
                else:
                    keys(n)

            def u_chunk(j, c):
                o = bank[j % SLOTS][:, 0:T]
                for h in range(2):
                    pe.wait_ge(lo_made, c * 2 + (h + 1))
                    for n in range(KD // 2):
                        k, p, kk = KD // 2 * h + n, (2 * j + h) % PIECES, slice(n * P, (n + 1) * P)
                        pe.matmul(o, hi[:, p, kk], h2_hi[:, k, :], start=(k == 0), stop=False)
                        pe.matmul(o, hi[:, p, kk], h2_lo[:, k, :], start=False, stop=False)
                        mm = pe.matmul(o, lo[:, p, kk], h2_hi[:, k, :], start=False, stop=(k == KD - 1))
                    mm.then_inc(piece_done, 1)

            def gates(j, g):
                pe.wait_ge(one1_made, g + 1)
                pe.wait_ge(one2_made, g + 1)
                for t in range(GT):
                    mm = pe.matmul(bank[4 + j][:, t * NK:(t + 1) * NK], ONE1[:, j, t, :], ONE2[:, j, t, :],
                                   start=True, stop=True)
                mm.then_inc(gates_done, 1)

            pe.wait_ge(h2_split, KD)
            for b in range(SLOTS):
                pe.wait_ge(bank_free[b], used[b])
            for j in range(2 * SLOTS):
                if j >= SLOTS:
                    pe.wait_ge(a_made, j + 1 - SLOTS)
                u_chunk(j, j)
            with pe.Fori(1, TURN_AT // (2 * SLOTS)) as i:
                for j in range(2 * SLOTS):
                    pe.wait_ge(a_made, i * (2 * SLOTS) + (j + 1 - SLOTS))
                    u_chunk(j, i * (2 * SLOTS) + j)
            for c in range(TURN_AT // (2 * SLOTS) * (2 * SLOTS), MERGE):
                if c == TURN_AT:
                    pe.wait_ge(choice_ready, TB)
                    for tb in range(TB):
                        pe.wait_ge(bank_free[6 + tb], used[6 + tb])
                        for n in range(3):
                            mm = pe.transpose(bank[6 + tb][:, n * P:(n + 1) * P], choice[:, n, tb, :], ident)
                        mm.then_inc(turned, 1)
                pe.wait_ge(a_made, c + 1 - SLOTS)
                u_chunk(c % SLOTS, c)
            for b in (4, 5):
                pe.wait_ge(bank_free[b], used[b])
            for j in range(SLOTS):
                if j >= 2:
                    pe.wait_ge(gated, j - 1)
                gates(j % 2, j)
                pe.wait_ge(a_made, MERGE + j + 1 - SLOTS)
                u_chunk(j, MERGE + j)
            with pe.Fori(1, (CHUNKS - MERGE) // SLOTS) as i:
                for j in range(SLOTS):
                    pe.wait_ge(gated, i * SLOTS + (j - 1))
                    gates(j % 2, i * SLOTS + j)
                    pe.wait_ge(a_made, i * SLOTS + (MERGE + j + 1 - SLOTS))
                    u_chunk(j, i * SLOTS + (MERGE + j))

            def v_chunk(j, v, first=False, last=False):
                pe.wait_ge(wlo_made, v + 1)
                order = [(tb, half) for half in range(2) for tb in range(TB)]
                for n, (tb, half) in enumerate(sorted(order) if last else order):
                    if last or n % TB == 0:
                        pe.wait_ge(lo_made, v * 2 + (2 * CHUNKS + half + 1))
                    p = (2 * j + half) % PIECES
                    o = bank[4 + 2 * tb + half][:, :]
                    tt = slice(tb * P, (tb + 1) * P)
                    pe.matmul(o, w_hi[:, j % 2, tt], hi[:, p, :], start=first, stop=False)
                    pe.matmul(o, w_hi[:, j % 2, tt], lo[:, p, :], start=False, stop=False)
                    mm = pe.matmul(o, w_lo[:, j % 2, tt], hi[:, p, :], start=False, stop=last)
                    if last:
                        mm.then_inc(out_full, 1)
                    elif n % TB == TB - 1:
                        mm.then_inc(piece_done, 1)

            pe.wait_ge(gated, GROUPS)
            pe.wait_ge(choice_t_ready, 2 * TB)
            for j in range(4):
                v_chunk(j, j, first=(j == 0))
            with pe.Fori(1, CHUNKS // 4 - 1) as i:
                for j in range(4):
                    v_chunk(j, i * 4 + j)
            for j in range(3):
                v_chunk(j, CHUNKS - 4 + j)
            v_chunk(3, CHUNKS - 1, last=True)

        def probs_out(act, v):
            name = ("turned", v)
            o = full(act, name)
            act.activation(PT[:, v % 3, :, :].rearrange("p c n -> p (c n)"), o[:, :], ACT.Copy)\
               .then_inc(pt_ready, 1)
            act.wait_ge(pt_ready, v + 1)
            act.sem_inc(free_sem(name), 1)

        def group_root(act, m):
            name = ("group", m)
            o = full(act, name)
            if m >= 2:
                act.wait_ge(yn_ready, 2 * m - 2)
            act.activation(roots[m % 2], o[:, :], ACT.Sqrt, bias=eps[:, :], scale=1.0 / HD).then_inc(yroot_ready, 1)

        @block.scalar
        def _(act):
            act.wait_ge(cols_in, 16)
            act.wait_ge(silu_zero, 1)
            act.activation(csil[:, :, 0:2], colv[:, COL_C:COL_C + 2 * KD].rearrange("p (k v) -> p k v", v=2),
                           ACT.Silu).then_inc(silu_ready, 1)
            act.wait_ge(eps_ready, 1)

            def round_h(part):
                for k in range(KD):
                    act.wait_ge(h_full, KD * part + k + 1)
                    act.activation(h_hi[part][:, k, :], H[:, k, part * T:(part + 1) * T], ACT.Copy)\
                       .then_inc(h_rounded, 1)

            def projection(b):
                for half in range(2 if b >= 7 else 1):
                    name = ("w_in", b, half)
                    o = full(act, name)
                    two = o[:, :].rearrange("p (m t) -> p m t", m=2)
                    if b == 3:
                        ins = act.activation(SU, two, ACT.Gelu_apprx_tanh)
                    elif b == 4:
                        ins = act.activation(SV, two, ACT.Gelu_apprx_tanh)
                    elif b in (5, 6):
                        ins = act.activation(Q[:, 2 * (b - 5):2 * (b - 5) + 2, :], two, ACT.Copy, scale=HD ** -0.5)
                    elif b in (7, 8):
                        ins = act.activation(K[:, 2 * (b - 7) + half, :], o[:, :], ACT.Copy)
                    elif b in (9, 10):
                        ins = act.activation(V[:, 2 * half:2 * half + 2, (b - 9) * BLK:(b - 8) * BLK], two, ACT.Copy)
                    else:
                        ins = act.activation(CV[:, 2 * b:2 * b + 2, :], two, ACT.Copy)
                    ins.then_inc(free_sem(name), 1)
                act.wait_ge(free_sem(name), place[name][1] + 1)
                act.sem_inc(proj_ready, 1)
                if b == 4:
                    act.activation(SVS, SV, ACT.Square).then_inc(sv_ready, 1)
                if b == 3:
                    act.wait_ge(gms_ready, 1)
                    act.activation(gms[:, 1, :], gms[:, 0, :], ACT.Sqrt, bias=eps[:, :], scale=1.0 / HD)\
                       .then_inc(svroot_ready, 1)

            def round_chunk(j, use, done=None):
                for h in range(2):
                    if done is not None:
                        act.wait_ge(piece_done, done + h)
                    if h == 0:
                        act.wait_ge(stage_full[j], use)
                    act.activation(hi[:, (2 * j + h) % PIECES, :], stage[:, j, h * PIECE:(h + 1) * PIECE], ACT.Copy)\
                       .then_inc(hi_made, 1)

            def round_h2(k):
                act.wait_ge(h2_ready, k + 1)
                act.activation(h2_hi[:, k, :], H2[:, k, :], ACT.Copy).then_inc(h2_hi_ready, 1)

            ada_seen = 0
            for kind, n in steps:
                if kind == "split":
                    block_name = splits[n]
                    slot = ring_of[block_name]
                    late = block_name[0] == "w_q"
                    if hi_free[n]:
                        name = hi_free[n]
                        full(act, last_read(name) if name in splits else name)
                    act.wait_ge(ring_full[late][slot % RING], 16 * (slot // RING + 1))
                    act.activation(weight_hi[n], (WR2 if late else WR)[:, slot % RING], ACT.Copy)\
                       .then_inc(weight_rounded, 1)
                elif kind == "column" and n == 4 * SH1 + 3:
                    round_h(0)
                elif kind == "quarter":
                    name, kk = ("w_out", n // 4), slice(n % 4 * 2, n % 4 * 2 + 2)
                    if n % 4 == 0:
                        free = hi_free[splits.index(name)]
                        if free:
                            full(act, last_read(free))
                        act.wait_ge(ring_full[0][ring_of[name] % RING], 16 * (ring_of[name] // RING + 1))
                    act.activation(weight_hi[splits.index(name)][:, kk, :], WR[:, ring_of[name] % RING, kk, :],
                                   ACT.Copy).then_inc(quarter_rounded, 1)
                elif kind == "yn":
                    for k in (2 * n, 2 * n + 1):
                        act.wait_ge(yn_ready, k + 1)
                        act.activation(yn_hi[:, k, :], YN[:, k, :], ACT.Copy).then_inc(yn_rounded, 1)
                elif kind == "ctx_squares":
                    act.wait_ge(ctx_in, 16)
                    act.activation(SQ[:, :, T:KEYS], C0, ACT.Square).then_inc(sq_ready, 1)
                elif kind == "context":
                    round_h(1)
                elif kind == "stat1":
                    if n == 0:
                        act.wait_ge(x_in, 16)
                        act.activation(SQ[:, :, 0:T], X1, ACT.Square).then_inc(sq_ready, 1)
                    o = full(act, (kind, n))
                    act.activation(root[:, n * T:(n + 1) * T], o[:, 0:T], ACT.Sqrt, bias=eps[:, :], scale=1.0 / D)\
                       .then_inc(root_ready, 1)
                elif kind == "ada":
                    o = full(act, (kind, n))
                    act.activation(mrow[:, ada_seen % 2, :], o[:, 0:BLK], ACT.Copy).then_inc(mrow_ready, 1)
                    ada_seen += 1
                    act.wait_ge(mrow_ready, ada_seen)
                    act.sem_inc(free_sem((kind, n)), 1)
                elif kind == "spread":
                    o = full(act, (kind, n))
                    act.activation(g2b[:, n % 4 * BLK:(n % 4 + 1) * BLK], o[:, 0:BLK], ACT.Copy)\
                       .then_inc(free_sem((kind, n)), 1)
                elif kind == "w_in":
                    projection(n)
                elif kind == "scores":
                    if n >= 2:
                        probs_out(act, n - 2)
                    o = full(act, (kind, n))
                    act.wait_ge(nmax_ready, n + 1)
                    if n >= 3:
                        act.wait_ge(pt_ready, n - 2)
                    act.activation(PR[:, n % 3, :], o[:, :], ACT.Exp, bias=nmax[:, n:n + 1],
                                   accum_out=psum_[:, n:n + 1]).then_inc(exp_ready, 1)
                    if n == HEADS * TB - 1:
                        probs_out(act, n - 1)
                        probs_out(act, n)
                elif kind == "squares":
                    act.wait_ge(yr_ready, n + 1)
                    act.activation(YS[:, 2 * n:2 * n + 2, :], YR[:, 2 * n:2 * n + 2, :], ACT.Square)\
                       .then_inc(ys_ready, 1)
                elif kind == "group":
                    group_root(act, n)
                elif kind == "w_out":
                    for b in range(4):
                        act.wait_ge(x1_ready, b + 1)
                        act.activation(YS[:, 2 * b:2 * b + 2, :], X1[:, 2 * b:2 * b + 2, :], ACT.Square)\
                           .then_inc(x1s_ready, 1)
                elif kind == "stat2":
                    o = full(act, (kind, n))
                    act.activation(root[:, 0:T], o[:, 0:T], ACT.Sqrt, bias=eps[:, :], scale=1.0 / D)\
                       .then_inc(root_ready, 1)
                elif kind == "x1_turned":
                    for k in range(KD):
                        act.wait_ge(h2_scaled, k + 1)
                        act.activation(H2[:, k, :], H2[:, k, :], ACT.Identity, bias=mod[:, SH2, k, 0:1])\
                           .then_inc(h2_ready, 1)
                        if k:
                            round_h2(k - 1)
                    round_h2(KD - 1)
                    for j in range(4):
                        name = (kind, j)
                        o = full(act, name)
                        act.activation(x1n[:, j // 2, (j % 2) * 512:(j % 2) * 512 + 512], o[:, :], ACT.Copy)\
                           .then_inc(free_sem(name), 1)
                elif kind == "first_chunks":
                    for c in range(2):
                        round_chunk(c, 16)
                elif kind == "w_q":
                    o = full(act, (kind, n))
                    act.activation(QP[:, 2 * n:2 * n + 2, :].rearrange("p l t -> p (l t)"), o[:, :], ACT.Copy)\
                       .then_inc(qp_ready, 1)
                    act.wait_ge(qp_ready, n + 1)
                    act.sem_inc(free_sem((kind, n)), 1)
                elif kind == "keys":
                    o = full(act, (kind, n))
                    act.activation(S[:, :, 2 * n:2 * n + 2, :].rearrange("p b l n -> p b (l n)"),
                                   o[:, :].rearrange("p (b n) -> p b n", b=TB), ACT.Copy).then_inc(keys_ready, 1)
                    act.wait_ge(keys_ready, n + 1)
                    act.sem_inc(free_sem((kind, n)), 1)

            def gelu_chunk(j, c):
                act.activation(A3[:, c, :], bank[j % SLOTS][:, 0:T], ACT.Gelu_apprx_tanh).then_inc(a_made, 1)

            def gelu_beside(j, n, reused=True):
                if reused:
                    act.wait_ge(multiplied, n - 1)
                act.activation(gelu_buf[:, j % 2, :], bank[j % SLOTS][:, 0:T], ACT.Gelu_apprx_tanh)\
                   .then_inc(a_made, 1)

            def u_steps(i, j):
                round_chunk(j, i * 16 + 16, i * (2 * SLOTS) + (2 * j - 3))
                gelu_chunk(j - 2, i * SLOTS + (j - 2))

            def one1_squares(j, g, reused=True):
                if reused:
                    act.wait_ge(gates_done, g - 1)
                for t in range(GT):
                    last = act.activation(ONE1[:, j % 2, t, :], iota, ACT.Square,
                                          bias=choice_t[:, 0, bass.ds(g * GT + t, 1)])
                last.then_inc(one1_square, 1)

            def one1_rest(j, g):
                act.wait_ge(one1_square, g + 1)
                act.activation(ONE1[:, j % 2], ONE1[:, j % 2], ACT.Relu, bias=1.0, scale=-1.0).then_inc(one1_made, 1)

            for c in (2, 3):
                round_chunk(c, 16, 2 * c - 3)
                gelu_chunk(c - 2, c - 2)
            with act.Fori(1, DECODE_UNTIL // SLOTS) as i:
                for j in range(SLOTS):
                    u_steps(i, j)
            act.wait_ge(shifted, TB)
            act.activation(choice[:, 2, :, :], choice[:, 2, :, :], ACT.Exp).then_inc(exped, 1)
            with act.Fori(DECODE_UNTIL // SLOTS, MERGE // SLOTS) as i:
                for j in range(SLOTS):
                    u_steps(i, j)
            act.wait_ge(choice_t_ready, 2 * TB)
            for j in range(SLOTS):
                c = MERGE + j
                one1_squares(j, j, reused=j >= 2)
                round_chunk(j, 16 * (c // SLOTS) + 16, 2 * c - 3)
                one1_rest(j, j)
                if j < 2:
                    gelu_chunk(j + 2, c - 2)
                else:
                    gelu_beside(j + 2, j - 2, reused=False)
            with act.Fori(1, (CHUNKS - MERGE) // SLOTS) as i:
                for j in range(SLOTS):
                    one1_squares(j, i * SLOTS + j)
                    round_chunk(j, i * 16 + (16 * (MERGE // SLOTS) + 16), i * (2 * SLOTS) + (2 * (MERGE + j) - 3))
                    one1_rest(j, i * SLOTS + j)
                    gelu_beside(j + 2, i * SLOTS + (j - 2))
            def w_round(j, v):
                act.activation(w_hi[:, j % 2, :], A3[:, v, :], ACT.Copy).then_inc(whi_made, 1)

            for j in range(2):
                n = CHUNKS + j
                round_chunk(j, 16 * (n // SLOTS) + 16, 2 * n - 3)
                gelu_beside(j + 2, n - 2 - MERGE)
                if j == 0:
                    act.wait_ge(gated, GROUPS)
                    act.wait_ge(piece_done, 2 * CHUNKS)
                w_round(j, j)

            act.wait_ge(multiplied, CHUNKS - MERGE)
            for v in (2, 3):
                act.wait_ge(piece_done, 2 * (CHUNKS + v - 1))
                w_round(v, v)
                round_chunk(v, 16 * (CHUNKS // SLOTS) + 16, 2 * (CHUNKS + v) - 3)
            with act.Fori(1, CHUNKS // SLOTS) as i:
                for j in range(SLOTS):
                    act.wait_ge(piece_done, i * (2 * SLOTS) + 2 * (CHUNKS + j - 1))
                    w_round(j, i * SLOTS + j)
                    round_chunk(j, i * 16 + (16 * (CHUNKS // SLOTS) + 16), i * (2 * SLOTS) + (2 * (CHUNKS + j) - 3))

            act.activation(fsum[:, 2, TB:TB + 1], eps[:, :], ACT.Sqrt)
            for tb in range(TB):
                for n in (2 * tb, 2 * tb + 1):
                    act.wait_ge(res_ready, n + 1)
                    act.activation(A[:, n * 512:n * 512 + 512], x1n[:, tb, n % 2 * 512:n % 2 * 512 + 512], ACT.Square,
                                   accum_out=fsum[:, 0, n:n + 1]).then_inc(fsq_ready, 1)
                act.wait_ge(fsum_ready, tb + 1)
                act.activation(fsum[:, 2, tb:tb + 1], fsum[:, 1, tb:tb + 1], ACT.Sqrt, bias=eps[:, :], scale=1.0 / D)\
                   .then_inc(froot_ready, 1)

        @block.vector
        def _(dve):
            chain = [0]

            def link(ins):
                chain[0] += 1
                ins.then_inc(dve_done, 1)
                dve.wait_ge(dve_done, chain[0])

            dve.memset(csil[:, :, :], 0.0).then_inc(silu_zero, 1)
            dve.memset(eps[:, :], EPS).then_inc(eps_ready, 1)
            dve.memset(Z[:, :, 0:1], 0.0)
            link(dve.memset(Z[:, :, T + 1:T + 2], 0.0))
            def modulation(s):
                o = full(dve, ("mod", s))
                b = colv[:, COL_ADA_B + s * KD:COL_ADA_B + (s + 1) * KD].unsqueeze(2).broadcast_to([P, KD, 2])
                link(dve.tensor_tensor(mod[:, s, :, :], o[:, 0:2 * KD].rearrange("p (k v) -> p k v", v=2), b, ALU.add))
                dve.sem_inc(free_sem(("mod", s)), 1)

            def scale_h(part):
                for k in range(KD):
                    h = H[:, k, part * T:(part + 1) * T]
                    dve.tensor_scalar(h, h, gain1[:, k, part:part + 1], mod[:, SH1, k, part:part + 1], ALU.mult,
                                      ALU.add).then_inc(h_full, 1)
                    if k:
                        rest_of_h(part, k - 1)
                rest_of_h(part, KD - 1)

            def rest_of_h(part, k):
                tt = slice(part * T, (part + 1) * T)
                dve.wait_ge(h_rounded, KD * part + k + 1)
                dve.tensor_tensor(H_lo[:, k, tt], H[:, k, tt], h_hi[part][:, k, :].bitcast(F32), ALU.subtract)\
                   .then_inc((h_ready, ctx_ready)[part], 1)

            def group_reciprocal(j):
                dve.wait_ge(yroot_ready, j + 1)
                dve.sem_inc(free_sem(("group", j)), 1)
                link(dve.reciprocal(roots[j % 2], roots[j % 2]))

            def group_norm(j):
                for m in range(2):
                    k = 2 * j + m
                    dve.scalar_tensor_tensor(YN[:, k, :], YR[:, k, :], colv[:, COL_OG + k:COL_OG + k + 1],
                                             roots[j % 2][:, m * T:(m + 1) * T], ALU.mult, ALU.mult)\
                       .then_inc(yn_ready, 1)
                dve.wait_ge(yn_ready, 2 * j + 2)

            def softmax(u):
                if u < HEADS * TB:
                    o = full(dve, ("scores", u))
                    dve.tensor_reduce(nmax[:, u:u + 1], o[:, :], AX.X, ALU.max, negate=True).then_inc(nmax_ready, 1)
                if u >= 1:
                    v = u - 1
                    dve.wait_ge(exp_ready, v + 1)
                    dve.sem_inc(free_sem(("scores", v)), 1)
                    link(dve.reciprocal(pinv[:, v:v + 1], psum_[:, v:v + 1]))
                    dve.tensor_scalar(PR[:, v % 3, :], PR[:, v % 3, :], pinv[:, v:v + 1], None, ALU.mult)\
                       .then_inc(prob_ready, 1)
                for j in ([(u - 7) // 4] if u >= 7 and u % 4 == 3 else [3] if u == HEADS * TB else []):
                    o = full(dve, ("attend", j))
                    link(dve.tensor_copy(YR[:, 4 + j, :], o[:, 0:T]))
                    dve.sem_inc(free_sem(("attend", j)), 1)
                    if j % 2:
                        dve.sem_inc(yr_ready, 1)

            def quarter_rest(n):
                name, kk = ("w_out", n // 4), slice(n % 4 * 2, n % 4 * 2 + 2)
                slot = ring_of[name] % RING
                dve.wait_ge(quarter_rounded, n + 1)
                dve.tensor_tensor(WR_lo[:, slot, kk, :], WR[:, slot, kk, :],
                                  weight_hi[splits.index(name)][:, kk, :].bitcast(F32), ALU.subtract)\
                   .then_inc(quarter_split, 1)

            def weight_rest(n):
                late = n >= q0
                slot = ring_of[splits[n]] % RING
                dve.wait_ge(weight_rounded, whole(n))
                dve.tensor_tensor((WR2_lo if late else WR_lo)[:, slot], (WR2 if late else WR)[:, slot],
                                  weight_hi[n].bitcast(F32), ALU.subtract).then_inc(weight_split, 1)

            pairs = [(tb, l) for tb in range(TB) for l in range(2)]
            all_i2 = all_i.rearrange("p (b h) l k -> p b h (l k)", b=TB)
            steps_done = [0]

            def choose(h, beside):
                def made(ins):
                    ins.then_inc(topk_step, 1)
                    steps_done[0] += 1

                def then(k):
                    beside(k)
                    dve.wait_ge(topk_step, steps_done[0])

                best = [tb * PH + h for tb in range(TB)]
                lists = [S[:, tb, 2 * h + l, :] for tb, l in pairs]
                for n, (tb, l) in enumerate(pairs):
                    last = dve.max(top_v[:, tb, l, 0:8], lists[n])
                made(last)
                then(1)
                for n, (tb, l) in enumerate(pairs):
                    dve.max_index(top_i[:, tb, l, 0:8], top_v[:, tb, l, 0:8], lists[n])
                    last = dve.match_replace(LS2[:, tb, l, :], top_v[:, tb, l, 0:8], lists[n], LOWEST)
                made(last)
                then(2)
                for tb, l in pairs:
                    last = dve.max(top_v[:, tb, l, 8:16], LS2[:, tb, l, :])
                made(last)
                then(3)
                for tb, l in pairs:
                    last = dve.max_index(top_i[:, tb, l, 8:16], top_v[:, tb, l, 8:16], LS2[:, tb, l, :])
                made(last)
                for tb in range(TB):
                    last = dve.tensor_tensor(CND[:, tb, :].rearrange("p (a b) -> p a b", b=TOPK),
                                             top_v[:, tb, 0, :].unsqueeze(2).broadcast_to([P, TOPK, TOPK]),
                                             top_v[:, tb, 1, :].unsqueeze(1).broadcast_to([P, TOPK, TOPK]), ALU.add)
                made(last)
                then(4)
                dve.tensor_copy(all_i2[:, :, h, :], top_i.rearrange("p b l k -> p b (l k)"))
                for tb, n in enumerate(best):
                    last = dve.max(all_v[:, n, 0:8], CND[:, tb, :])
                made(last)
                then(5)
                for tb, n in enumerate(best):
                    dve.max_index(all_p[:, n, 0:8], all_v[:, n, 0:8], CND[:, tb, :])
                    last = dve.match_replace(CN2[:, tb, :], all_v[:, n, 0:8], CND[:, tb, :], LOWEST)
                made(last)
                then(6)
                for tb, n in enumerate(best):
                    last = dve.max(all_v[:, n, 8:16], CN2[:, tb, :])
                made(last)
                then(7)
                for tb, n in enumerate(best):
                    last = dve.max_index(all_p[:, n, 8:16], all_v[:, n, 8:16], CN2[:, tb, :])
                made(last)
                then(8)

            def rest(j, c):
                for h in range(2):
                    p = (2 * j + h) % PIECES
                    dve.wait_ge(hi_made, c * 2 + (h + 1))
                    dve.tensor_tensor(lo[:, p, :], stage[:, j, h * PIECE:(h + 1) * PIECE], hi[:, p, :].bitcast(F32),
                                      ALU.subtract).then_inc(lo_made, 1)

            for kind, n in steps:
                if kind == "group" and n < 2:
                    group_reciprocal(n)
                elif kind == "split":
                    if n < q0 + 3:
                        weight_rest(n)
                elif kind == "stat1":
                    tt = slice(n * T, (n + 1) * T)
                    dve.wait_ge(root_ready, n + 1)
                    link(dve.reciprocal(rinv[:, tt], root[:, tt]))
                    dve.sem_inc(free_sem((kind, n)), 1)
                    link(dve.tensor_tensor(H[:, :, tt], (X1, C0)[n], rinv[:, tt].unsqueeze(1).broadcast_to([P, KD, T]),
                                           ALU.mult))
                elif kind == "column" and n % 4 == 3:
                    modulation(n // 4)
                    if n // 4 == SC1:
                        link(dve.scalar_tensor_tensor(gain1[:, :, :], mod[:, SC1, :, :], 1.0,
                                                      colv[:, COL_N1:COL_N1 + KD].unsqueeze(2)
                                                      .broadcast_to([P, KD, 2]), ALU.add, ALU.mult))
                    elif n // 4 == SC2:
                        link(dve.scalar_tensor_tensor(gain2[:, :], mod[:, SC2, :, 0], 1.0,
                                                      colv[:, COL_N2:COL_N2 + KD], ALU.add, ALU.mult))
                    elif n // 4 == SH1:
                        scale_h(0)
                elif kind == "context":
                    scale_h(1)
                elif (kind, n) == ("w_in", 3):
                    dve.wait_ge(sv_ready, 1)
                    dve.wait_ge(gating_in, 48)
                    groups = "p b (g c) -> p (b g) c"
                    dve.tensor_reduce(gms[:, 0, :], SVS.rearrange(groups, c=HD), AX.X, ALU.add).then_inc(gms_ready, 1)
                    dve.wait_ge(svroot_ready, 1)
                    link(dve.reciprocal(gms[:, 2, :], gms[:, 1, :]))
                    link(dve.tensor_tensor(SV.rearrange(groups, c=HD), SV.rearrange(groups, c=HD),
                                           gms[:, 2, :].unsqueeze(2).broadcast_to([P, TB * SGU_G, HD]), ALU.mult))
                    dve.tensor_tensor(SV, SV, sg_gain.unsqueeze(1).broadcast_to([P, TB, BLK]), ALU.mult)\
                       .then_inc(svn_ready, 1)
                elif (kind, n) == ("w_in", 5):
                    dve.wait_ge(proj_ready, 5)
                    o = full(dve, ("gating", 0))
                    link(dve.tensor_tensor(YR[:, 2:4, :], SU, o[:, :].rearrange("p (m t) -> p m t", m=2), ALU.mult))
                    dve.sem_inc(free_sem(("gating", 0)), 1)
                    link(dve.tensor_tensor(Z[:, :, 1:T + 1], CV[:, 2:4, :], CV[:, 4:6, :], ALU.mult))
                    for tap in range(3):
                        for m in range(CONV_T):
                            w = colv[:, COL_CONV + 3 * m + tap:COL_CONV + 3 * m + tap + 1]
                            z = Z[:, m, tap:tap + T]
                            if tap == 0:
                                ins = dve.tensor_scalar(YR[:, m, :], z, w, None, ALU.mult)
                            else:
                                ins = dve.scalar_tensor_tensor(YR[:, m, :], z, w, YR[:, m, :], ALU.mult, ALU.add)
                        link(ins)
                    dve.tensor_tensor(YR[:, 0:2, :], YR[:, 0:2, :], CV[:, 0:2, :], ALU.mult).then_inc(yr_ready, 1)
                    dve.sem_inc(yr_ready, 1)
                elif kind == "scores":
                    softmax(n)
                    if n in (4, 8):
                        group_norm(n // 4 - 1)
                elif kind == "squares" and n == 3:
                    softmax(HEADS * TB)
                elif kind == "group":
                    group_reciprocal(n)
                    group_norm(n)
                elif kind == "w_out":
                    for b in range(4):
                        name = ("w_out", b)
                        o = full(dve, name)
                        for m in range(2):
                            k = 2 * b + m
                            ins = dve.scalar_tensor_tensor(X1[:, k, :], o[:, m * T:(m + 1) * T], mod[:, G1, k, 0:1],
                                                           X1[:, k, :], ALU.mult, ALU.add)
                        ins.then_inc(x1_ready, 1)
                        dve.wait_ge(x1_ready, b + 1)
                        dve.sem_inc(free_sem(name), 1)
                elif kind == "stat2":
                    dve.wait_ge(root_ready, 3)
                    dve.sem_inc(free_sem(("stat2", 0)), 1)
                    link(dve.reciprocal(rinv[:, 0:T], root[:, 0:T]))
                    LAG = 3
                    for k in range(KD + LAG):
                        if k < KD:
                            dve.scalar_tensor_tensor(H2[:, k, :], X1[:, k, :], gain2[:, k:k + 1], rinv[:, 0:T],
                                                     ALU.mult, ALU.mult).then_inc(h2_scaled, 1)
                        if k >= LAG:
                            dve.wait_ge(h2_hi_ready, k - LAG + 1)
                            m = k - LAG
                            dve.tensor_tensor(h2_lo[:, m, :], H2[:, m, :], h2_hi[:, m, :].bitcast(F32),
                                              ALU.subtract).then_inc(h2_split, 1)
                elif kind == "quarter":
                    if n < 4:
                        quarter_rest(n)
                    elif n > 4:
                        quarter_rest(n - 1)
                elif kind == "squares" and n == 2:
                    quarter_rest(15)
                elif kind == "yn":
                    for k in (2 * n, 2 * n + 1):
                        dve.wait_ge(yn_rounded, k + 1)
                        dve.tensor_tensor(YN_lo[:, k, :], YN[:, k, :], yn_hi[:, k, :].bitcast(F32), ALU.subtract)\
                           .then_inc(yn_split, 1)
                elif kind == "first_chunks":
                    for c in range(2):
                        rest(c, c)
                elif kind == "keys" and n < EARLY:
                    dve.wait_ge(keys_ready, n + 1)
                    choose(n, lambda at: None)

            dve.wait_ge(keys_ready, PH)
            chunk = [2]

            def another():
                rest(chunk[0] % SLOTS, chunk[0])
                chunk[0] += 1

            for h in range(EARLY, PH):
                def rest_between(at):
                    if BESIDE * (h - EARLY) + at > chunk[0]:
                        another()

                choose(h, rest_between)
            assert chunk[0] == TOPK_UNTIL

            iota16 = iota[:, 0:TOPK].unsqueeze(1).broadcast_to([P, PH * TOPK, TOPK])
            for tb in range(TB):
                heads = slice(tb * PH, (tb + 1) * PH)
                dve.tensor_tensor(choice[:, 2, tb, :].rearrange("p (h k) -> p h k", k=TOPK), all_v[:, heads, :],
                                  all_v[:, heads, 0:1].broadcast_to([P, PH, TOPK]), ALU.subtract)\
                   .then_inc(shifted, 1)
                places = all_p[:, heads, :].rearrange("p h k -> p (h k)")
                dve.tensor_scalar(digit[:, 0, :], places, 4, None, ALU.logical_shift_right)
                link(dve.tensor_scalar(digit[:, 1, :], places, TOPK - 1, None, ALU.bitwise_and))
                for p in range(2):
                    b3 = BIG.rearrange("p (m a) -> p m a", a=TOPK)
                    another()
                    another()
                    link(dve.tensor_tensor(b3, digit[:, p, :].unsqueeze(2).broadcast_to([P, PH * TOPK, TOPK]),
                                           iota16, ALU.is_equal))
                    another()
                    another()
                    b4 = BIG.rearrange("p (h k a) -> p h k a", k=TOPK, a=TOPK)
                    link(dve.tensor_tensor(b4, b4, all_i[:, heads, p, :].unsqueeze(2)
                                           .broadcast_to([P, PH, TOPK, TOPK]), ALU.mult))
                    another()
                    another()
                    link(dve.tensor_reduce(choice[:, p, tb, :], b3, AX.X, ALU.add))
            assert chunk[0] == DECODE_UNTIL
            dve.sem_inc(scratch_free, 1)
            another()
            dve.wait_ge(exped, 1)
            e3 = choice[:, 2, :, :].rearrange("p b (h k) -> p (b h) k", k=TOPK)
            link(dve.tensor_reduce(gsum[:, 0, :], e3, AX.X, ALU.add))
            another()
            link(dve.reciprocal(gsum[:, 1, :], gsum[:, 0, :]))
            another()
            dve.tensor_tensor(e3, e3, gsum[:, 1, :].unsqueeze(2).broadcast_to([P, TB * PH, TOPK]), ALU.mult)\
               .then_inc(choice_ready, TB)
            another()
            for c in range(SOFTMAX_UNTIL, TURN_AT + 2):
                rest(c % SLOTS, c)
            for tb in range(TB):
                dve.wait_ge(turned, tb + 1)
                tt = slice(tb * P, (tb + 1) * P)
                dve.tensor_scalar(choice_t[:, 0, tt], bank[6 + tb][:, 0:P], -1.0, None, ALU.mult)\
                   .then_inc(choice_t_ready, 1)
                dve.tensor_copy(choice_t[:, 1:3, tt], bank[6 + tb][:, P:3 * P].rearrange("p (n t) -> p n t", n=2))\
                   .then_inc(choice_t_ready, 1)
            for c in range(TURN_AT + 2, MERGE):
                rest(c % SLOTS, c)

            def one2(j, g):
                for t in range(GT):
                    tt = g * GT + t
                    last = dve.tensor_scalar(ONE2[:, j % 2, t, :], iota, choice_t[:, 1, bass.ds(tt, 1)],
                                             choice_t[:, 2, bass.ds(tt, 1)], ALU.is_equal, ALU.mult)
                last.then_inc(one2_made, 1)

            def gate(j, g):
                dve.wait_ge(gates_done, g + 1)
                a = A3[:, :, bass.ds(g * GT, GT)]
                dve.tensor_tensor(a, a, bank[4 + j % 2][:, :].rearrange("p (t c) -> p c t", t=GT), ALU.mult)\
                   .then_inc(gated, 1)

            def multiply(j, n):
                dve.wait_ge(a_made, n + (MERGE + 1))
                dve.tensor_tensor(A3[:, n + MERGE, :], A3[:, n + MERGE, :], gelu_buf[:, j % 2, :], ALU.mult)\
                   .then_inc(multiplied, 1)

            dve.wait_ge(choice_t_ready, 2 * TB)
            for j in range(SLOTS):
                one2(j, j)
                rest(j, MERGE + j)
                if j == 1:
                    dve.wait_ge(ones_made, 2)
                    dve.wait_ge(a_made, MERGE)
                if j >= 2:
                    dve.wait_ge(gated, j - 1)
                    multiply(j, j - 2)
                    dve.wait_ge(multiplied, j - 1)
                if j:
                    gate(j - 1, j - 1)
            with dve.Fori(1, (CHUNKS - MERGE) // SLOTS) as i:
                for j in range(SLOTS):
                    one2(j, i * SLOTS + j)
                    rest(j, i * SLOTS + (MERGE + j))
                    dve.wait_ge(gated, i * SLOTS + (j - 1))
                    multiply(j, i * SLOTS + (j - 2))
                    dve.wait_ge(multiplied, i * SLOTS + (j - 1))
                    gate(j - 1, i * SLOTS + (j - 1))
            def w_rest(j, v):
                dve.wait_ge(whi_made, v + 1)
                dve.tensor_tensor(w_lo[:, j % 2, :], A3[:, v, :], w_hi[:, j % 2, :].bitcast(F32), ALU.subtract)\
                   .then_inc(wlo_made, 1)

            gate(GROUPS - 1, GROUPS - 1)
            for j in range(2):
                rest(j, CHUNKS + j)
                if j == 0:
                    dve.wait_ge(gated, GROUPS)
                multiply(j, CHUNKS - MERGE - 2 + j)
                w_rest(j, j)

            for v in (2, 3):
                w_rest(v, v)
                rest(v, CHUNKS + v)
            with dve.Fori(1, CHUNKS // SLOTS) as i:
                for j in range(SLOTS):
                    w_rest(j, i * SLOTS + j)
                    rest(j, i * SLOTS + (CHUNKS + j))

            def residual(n):
                tb, half = n // 2, slice(n % 2 * 512, n % 2 * 512 + 512)
                tmp = A[:, 4096 + n * 512:4096 + n * 512 + 512]
                dve.wait_ge(out_full, n + 1)
                link(dve.tensor_tensor(tmp, bank[4 + n][:, :], g2b[:, half], ALU.mult))
                dve.tensor_tensor(x1n[:, tb, half], x1n[:, tb, half], tmp, ALU.add).then_inc(res_ready, 1)

            def final_sum(tb):
                dve.wait_ge(fsq_ready, 2 * tb + 2)
                dve.tensor_tensor(fsum[:, 1, tb:tb + 1], fsum[:, 0, 2 * tb:2 * tb + 1], fsum[:, 0, 2 * tb + 1:2 * tb + 2],
                                  ALU.add).then_inc(fsum_ready, 1)

            def final_norm(tb):
                dve.wait_ge(froot_ready, tb + 1)
                link(dve.reciprocal(fsum[:, 1, TB + tb:TB + tb + 1], fsum[:, 2, tb:tb + 1]))
                for half in (slice(0, 512), slice(512, D)):
                    dve.scalar_tensor_tensor(x1n[:, tb, half], x1n[:, tb, half], fsum[:, 1, TB + tb:TB + tb + 1],
                                             fin[:, half], ALU.mult, ALU.mult).then_inc(out_ready, 1)

            residual(0)
            residual(1)
            residual(2)
            final_sum(0)
            residual(3)
            dve.wait_ge(fin_in, 16)
            dve.wait_ge(res_ready, 2 * TB)
            final_norm(0)
            final_sum(1)
            final_norm(1)

        @block.gpsimd
        def _(pool):
            for n in range(q0 + 3, q0 + PH):
                slot = ring_of[splits[n]] % RING
                pool.wait_ge(weight_rounded, whole(n))
                pool.tensor_tensor(WR2_lo[:, slot], WR2[:, slot], weight_hi[n].bitcast(F32), ALU.subtract)\
                    .then_inc(query_split, 1)
            pool.wait_ge(a_made, 1)
            pool.memset(A3[:, MERGE:SCRATCH, :], 1.0).then_inc(ones_made, 1)
            pool.wait_ge(scratch_free, 1)
            pool.memset(A3[:, SCRATCH:CHUNKS, :], 1.0).then_inc(ones_made, 1)


def bias_places():
    import numpy as np

    grid_w, kh, kw = 64, 8, 16
    q = np.arange(T)
    r, c = q // grid_w, q % grid_w
    start = np.clip(c - kw // 2, 0, grid_w - kw)
    inside = (c[None, :] >= start[:, None]) & (c[None, :] < start[:, None] + kw)
    dr = r[None, :] - r[:, None] + kh - 1
    dc = np.where(inside, c[None, :] - c[:, None] + kw - 1, 0)
    return inside, dr, dc


def kernel(**inputs):
    import numpy as np
    import concourse.bacc as bacc
    from concourse.bass_utils import run_bass_kernel_spmd

    f = {k: np.asarray(v) for k, v in inputs.items()}
    one = {k: f[k][0] for k in f if k not in ("c", "c_ctx", "final_norm_g")}

    def tiles(a):
        return np.ascontiguousarray(a.reshape(-1, P, a.shape[-1]).transpose(1, 0, 2))

    def column(a):
        return a.reshape(-1, P).T

    def in_blocks(a):
        return np.ascontiguousarray(a.reshape(KD, P, -1, BLK).transpose(2, 1, 0, 3))

    c2 = np.stack([column(f["c"][0]), column(f["c_ctx"])], axis=-1).reshape(P, 2 * KD)
    conv = one["conv_w"].reshape(3, CONV_T, P).transpose(2, 1, 0).reshape(P, 3 * CONV_T)
    cols = np.concatenate([c2, column(one["ada_b"]), column(one["norm1_g"]), column(one["norm2_g"]),
                           column(one["out_norm_g"]), conv], axis=1)
    rows = np.concatenate([one["sgu_b"].reshape(-1), one["ada_b"][G2 * D:]])[None]
    pick = np.kron(np.ones((4, 1)), np.eye(32))
    constants = np.concatenate([np.eye(P), np.ones((P, P)), np.kron(np.eye(2), np.ones((HD, HD))),
                                np.tile(np.arange(P), (P, 1)), np.tile(pick[:, 0:1], (1, P)), pick[:, 0:2]],
                               axis=1).astype(np.float32)
    inside, dr, dc = bias_places()
    bias_mask = np.full((HEADS, T, T), NEG, np.float32)
    bias_mask[:, inside] = one["na_rpb"][:, dr[inside], dc[inside]]
    bias_mask = bias_mask.reshape(HEADS, TB, P, T).transpose(2, 0, 1, 3)
    arrays = {
        "x_t": tiles(one["x"].T),
        "ctx_t": tiles(one["ctx"].T),
        "cols": cols,
        "rows": rows,
        "sgu_gain": np.broadcast_to(one["sgu_norm_g"], (P, BLK)),
        "final_gain": np.broadcast_to(f["final_norm_g"], (P, D)),
        "constants": constants,
        "sgu_wt": one["sgu_w"].transpose(2, 0, 1),
        "bias_mask": bias_mask,
        "ada_w": in_blocks(one["ada_w"]),
        "w_in": in_blocks(one["w_in"]),
        "w_out": in_blocks(one["w_out"]),
        "w_q": in_blocks(one["peer_wq"]),
        "subkeys_t": one["peer_subkeys"].transpose(3, 0, 1, 2).reshape(P, LISTS, NK),
        "peer_u_t": one["peer_u"].reshape(NK, NK, KD, P).transpose(1, 3, 2, 0).reshape(NK, P, D),
        "peer_v": one["peer_v"],
    }
    nc = bacc.Bacc("TRN2", target_bir_lowering=False, num_devices=1)
    arrays = {f"in_{k}": np.ascontiguousarray(v) for k, v in arrays.items()}
    args = [nc.dram_tensor(k, v.shape, mybir.dt.from_np(v.dtype), kind="ExternalInput").ap()
            for k, v in arrays.items()]
    result = nc.dram_tensor("out_x", (T, D), F32, kind="ExternalOutput").ap()
    build(nc, *args, result)
    r = run_bass_kernel_spmd(nc, [arrays], core_ids=[0])
    return r.results[0]["out_x"].reshape(1, T, D)
```
